# Optimizing a Trainium2 kernel written in Bass

```python
import jax, jax.numpy as jnp
from jax import lax
import numpy as np
import math
import jax
import jax.numpy as jnp

D_MODEL = 1024
BATCH = 1
SEQ = 256
DEPTH = 2

WINDOWS = (128, 512, 2048)
DILATIONS = (1, 4, 16)
N_GROUPS = 3
HEADS_PER_GROUP = 8
HEAD_DIM = 128
N_ATTN_HEADS = N_GROUPS * HEADS_PER_GROUP
ATTN_OUT_WIDTH = HEADS_PER_GROUP * HEAD_DIM
QKV_WIDTH = N_GROUPS * 3 * HEADS_PER_GROUP * HEAD_DIM
NUM_BUCKETS = 32
MAX_DISTANCE = 2048
LRU_WIDTH = D_MODEL
LRU_BLOCKS = 4
LRU_BLOCK_WIDTH = LRU_WIDTH // LRU_BLOCKS
LRU_CONV_WIDTH = 4
LRU_C = 8.0
D_FF = 3 * D_MODEL
FFN_CONV_WIDTH = 3

RMS_EPS = 1e-6
NEG_INF = -1e30
N_ATTN_LAYERS = (DEPTH + 1) // 2
N_LRU_LAYERS = DEPTH // 2


def rms_norm(x, g):
    xf = x.astype(jnp.float32)
    y = xf * lax.rsqrt(jnp.mean(xf * xf, axis=-1, keepdims=True) + RMS_EPS)
    return (y * g.astype(jnp.float32)).astype(x.dtype)

def causal_dwconv(x, w, b):
    K = w.shape[0]
    S = x.shape[1]
    xp = jnp.pad(x, ((0, 0), (K - 1, 0), (0, 0)))
    out = b
    for k in range(K):
        out = out + xp[:, k:k + S] * w[k]
    return out

def t5_bucket(dist):
    max_exact = NUM_BUCKETS // 2
    d = np.maximum(dist, 1).astype(np.float64)
    large = max_exact + (np.log(d / max_exact) / np.log(MAX_DISTANCE / max_exact)
                         * (NUM_BUCKETS - max_exact)).astype(np.int32)
    large = np.minimum(large, NUM_BUCKETS - 1)
    return np.where(dist < max_exact, dist, large).astype(np.int32)

def band_geometry(band):
    i = np.arange(band)[:, None]
    k = np.arange(2 * band)[None, :]
    m = i + band - k
    valid = (m >= 0) & (m <= band)
    return m, valid, k

def dilated_group_attention(q, k, v, bias_table, window, dilation):
    B, S, H, Dh = q.shape
    band = window // dilation
    span = dilation * band
    S_pad = -(-S // span) * span
    U = S_pad // dilation
    nb = U // band

    def to_strided(t):
        t = jnp.pad(t, ((0, 0), (0, S_pad - S), (0, 0), (0, 0)))
        t = t.reshape(B, U, dilation, H, Dh).transpose(0, 2, 3, 1, 4)
        return t.reshape(B, dilation, H, nb, band, Dh)

    qs, ks, vs = to_strided(q), to_strided(k), to_strided(v)
    pad_blk = ((0, 0), (0, 0), (0, 0), (1, 0), (0, 0), (0, 0))
    kk = jnp.concatenate([jnp.pad(ks, pad_blk)[:, :, :, :-1], ks], axis=-2)
    vv = jnp.concatenate([jnp.pad(vs, pad_blk)[:, :, :, :-1], vs], axis=-2)

    m, valid, kidx = band_geometry(band)
    bucket = t5_bucket(np.clip(m, 0, band) * dilation)
    bias = jnp.transpose(bias_table.astype(jnp.float32)[bucket], (2, 0, 1))
    blk = np.arange(nb)[:, None, None]
    mask = valid[None] & ((blk > 0) | (kidx[None] >= band))

    scale = HEAD_DIM ** -0.5
    logits = jnp.einsum('bxhnqd,bxhnkd->bxhnqk', qs, kk,
                        preferred_element_type=jnp.float32) * scale
    logits = logits + bias[None, None, :, None]
    logits = jnp.where(mask[None, None, None], logits, NEG_INF)
    mx = jnp.max(logits, axis=-1, keepdims=True)
    p = jnp.exp(logits - mx)
    s = jnp.sum(p, axis=-1, keepdims=True)
    o = jnp.einsum('bxhnqk,bxhnkd->bxhnqd', p, vv.astype(jnp.float32)) / s
    lse = (mx + jnp.log(s))[..., 0]

    o = o.reshape(B, dilation, H, U, Dh).transpose(0, 3, 1, 2, 4).reshape(B, S_pad, H, Dh)[:, :S]
    lse = lse.reshape(B, dilation, H, U).transpose(0, 3, 1, 2).reshape(B, S_pad, H)[:, :S]
    return o, lse

def dilated_attention_mixer(x, w_qkv, w_o, rel_bias):
    B, S, _ = x.shape
    qkv = (x @ w_qkv).reshape(B, S, N_GROUPS, 3, HEADS_PER_GROUP, HEAD_DIM)
    outs, lses = [], []
    for g in range(N_GROUPS):
        tbl = rel_bias[:, g * HEADS_PER_GROUP:(g + 1) * HEADS_PER_GROUP]
        o, lse = dilated_group_attention(qkv[:, :, g, 0], qkv[:, :, g, 1], qkv[:, :, g, 2],
                                         tbl, WINDOWS[g], DILATIONS[g])
        outs.append(o)
        lses.append(lse)
    alpha = jax.nn.softmax(jnp.stack(lses), axis=0)
    o = jnp.sum(alpha[..., None] * jnp.stack(outs), axis=0)
    return o.reshape(B, S, ATTN_OUT_WIDTH).astype(x.dtype) @ w_o

def _lru_combine(c1, c2):
    a1, b1 = c1
    a2, b2 = c2
    return a1 * a2, a2 * b1 + b2

def rglru_mixer(x, w_in, conv_w, conv_b, ga_w, ga_b, gx_w, gx_b, lam, w_out):
    B, S, _ = x.shape
    h = x @ w_in
    xb, gb = h[..., :LRU_WIDTH], h[..., LRU_WIDTH:]
    gate = jax.nn.gelu(gb, approximate=True)
    xb = causal_dwconv(xb, conv_w, conv_b)
    xr = xb.reshape(B, S, LRU_BLOCKS, LRU_BLOCK_WIDTH)
    r = jax.nn.sigmoid(jnp.einsum('bsnc,ncd->bsnd', xr, ga_w) + ga_b).reshape(B, S, LRU_WIDTH)
    i = jax.nn.sigmoid(jnp.einsum('bsnc,ncd->bsnd', xr, gx_w) + gx_b).reshape(B, S, LRU_WIDTH)
    log_a = LRU_C * r.astype(jnp.float32) * jax.nn.log_sigmoid(lam.astype(jnp.float32))
    a = jnp.exp(log_a)
    mult = jnp.sqrt(jnp.maximum(-jnp.expm1(2.0 * log_a), 0.0))
    b = mult * i.astype(jnp.float32) * xb.astype(jnp.float32)
    _, hs = lax.associative_scan(_lru_combine, (a, b), axis=1)
    return (hs.astype(x.dtype) * gate) @ w_out

def conv_ffn(x, w_up, conv_w, conv_b, w_down):
    u = causal_dwconv(x @ w_up, conv_w, conv_b)
    g, v = u[..., :D_FF], u[..., D_FF:]
    return (jax.nn.gelu(g, approximate=True) * v) @ w_down

def first_inputs(seed: int = 0) -> dict:
    key = jax.random.key(seed)
    ks = jax.random.split(key, 32)
    f32 = jnp.float32
    nrm = lambda k, shape, s: jax.random.normal(k, shape, f32) * s
    gain = lambda k: 1.0 + 0.05 * jax.random.normal(k, (DEPTH, D_MODEL), f32)
    a_target = jax.random.uniform(ks[20], (N_LRU_LAYERS, LRU_WIDTH), f32, 0.9, 0.999)
    p = a_target ** (1.0 / LRU_C)
    lam = jnp.log(p) - jnp.log1p(-p)
    return {
        "x": nrm(ks[0], (BATCH, SEQ, D_MODEL), 1.0),
        "norm_mix_pre": gain(ks[1]),
        "norm_mix_post": gain(ks[2]),
        "norm_ffn_pre": gain(ks[3]),
        "norm_ffn_post": gain(ks[4]),
        "rel_bias": nrm(ks[5], (NUM_BUCKETS, N_ATTN_HEADS), 0.5),
        "attn_w_qkv": nrm(ks[6], (N_ATTN_LAYERS, D_MODEL, QKV_WIDTH), D_MODEL ** -0.5),
        "attn_w_o": nrm(ks[7], (N_ATTN_LAYERS, ATTN_OUT_WIDTH, D_MODEL), ATTN_OUT_WIDTH ** -0.5),
        "lru_w_in": nrm(ks[8], (N_LRU_LAYERS, D_MODEL, 2 * LRU_WIDTH), D_MODEL ** -0.5),
        "lru_conv_w": nrm(ks[9], (N_LRU_LAYERS, LRU_CONV_WIDTH, LRU_WIDTH), LRU_CONV_WIDTH ** -0.5),
        "lru_conv_b": nrm(ks[10], (N_LRU_LAYERS, LRU_WIDTH), 0.02),
        "lru_ga_w": nrm(ks[11], (N_LRU_LAYERS, LRU_BLOCKS, LRU_BLOCK_WIDTH, LRU_BLOCK_WIDTH), LRU_BLOCK_WIDTH ** -0.5),
        "lru_ga_b": nrm(ks[12], (N_LRU_LAYERS, LRU_BLOCKS, LRU_BLOCK_WIDTH), 0.02),
        "lru_gx_w": nrm(ks[13], (N_LRU_LAYERS, LRU_BLOCKS, LRU_BLOCK_WIDTH, LRU_BLOCK_WIDTH), LRU_BLOCK_WIDTH ** -0.5),
        "lru_gx_b": nrm(ks[14], (N_LRU_LAYERS, LRU_BLOCKS, LRU_BLOCK_WIDTH), 0.02),
        "lru_lambda": lam,
        "lru_w_out": nrm(ks[15], (N_LRU_LAYERS, LRU_WIDTH, D_MODEL), LRU_WIDTH ** -0.5),
        "ffn_w_up": nrm(ks[16], (DEPTH, D_MODEL, 2 * D_FF), D_MODEL ** -0.5),
        "ffn_conv_w": nrm(ks[17], (DEPTH, FFN_CONV_WIDTH, 2 * D_FF), FFN_CONV_WIDTH ** -0.5),
        "ffn_conv_b": nrm(ks[18], (DEPTH, 2 * D_FF), 0.02),
        "ffn_w_down": nrm(ks[19], (DEPTH, D_FF, D_MODEL), D_FF ** -0.5),
    }

def first_block(x, norm_mix_pre, norm_mix_post, norm_ffn_pre, norm_ffn_post, rel_bias,
              attn_w_qkv, attn_w_o, lru_w_in, lru_conv_w, lru_conv_b, lru_ga_w, lru_ga_b,
              lru_gx_w, lru_gx_b, lru_lambda, lru_w_out, ffn_w_up, ffn_conv_w, ffn_conv_b,
              ffn_w_down):
    for layer in range(DEPTH):
        j = layer // 2
        h = rms_norm(x, norm_mix_pre[layer])
        if layer % 2 == 0:
            h = dilated_attention_mixer(h, attn_w_qkv[j], attn_w_o[j], rel_bias)
        else:
            h = rglru_mixer(h, lru_w_in[j], lru_conv_w[j], lru_conv_b[j], lru_ga_w[j], lru_ga_b[j],
                            lru_gx_w[j], lru_gx_b[j], lru_lambda[j], lru_w_out[j])
        x = x + rms_norm(h, norm_mix_post[layer])
        h = rms_norm(x, norm_ffn_pre[layer])
        h = conv_ffn(h, ffn_w_up[layer], ffn_conv_w[layer], ffn_conv_b[layer], ffn_w_down[layer])
        x = x + rms_norm(h, norm_ffn_post[layer])
    return x


DEPTH_2 = 1

CTX_LEN = 256
GRID_W = 64
N_HEADS_GDN = 4
N_HEADS_RET = 4
W_GDN = N_HEADS_GDN * HEAD_DIM
W_RET = N_HEADS_RET * HEAD_DIM
MIX_WIDTH = W_GDN + W_RET
IN_COLS = 4 * W_GDN + 4 * N_HEADS_GDN + 4 * W_RET
CONV_K = 5
CHUNK = 64
D_FF_2 = ((8 * D_MODEL + 3 * 256 - 1) // (3 * 256)) * 256
ROPE_THETA = 10000.0
ROPE_SEQ_PAIRS = 16
ROPE_ROW_PAIRS = 24
ROPE_COL_PAIRS = 24
HALF = HEAD_DIM // 2
NORM_EPS = 1e-6


def rms_norm_2(x, g):
    xf = x.astype(jnp.float32)
    y = xf * lax.rsqrt(jnp.mean(xf * xf, axis=-1, keepdims=True) + NORM_EPS)
    return (y * g.astype(jnp.float32)).astype(x.dtype)

def head_group_norm(t, g):
    mu = jnp.mean(t, axis=-1, keepdims=True)
    var = jnp.mean(jnp.square(t - mu), axis=-1, keepdims=True)
    return (t - mu) * lax.rsqrt(var + NORM_EPS) * g.astype(jnp.float32)

def l2_normalize(t):
    return t * lax.rsqrt(jnp.sum(t * t, axis=-1, keepdims=True) + NORM_EPS)

def modulate(h, shift, scale):
    return h * (1.0 + scale) + shift

def adaln(cond, w, b):
    mod = (jax.nn.silu(cond) @ w + b)[:, None, :]
    return jnp.split(mod, 6, axis=-1)

def swiglu(h, w_in, w_out):
    gate, up = jnp.split(h @ w_in, 2, axis=-1)
    return (jax.nn.silu(gate) * up) @ w_out

def axis_angles(pos, n_pairs):
    inv_freq = ROPE_THETA ** (-jnp.arange(n_pairs, dtype=jnp.float32) / n_pairs)
    return pos[:, None] * inv_freq[None, :]

def rope_tables(rows):
    n_lat = rows * GRID_W
    row = jnp.repeat(jnp.arange(rows, dtype=jnp.float32), GRID_W)
    col = jnp.tile(jnp.arange(GRID_W, dtype=jnp.float32), rows)
    zeros_ctx = jnp.zeros((CTX_LEN,), jnp.float32)
    p_seq = jnp.concatenate([jnp.arange(CTX_LEN, dtype=jnp.float32),
                             jnp.full((n_lat,), float(CTX_LEN), jnp.float32)])
    p_row = jnp.concatenate([zeros_ctx, row])
    p_col = jnp.concatenate([zeros_ctx, col])
    ang = jnp.concatenate([axis_angles(p_seq, ROPE_SEQ_PAIRS),
                           axis_angles(p_row, ROPE_ROW_PAIRS),
                           axis_angles(p_col, ROPE_COL_PAIRS)], axis=-1)
    return jnp.cos(ang), jnp.sin(ang)

def apply_rope(t, cos, sin):
    c = cos[None, :, None, :]
    s = sin[None, :, None, :]
    t1, t2 = t[..., :HALF], t[..., HALF:]
    return jnp.concatenate([t1 * c - t2 * s, t1 * s + t2 * c], axis=-1)

def to_bwd(t):
    return jnp.concatenate([jnp.flip(t[:, :CTX_LEN], axis=1), jnp.flip(t[:, CTX_LEN:], axis=1)], axis=1)

def short_conv(u, w):
    n = u.shape[1]
    pad = (CONV_K - 1) // 2
    up = jnp.pad(u, ((0, 0), (pad, pad), (0, 0)))
    y = up[:, 0:n] * w[0]
    for i in range(1, CONV_K):
        y = y + up[:, i:i + n] * w[i]
    return jax.nn.silu(y)

def to_chunks(t):
    b, tl, h = t.shape[:3]
    t = t.reshape((b, tl // CHUNK, CHUNK, h) + t.shape[3:])
    return t.transpose((1, 0, 3, 2) + tuple(range(4, t.ndim)))

def from_chunks(o):
    nc, b, h, cl, d = o.shape
    return o.transpose(1, 0, 3, 2, 4).reshape(b, nc * cl, h, d)

def gated_delta_rule(q, k, v, g, beta):
    b, tl, h, dk = q.shape
    dv = v.shape[-1]
    qc, kc, vc = to_chunks(q), to_chunks(k), to_chunks(v)
    gc, bc = to_chunks(g), to_chunks(beta)
    G = jnp.cumsum(gc, axis=-1)
    idx = jnp.arange(CHUNK)
    incl = idx[:, None] >= idx[None, :]
    strict = idx[:, None] > idx[None, :]
    diff = G[..., :, None] - G[..., None, :]
    decay = jnp.where(incl, jnp.exp(jnp.where(incl, diff, 0.0)), 0.0)
    kb = kc * bc[..., None]
    A = jnp.where(strict, jnp.einsum('nbhid,nbhjd->nbhij', kb, kc) * decay, 0.0)
    rhs = jnp.concatenate([vc * bc[..., None], kb * jnp.exp(G)[..., None]], axis=-1)
    sol = lax.linalg.triangular_solve(A + jnp.eye(CHUNK, dtype=A.dtype), rhs,
                                      left_side=True, lower=True, unit_diagonal=True)
    u, w = sol[..., :dv], sol[..., dv:]
    qk = jnp.einsum('nbhid,nbhjd->nbhij', qc, kc) * decay
    q_dec = qc * jnp.exp(G)[..., None]
    k_dec = kc * jnp.exp(G[..., -1:] - G)[..., None]
    g_last = jnp.exp(G[..., -1])[..., None, None]

    def step(S, xs):
        u_c, w_c, q_c, qk_c, k_c, gl = xs
        v_new = u_c - jnp.einsum('bhck,bhkv->bhcv', w_c, S)
        o = jnp.einsum('bhck,bhkv->bhcv', q_c, S) + jnp.einsum('bhij,bhjv->bhiv', qk_c, v_new)
        S = gl * S + jnp.einsum('bhck,bhcv->bhkv', k_c, v_new)
        return S, o

    S0 = jnp.zeros((b, h, dk, dv), q.dtype)
    _, o = lax.scan(step, S0, (u, w, q_dec, qk, k_dec, g_last))
    return from_chunks(o)

def retention_chunkwise(q, k, v, log_gamma):
    b, tl, h, dk = q.shape
    dv = v.shape[-1]
    qc, kc, vc = to_chunks(q), to_chunks(k), to_chunks(v)
    pos = jnp.arange(CHUNK, dtype=jnp.float32)
    lg = log_gamma.astype(jnp.float32)[:, None]
    diff = pos[:, None] - pos[None, :]
    decay = jnp.where(diff >= 0, jnp.exp(lg[:, :, None] * jnp.maximum(diff, 0.0)), 0.0)
    xi = jnp.exp(lg * (pos + 1.0))
    zeta = jnp.exp(lg * (CHUNK - 1.0 - pos))
    g_chunk = jnp.exp(lg * CHUNK)[..., None]
    inner = jnp.einsum('nbhij,nbhjv->nbhiv', jnp.einsum('nbhid,nbhjd->nbhij', qc, kc) * decay, vc)

    def step(R, xs):
        q_c, k_c, v_c = xs
        o = jnp.einsum('bhik,bhkv->bhiv', q_c * xi[..., None], R)
        R = g_chunk * R + jnp.einsum('bhjk,bhjv->bhkv', k_c * zeta[..., None], v_c)
        return R, o

    R0 = jnp.zeros((b, h, dk, dv), q.dtype)
    _, cross = lax.scan(step, R0, (qc, kc, vc))
    return from_chunks(inner + cross)

def hybrid_mixer(h_ctx, h_lat, w_in, conv_w, gdn_a_log, gdn_dt_bias, gdn_norm_g,
                 ret_decay_logit, ret_norm_g, cos, sin):
    out_dtype = h_lat.dtype
    f32 = jnp.float32
    h = jnp.concatenate([h_ctx, h_lat], axis=1)
    p = (h @ w_in).astype(f32)
    b, tl, _ = p.shape
    splits = [3 * W_GDN, 4 * W_GDN, 4 * W_GDN + 4 * N_HEADS_GDN,
              4 * W_GDN + 4 * N_HEADS_GDN + W_RET,
              4 * W_GDN + 4 * N_HEADS_GDN + 2 * W_RET,
              4 * W_GDN + 4 * N_HEADS_GDN + 3 * W_RET]
    qkv_a, z, ab, rq, rk, rv, rg = jnp.split(p, splits, axis=-1)

    cw = conv_w.astype(f32)
    qkv_a = jnp.concatenate([short_conv(qkv_a[:, :CTX_LEN], cw), short_conv(qkv_a[:, CTX_LEN:], cw)], axis=1)
    q, k, v = [t.reshape(b, tl, N_HEADS_GDN, HEAD_DIM) for t in jnp.split(qkv_a, 3, axis=-1)]
    q = l2_normalize(q) * (HEAD_DIM ** -0.5)
    k = l2_normalize(k)
    a_f, a_b, b_f, b_b = jnp.split(ab, 4, axis=-1)
    A = jnp.exp(gdn_a_log.astype(f32))
    dtb = gdn_dt_bias.astype(f32)
    g_f = -A[0] * jax.nn.softplus(a_f + dtb[0])
    g_b = -A[1] * jax.nn.softplus(a_b + dtb[1])
    o_f = gated_delta_rule(q, k, v, g_f, jax.nn.sigmoid(b_f))
    o_b = to_bwd(gated_delta_rule(to_bwd(q), to_bwd(k), to_bwd(v), to_bwd(g_b), to_bwd(jax.nn.sigmoid(b_b))))
    o_gdn = rms_norm_2(o_f + o_b, gdn_norm_g) * jax.nn.silu(z.reshape(b, tl, N_HEADS_GDN, HEAD_DIM))

    rq = apply_rope(rq.reshape(b, tl, N_HEADS_RET, HEAD_DIM), cos, sin)
    rk = apply_rope(rk.reshape(b, tl, N_HEADS_RET, HEAD_DIM), cos, sin) * (HEAD_DIM ** -0.5)
    rv = rv.reshape(b, tl, N_HEADS_RET, HEAD_DIM)
    lg = jax.nn.log_sigmoid(ret_decay_logit.astype(f32))
    r_f = retention_chunkwise(rq, rk, rv, lg[0])
    r_b = to_bwd(retention_chunkwise(to_bwd(rq), to_bwd(rk), to_bwd(rv), lg[1]))
    o_ret = head_group_norm(r_f + r_b, ret_norm_g) * jax.nn.silu(rg.reshape(b, tl, N_HEADS_RET, HEAD_DIM))

    y = jnp.concatenate([o_gdn.reshape(b, tl, W_GDN), o_ret.reshape(b, tl, W_RET)], axis=-1)
    return y.astype(out_dtype)

def second_inputs(seed: int = 0) -> dict:
    key = jax.random.key(seed)
    ks = jax.random.split(key, 19)
    f32 = jnp.float32

    def nrm(k, shape, scale):
        return scale * jax.random.normal(k, shape, f32)

    x = nrm(ks[0], (BATCH, SEQ, D_MODEL), 1.0)
    c = nrm(ks[1], (BATCH, D_MODEL), 1.0)
    ctx = nrm(ks[2], (BATCH, CTX_LEN, D_MODEL), 1.0)
    c_ctx = nrm(ks[3], (D_MODEL,), 1.0)
    ada_w = nrm(ks[4], (DEPTH_2, D_MODEL, 6 * D_MODEL), D_MODEL ** -0.5)
    ada_b = nrm(ks[5], (DEPTH_2, 6 * D_MODEL), 0.02)
    norm_mix_g = 1.0 + nrm(ks[6], (DEPTH_2, D_MODEL), 0.05)
    norm_ffn_g = 1.0 + nrm(ks[7], (DEPTH_2, D_MODEL), 0.05)
    w_in = nrm(ks[8], (DEPTH_2, D_MODEL, IN_COLS), D_MODEL ** -0.5)
    conv_w = nrm(ks[9], (DEPTH_2, CONV_K, 3 * W_GDN), CONV_K ** -0.5)
    gdn_a_log = jnp.log(jax.random.uniform(ks[10], (DEPTH_2, 2, N_HEADS_GDN), f32, 1.0, 16.0))
    dt = jnp.exp(jax.random.uniform(ks[11], (DEPTH_2, 2, N_HEADS_GDN), f32, math.log(1e-3), math.log(1e-1)))
    gdn_dt_bias = dt + jnp.log(-jnp.expm1(-dt))
    gdn_norm_g = 1.0 + nrm(ks[12], (DEPTH_2, HEAD_DIM), 0.05)
    heads = jnp.arange(N_HEADS_RET, dtype=f32)
    ret_decay_logit = jnp.log(2.0 ** (5.0 + heads) - 1.0) + nrm(ks[13], (DEPTH_2, 2, N_HEADS_RET), 0.01)
    ret_norm_g = 1.0 + nrm(ks[14], (DEPTH_2, HEAD_DIM), 0.05)
    w_out = nrm(ks[15], (DEPTH_2, MIX_WIDTH, D_MODEL), MIX_WIDTH ** -0.5)
    w_ffn_in = nrm(ks[16], (DEPTH_2, D_MODEL, 2 * D_FF_2), D_MODEL ** -0.5)
    w_ffn_out = nrm(ks[17], (DEPTH_2, D_FF_2, D_MODEL), D_FF_2 ** -0.5)
    final_g = 1.0 + nrm(ks[18], (D_MODEL,), 0.05)
    return {"x": x, "c": c, "ctx": ctx, "c_ctx": c_ctx, "ada_w": ada_w, "ada_b": ada_b,
            "norm_mix_g": norm_mix_g, "norm_ffn_g": norm_ffn_g, "w_in": w_in, "conv_w": conv_w,
            "gdn_a_log": gdn_a_log, "gdn_dt_bias": gdn_dt_bias, "gdn_norm_g": gdn_norm_g,
            "ret_decay_logit": ret_decay_logit, "ret_norm_g": ret_norm_g, "w_out": w_out,
            "w_ffn_in": w_ffn_in, "w_ffn_out": w_ffn_out, "final_g": final_g}

def second_block(x, c, ctx, c_ctx, ada_w, ada_b, norm_mix_g, norm_ffn_g, w_in, conv_w,
              gdn_a_log, gdn_dt_bias, gdn_norm_g, ret_decay_logit, ret_norm_g, w_out,
              w_ffn_in, w_ffn_out, final_g):
    n_lat = x.shape[1]
    rows = n_lat // GRID_W
    cos, sin = rope_tables(rows)
    x_ctx = ctx
    for layer in range(DEPTH_2):
        sh1, sc1, g1, sh2, sc2, g2 = adaln(c, ada_w[layer], ada_b[layer])
        csh1, csc1, cg1, csh2, csc2, cg2 = adaln(c_ctx[None, :], ada_w[layer], ada_b[layer])
        h_lat = modulate(rms_norm_2(x, norm_mix_g[layer]), sh1, sc1)
        h_ctx = modulate(rms_norm_2(x_ctx, norm_mix_g[layer]), csh1, csc1)
        y = hybrid_mixer(h_ctx, h_lat, w_in[layer], conv_w[layer], gdn_a_log[layer],
                         gdn_dt_bias[layer], gdn_norm_g[layer], ret_decay_logit[layer],
                         ret_norm_g[layer], cos, sin)
        x = x + g1 * (y[:, CTX_LEN:] @ w_out[layer])
        x = x + g2 * swiglu(modulate(rms_norm_2(x, norm_ffn_g[layer]), sh2, sc2),
                            w_ffn_in[layer], w_ffn_out[layer])
        if layer < DEPTH_2 - 1:
            x_ctx = x_ctx + cg1 * (y[:, :CTX_LEN] @ w_out[layer])
            x_ctx = x_ctx + cg2 * swiglu(modulate(rms_norm_2(x_ctx, norm_ffn_g[layer]), csh2, csc2),
                                         w_ffn_in[layer], w_ffn_out[layer])
    return rms_norm_2(x, final_g)


def setup_inputs(seed=0):
    out = dict(first_inputs(seed))
    for name, value in second_inputs(seed + 1).items():
        if name != "x":
            out[name + "_2"] = value
    return out


def reference(
    x, norm_mix_pre, norm_mix_post, norm_ffn_pre, norm_ffn_post, rel_bias, attn_w_qkv, attn_w_o,
    lru_w_in, lru_conv_w, lru_conv_b, lru_ga_w, lru_ga_b, lru_gx_w, lru_gx_b, lru_lambda,
    lru_w_out, ffn_w_up, ffn_conv_w, ffn_conv_b, ffn_w_down, c_2, ctx_2, c_ctx_2, ada_w_2,
    ada_b_2, norm_mix_g_2, norm_ffn_g_2, w_in_2, conv_w_2, gdn_a_log_2, gdn_dt_bias_2,
    gdn_norm_g_2, ret_decay_logit_2, ret_norm_g_2, w_out_2, w_ffn_in_2, w_ffn_out_2, final_g_2,
):
    x = first_block(
        x, norm_mix_pre, norm_mix_post, norm_ffn_pre, norm_ffn_post, rel_bias, attn_w_qkv,
        attn_w_o, lru_w_in, lru_conv_w, lru_conv_b, lru_ga_w, lru_ga_b, lru_gx_w, lru_gx_b,
        lru_lambda, lru_w_out, ffn_w_up, ffn_conv_w, ffn_conv_b, ffn_w_down,
    )
    return second_block(
        x, c_2, ctx_2, c_ctx_2, ada_w_2, ada_b_2, norm_mix_g_2, norm_ffn_g_2, w_in_2, conv_w_2,
        gdn_a_log_2, gdn_dt_bias_2, gdn_norm_g_2, ret_decay_logit_2, ret_norm_g_2, w_out_2,
        w_ffn_in_2, w_ffn_out_2, final_g_2,
    )


_drawn_inputs = setup_inputs


def setup_inputs(seed=0):
    import zlib

    import numpy as np

    out = dict(_drawn_inputs(seed))
    spreads = {}
    factors = {'lru_ga_b': 8.0,
     'lru_gx_b': 8.0,
     'ada_b_2': 3.05,
     'norm_mix_g_2': 3.425,
     'norm_ffn_g_2': 3.069,
     'gdn_a_log_2': 3.271,
     'gdn_norm_g_2': 8.0,
     'ret_norm_g_2': 6.952}
    for name, (base, spread) in spreads.items():
        noise = np.random.default_rng([zlib.crc32(name.encode()), seed]).standard_normal(out[name].shape)
        drawn = base * np.exp(spread * noise) if base else spread * noise
        out[name] = jnp.asarray(drawn.astype(out[name].dtype))
    for name, factor in factors.items():
        out[name] = (out[name] * factor).astype(out[name].dtype)
    return out
```

```python
from contextlib import ExitStack

import numpy as np

import concourse.bass as bass
from concourse import mybir

F32 = mybir.dt.float32
ALU = mybir.AluOpType
ACT = mybir.ActivationFunctionType
AX = mybir.AxisListType

P = 128
D = 1024
KT = D // P
TT = 2
S = TT * P
EPS = 1e-6
NS = 3
SLOT = 4096
HD_SCALE = float(P) ** -0.5

GROUPS = 3
HEADS = 8
DILATIONS = (1, 4, 16)
BAND = 128
BUCKETS = 32
MAX_DISTANCE = 2048
NEG = -1e30
WLEN = 384

FF = 3 * D
FT = FF // P
FF2 = 2816
FT2 = FF2 // P

H4 = 4
NG = 16
TT2 = 4
LEVELS = 7

PC = {}
_at = 0
for _name, _n in (("mix_pre", 16), ("ffn_pre", 16), ("lru_conv_w", 32), ("lru_conv_b", 8),
                  ("ga_b", 8), ("gx_b", 8), ("lam", 8), ("mix_g2", 8), ("ffn_g2", 8),
                  ("ffn_conv_w", 288), ("ffn_conv_b", 96), ("conv_w2", 60), ("ada_b", 48),
                  ("cond", 16)):
    PC[_name] = _at
    _at += _n
NPC = _at
CONV2_K = 5

C_LE, C_GE, C_GT, C_LT, C_ONE, C_ID = range(6)
C_LEVEL = 6
NCONST = 6 + 2 * LEVELS


def attention_order():
    k = lambda hp, g: ("K", hp, g)
    v = lambda q, g: ("V", q, g)
    s = lambda h: ("S", h, 0)
    t = lambda h: ("T", h, 0)
    o = lambda h: ("O", h, 0)
    return [v(0, 0), v(0, 1), v(0, 2), k(0, 0), k(0, 1), k(0, 2),
            s(0), k(1, 0), t(0), s(1), k(1, 1), o(0), t(1), k(1, 2),
            o(1), s(2), k(2, 0), t(2), s(3), k(2, 1), o(2), t(3), k(2, 2),
            o(3), s(4), v(1, 0), t(4), s(5), v(1, 1), v(1, 2),
            o(4), t(5), k(3, 0), o(5), k(3, 1), k(3, 2),
            s(6), t(6), s(7), o(6), t(7), o(7)]


def stream_order():
    ada = [("ada", i, 0) for i in range(12)]
    return ([c for c in attention_order() if c[0] in "VK"]
            + [("wo", i, 0) for i in range(2)] + ada[0:3]
            + [("up", 0, i) for i in range(12)] + [("down", 0, i) for i in range(6)] + ada[3:6]
            + [("lin", i, 0) for i in range(4)] + [("lout", i, 0) for i in range(2)] + ada[6:9]
            + [("up", 1, i) for i in range(12)] + [("down", 1, i) for i in range(6)] + ada[9:12]
            + [("win", i, 0) for i in range(8)] + [("wo2", i, 0) for i in range(2)]
            + [("up2", i, 0) for i in range(11)] + [("down2", i, 0) for i in range(6)])


STREAM = stream_order()
NCH = len(STREAM)
POSITION = {c: i for i, c in enumerate(STREAM)}


def build_program(nc, A, out):
    ctx = ExitStack()
    with ctx:
        def sb(name, shape):
            return ctx.enter_context(nc.sbuf_tensor(name, shape, F32))

        sems = {}

        def S_(name):
            if name not in sems:
                sems[name] = ctx.enter_context(nc.semaphore(name))
            return sems[name]

        ring = sb("ring", [P, NS, SLOT])
        x = sb("x", [P, TT, D])
        gains = sb("gains", [P, 2, D])
        gates = sb("gates", [P, 2, D])
        par = sb("par", [P, NPC])
        row = sb("row", [2, 2, 512])
        sel = sb("sel", [2, P])
        cst = sb("cst", [P, 6, P])
        modT = sb("modT", [P, 48, 2])
        small = sb("small", [P, 192])
        smallp = sb("smallp", [P, 64])
        arena = sb("arena", [P, 30720])
        ps = ctx.enter_context(nc.psum_tensor("ps", [P, 8, 512], F32))
        table = nc.dram_tensor("distance_tables", [HEADS, P, GROUPS * WLEN], F32)

        ident = cst[:, C_ID, :]
        def region(start, *shape):
            n = int(np.prod(shape))
            assert start + n <= 30720, (start, shape)
            v = arena[:, start:start + n]
            if len(shape) == 1:
                return v
            names = "abcd"[:len(shape)]
            return v.rearrange(f"p ({' '.join(names)}) -> p {' '.join(names)}",
                               **{k: m for k, m in zip(names, shape)})

        def pcol(name, i=0, n=1):
            return par[:, PC[name] + i:PC[name] + i + n]

        xn = region(0, TT, D)
        hT = region(2048, KT, S)
        bias = region(4096, HEADS, GROUPS, S)
        V = region(10240, TT, GROUPS, 4, P)
        QKb = [region(13312 + 3072 * b, GROUPS, 4, S) for b in range(2)]
        L = [region(19456 + 1152 * b, GROUPS, 384) for b in range(2)]
        PT = region(21760, 9, P)
        oT = region(22912, HEADS, S)
        onehot = region(24960, GROUPS, WLEN)
        negm = region(26112, GROUPS, WLEN)
        wtab = region(27264, GROUPS, WLEN)
        relb = region(28416, 24)
        aT = region(4096, FT, S)
        u = [region(10240 + 1024 * b, 4, S) for b in range(2)]
        gl = [region(12288 + 512 * b, 2, S) for b in range(2)]
        xc = region(4096, KT, S)
        gb = region(6144, KT, S)
        tr = region(8192, KT, S)
        ti = region(10240, KT, S)
        av = region(12288, KT, S)
        th = region(14336, KT, S)
        mu = region(16384, KT, S)
        lT = region(18432, KT, S)
        lgw = region(20480, 2, 4, 2, S)

        def mm(o, l, r, start, stop):
            return nc.tensor.matmul(o, l, r, start=start, stop=stop)

        def landed(pe, chunk):
            i = POSITION[chunk]
            pe.wait_ge(S_(f"landed{i % NS}"), 16 * (i // NS + 1))
            return ring[:, i % NS, :]

        def chunk_done(eng, chunk):
            eng.wait_ge(S_("chunk_used"), POSITION[chunk] + 1)

        class Norm:

            def __init__(self, index, col, src, scaled, dst, gain, shift, ready, banks=(4, 5, 6, 7)):
                self.index, self.col, self.src, self.scaled, self.dst = index, col, src, scaled, dst
                self.gain, self.shift, self.ready, self.banks = gain, shift, ready, banks

            def scalar_square(self, act):
                for t in range(TT):
                    self.ready(act, t)
                    nc.scalar.activation(xn[:, t, :], self.src[:, t, :], ACT.Square,
                                         accum_out=small[:, self.col + t:self.col + t + 1]).then_inc(S_("norm_squared"), 1)

            def pool(self, pool):
                rstd(pool, "norm", self.index, self.col)

            def vector_scale(self, dve):
                for t in range(TT):
                    dve.wait_ge(S_("norm_rstd"), TT * self.index + t + 1)
                    nc.vector.tensor_scalar(self.scaled[:, t, :], self.src[:, t, :],
                                            smallp[:, self.col + t:self.col + t + 1], None, ALU.mult).then_inc(S_("norm_scaled"), 1)

            def tensor(self, pe):
                for t in range(TT):
                    pe.wait_ge(S_("norm_scaled"), TT * self.index + t + 1)
                    for k in range(KT):
                        o = ps[:, self.banks[k // 2], (k % 2) * S + t * P:(k % 2) * S + (t + 1) * P]
                        last = nc.tensor.transpose(o, self.scaled[:, t, k * P:(k + 1) * P], ident)
                        if t == TT - 1 and k % 2:
                            last.then_inc(S_("norm_transposed"), 1)

            def evacuate(self, eng, which):
                for k in range(KT):
                    if k // 2 % 2 != which:
                        continue
                    eng.wait_ge(S_("norm_transposed"), KT // 2 * self.index + k // 2 + 1)
                    src = ps[:, self.banks[k // 2], (k % 2) * S:(k % 2 + 1) * S]
                    done = S_(("norm_out_scalar", "norm_out_vector")[which])
                    if which == 0:
                        b = self.shift(k) if self.shift else 0.0
                        nc.scalar.activation(self.dst[:, k, :], src, ACT.Identity, scale=self.gain(k), bias=b).then_inc(done, 1)
                    elif self.shift:
                        nc.vector.tensor_scalar(self.dst[:, k, :], src, self.gain(k), self.shift(k), ALU.mult, ALU.add).then_inc(done, 1)
                    else:
                        nc.vector.tensor_scalar(self.dst[:, k, :], src, self.gain(k), None, ALU.mult).then_inc(done, 1)

            def done(self, eng):
                eng.wait_ge(S_("norm_out_scalar"), KT // 2 * (self.index + 1))
                eng.wait_ge(S_("norm_out_vector"), KT // 2 * (self.index + 1))

        def rstd(pool, name, index, col):
            for t in range(TT):
                pool.wait_ge(S_(name + "_squared"), TT * index + t + 1)
                c = slice(col + t, col + t + 1)
                nc.gpsimd.tensor_scalar(smallp[:, 32 + col + t:33 + col + t], small[:, c], 1.0 / D, EPS, ALU.mult, ALU.add).then_inc(S_("pool_step"), 1)
                pool_steps[0] += 1
                pool.wait_ge(S_("pool_step"), pool_steps[0])
                nc.gpsimd.tensor_tensor(smallp[:, c], smallp[:, 32 + col + t:33 + col + t], smallp[:, 31:32], ALU.pow).then_inc(S_(name + "_rstd"), 1)

        pool_steps = [0]

        class Residual:

            def __init__(self, index, col, gain, chunk, normed=True, gain_ready=None):
                self.index, self.col, self.gain, self.normed, self.gain_ready = index, col, gain, normed, gain_ready
                self.chunk = chunk

            def y_ready(self, eng, t):
                if t == 0:
                    eng.wait_ge(S_("out_y"), self.index + 1)
                else:
                    chunk_done(eng, self.chunk)

            def y(self, t):
                return ps[:, 2 * t:2 * t + 2, :]

            def scalar(self, act):
                if not self.normed:
                    return
                for t in range(TT):
                    self.y_ready(act, t)
                    nc.scalar.activation(xn[:, t, :].rearrange("p (a b) -> p a b", a=2), self.y(t), ACT.Square,
                                         accum_out=small[:, self.col + t:self.col + t + 1]).then_inc(S_("out_squared"), 1)

            def pool(self, pool):
                if self.normed:
                    rstd(pool, "out", self.index, self.col)

            def vector(self, dve):
                self.gain_ready(dve)
                g = self.gain.rearrange("p (a b) -> p a b", a=2)
                for t in range(TT):
                    tmp = xn[:, t, :].rearrange("p (a b) -> p a b", a=2)
                    if self.normed:
                        dve.wait_ge(S_("out_rstd"), TT * self.index + t + 1)
                        nc.vector.scalar_tensor_tensor(tmp, self.y(t), smallp[:, self.col + t:self.col + t + 1], g, ALU.mult, ALU.mult).then_inc(S_("out_gained"), 1)
                    else:
                        self.y_ready(dve, t)
                        nc.vector.tensor_tensor(tmp, self.y(t), g, ALU.mult).then_inc(S_("out_gained"), 1)
                    dve.wait_ge(S_("out_gained"), TT * self.index + t + 1)
                    nc.vector.tensor_tensor(x[:, t, :], x[:, t, :], xn[:, t, :], ALU.add).then_inc(S_("out_x"), 1)

            def x_ready(self, eng, t):
                eng.wait_ge(S_("out_x"), TT * self.index + t + 1)

        def gain_ready(i):
            return lambda dve: dve.wait_ge(S_("gain"), 16 * (i + 1))

        r_mix0 = Residual(0, 2, gains[:, 0, :], ("wo", 1, 0), gain_ready=gain_ready(0))
        r_ffn0 = Residual(1, 6, gains[:, 1, :], ("down", 0, 5), gain_ready=gain_ready(1))
        r_mix1 = Residual(2, 10, gains[:, 0, :], ("lout", 1, 0), gain_ready=gain_ready(2))
        r_ffn1 = Residual(3, 14, gains[:, 1, :], ("down", 1, 5), gain_ready=gain_ready(3))
        r_mix2 = Residual(4, 20, gates[:, 0, :], ("wo2", 1, 0), normed=False, gain_ready=lambda e: e.wait_ge(S_("ada_out"), 12))
        r_ffn2 = Residual(5, 24, gates[:, 1, :], ("down2", 5, 0), normed=False, gain_ready=lambda e: e.wait_ge(S_("ada_out"), 12))
        n_mix0 = Norm(0, 0, x, xn, hT, lambda k: pcol("mix_pre", k), None, lambda e, t: e.wait_ge(S_("x_in"), 16))
        n_ffn0 = Norm(1, 4, x, xn, hT, lambda k: pcol("ffn_pre", k), None, r_mix0.x_ready)
        n_mix1 = Norm(2, 8, x, xn, hT, lambda k: pcol("mix_pre", 8 + k), None, r_ffn0.x_ready)
        n_ffn1 = Norm(3, 12, x, xn, hT, lambda k: pcol("ffn_pre", 8 + k), None, r_mix1.x_ready)

        hT2 = region(2048, KT, 2 * S)
        ctxx = region(6144, TT, D)
        modc = small[:, 96:96 + 24]
        rope = region(8192, TT2, 2, P)
        lvl = region(9216, 2, LEVELS, P)
        qT = region(11008, H4, S)
        kT = region(12032, H4, 2 * S)
        vT = region(14080, H4, 2 * S)
        zt = region(16128, TT, 512)
        rgt = region(17152, TT, 512)
        rv = region(18176, TT2, H4, P)
        rk = region(20224, TT2, H4, P)
        rq = region(22272, TT, H4, P)
        cu = [region(23296 + 512 * b, 512) for b in range(2)]
        ct = [region(24320 + 512 * b, 512) for b in range(2)]
        wab = region(25344, KT, 16)
        normg2 = region(25472, 2, P)
        dec = region(25728, TT2, NG)
        beta = region(25792, TT2, 8)
        EX = region(25824, 5, TT2, NG)
        absc = region(26144, 8, 64)
        kn = region(0, TT2, H4, P)
        v_t = region(2048, TT2, H4, P)
        qn = region(4096, TT, H4, P)
        rqT = region(5120, H4, S)
        rkT = region(6144, H4, 2 * S)
        gS = region(14080, H4, P)
        E = region(14592, H4, P)
        ET = region(15104, H4, P)
        Am = region(15616, H4, P)
        X = region(23296, H4, P)
        XT = region(23808, H4, P)
        Yt = region(24320, H4, P)
        Rv = region(26656, H4, P)
        Rk = region(27168, H4, P)
        wT = region(27680, H4, P)
        kdec = region(28192, H4, P)
        vnew = region(28704, H4, P)
        Pm = region(29216, H4, P)
        tmp = region(29728, H4, P)
        St = region(8192, H4, P)
        rsq = region(8704, 32)
        sqk = region(26656, 3072)
        hw2 = region(30240, 60)
        tmpr = tmp
        AB = ps[:, 2, 0:64].rearrange("p (t c) -> p t c", t=TT2)
        condT = small[:, 64:80].rearrange("p (k c) -> p k c", k=KT)
        tmpc = sb("tmpc", [P, 40])

        TOKU = ([("z", t) for t in (2, 3)] + [("rq", t) for t in (2, 3)] + [("rk", t) for t in range(4)]
                + [("rv", t) for t in range(4)] + [("rg", t) for t in (2, 3)])
        TOKA = [sum(w in ("z", "rg", "rv") for w, _ in TOKU[:n]) for n in range(len(TOKU))]
        TOKV = [sum(w != "rv" for w, _ in TOKU[:n]) for n in range(len(TOKU))]

        WHATS = ("z", "rq", "rk", "rv", "rg")
        TOKP = [sum(t < 3 for _, t in TOKU[:n]) for n in range(len(TOKU))]

        def unit_done(eng, n):
            what, t = TOKU[n]
            if t < 3:
                eng.wait_ge(S_("tokproj"), TOKP[n] + 1)
            else:
                chunk_done(eng, ("win", 3 + WHATS.index(what), 0))

        def wait_unit(pe, n):
            if TOKU[n][0] == "rv":
                pe.wait_ge(S_("tok_act"), TOKA[n] + 1)
            else:
                pe.wait_ge(S_("tok_v"), TOKV[n] + 1)

        TRANS = ([("v", t) for t in range(4)] + [("kn", t) for t in range(4)] + [("qn", t) for t in (2, 3)]
                 + [("rkT", t) for t in range(4)] + [("rqT", t) for t in (2, 3)]
                 + [("knT", t) for t in range(4)] + [("qnT", t) for t in (2, 3)])
        ON_VECTOR = ("v", "kn", "qn")

        def trans_out(pe, n):
            mine = TRANS[n][0] in ON_VECTOR
            before = sum((w in ON_VECTOR) == mine for w, _ in TRANS[:n])
            pe.wait_ge(S_("trans_v" if mine else "trans_a"), before + 1)

        def B4(b):
            return ps[:, b, :].rearrange("p (h d) -> p h d", h=H4)

        def TB(n):
            return B4(n % 8)

        def LENAT(i):
            return (i % 4) * S + (i // 4) * P if i < 8 else 1024 + (i % 4) * 2 * S + ((i - 8) // 4) * P

        GROUPLIST = [(kind, dr, t) for kind in range(2) for dr in range(2) for t in ((0, 1, 2, 3), (1, 0, 3, 2))[dr]]
        DELTAS = [sum(g[0] == 0 for g in GROUPLIST[:n]) for n in range(16)]
        LATER = [sum(g[2] >= TT for g in GROUPLIST[:n]) for n in range(16)]
        DIFFS = [sum(g[0] == 0 or g[2] >= TT for g in GROUPLIST[:n]) for n in range(16)]
        UPDATES = [sum(m % 4 != 3 for m in range(n)) for n in range(16)]
        y2 = [region(22272, TT, H4, P), region(4096, TT, H4, P)]
        yT = region(2048, KT, S)

        n_ctx = Norm(4, 16, ctxx, ctxx, hT2[:, :, 0:S], lambda k: modc[:, 8 + k:9 + k], lambda k: modT[:, k, 1:2],
                     lambda e, t: (e.wait_ge(S_("ctx_in"), 16), r_ffn1.x_ready(e, t)))
        n_lat = Norm(5, 18, x, xn, hT2[:, :, S:2 * S], lambda k: modc[:, k:k + 1], lambda k: modT[:, k, 0:1], r_ffn1.x_ready)
        n_ffn2 = Norm(6, 22, x, xn, hT, lambda k: modc[:, 16 + k:17 + k], lambda k: modT[:, 24 + k, 0:1], r_mix2.x_ready)

        ORDER = attention_order()
        proj = [c for c in ORDER if c[0] in "VK"]
        UNIT = {c: 2 * i for i, c in enumerate(proj)}

        block = ctx.enter_context(nc.Block())

        @block.sync
        def _(sp):
            for s in range(NS):
                sp.dma_start(ring[:, s, :], A["W"][s]).then_inc(S_(f"landed{s}"), 16)
            with sp.Fori(1, NCH // NS) as r:
                for s in range(NS):
                    sp.wait_ge(S_("chunk_used"), NS * (r - 1) + s + 1)
                    sp.dma_start(ring[:, s, :], A["W"][r * NS + s]).then_inc(S_(f"landed{s}"), 16)
            for i in range(NCH // NS * NS, NCH):
                sp.wait_ge(S_("chunk_used"), i - NS + 1)
                sp.dma_start(ring[:, i % NS, :], A["W"][i]).then_inc(S_(f"landed{i % NS}"), 16)
            for t in range(TT):
                sp.wait_ge(S_("final"), t + 1)
                sp.dma_start(out[t * P:(t + 1) * P, :], xn[:, t, :]).then_inc(S_("stored"), 16)
            sp.wait_ge(S_("stored"), 16 * TT)

        @block.gpsimd
        def _(pool):
            nc.gpsimd.memset(smallp[:, 31:32], -0.5).then_inc(S_("pool_step"), 1)
            pool_steps[0] += 1
            pool.wait_ge(S_("pool_step"), 1)

            def load_gain(i):
                if i >= 2:
                    pool.wait_ge(S_("out_gained"), TT * (i - 1))
                pool.dma_start(gains[:, i % 2, :], A["gains"][i:i + 1, :].to_broadcast([P, D])).then_inc(S_("gain"), 16)
                pool.wait_ge(S_("gain"), 16 * (i + 1))

            for i in range(2):
                pool.dma_start(gates[:, i, :], A["ada_gate_b"][i:i + 1, :].to_broadcast([P, D])).then_inc(S_("gate_bias_in"), 16)
            load_gain(0)
            load_gain(1)
            n_mix0.pool(pool)
            r_mix0.pool(pool)
            n_ffn0.pool(pool)
            load_gain(2)
            r_ffn0.pool(pool)
            n_mix1.pool(pool)
            load_gain(3)
            r_mix1.pool(pool)
            n_ffn1.pool(pool)
            load_gain(4)
            r_ffn1.pool(pool)
            n_ctx.pool(pool)
            n_lat.pool(pool)
            pool.wait_ge(S_("lengths"), 1)
            nc.gpsimd.tensor_tensor(rsq[:, 0:24], rsq[:, 0:24], smallp[:, 31:32].to_broadcast([P, 24]), ALU.pow).then_inc(S_("lengths_r"), 1)
            pool.wait_ge(S_("head_var"), 1)
            nc.gpsimd.tensor_tensor(small[:, 160:176], small[:, 160:176], smallp[:, 31:32].to_broadcast([P, 16]), ALU.pow).then_inc(S_("head_rstd"), 1)
            n_ffn2.pool(pool)
            rstd(pool, "last", 0, 26)

        @block.scalar
        def _(act):
            nc_a = nc.scalar
            act.dma_start(x[:, :, :], A["x"].rearrange("(t p) d -> p t d", p=P)).then_inc(S_("x_in"), 16)
            act.dma_start(par[:, :], A["par"]).then_inc(S_("par_in"), 16)
            act.dma_start(cst[:, :, :], A["cst"][:, 0:6, :]).then_inc(S_("cst_in"), 16)
            act.dma_start(sel[:, :], A["sel"]).then_inc(S_("sel_in"), 16)
            act.dma_start(onehot[0:BUCKETS, :, :], A["onehot"]).then_inc(S_("rel_in"), 16)
            act.dma_start(relb[0:BUCKETS, :], A["rel_bias"]).then_inc(S_("rel_in"), 16)
            act.dma_start(negm[0:HEADS, :, :], A["negm"]).then_inc(S_("neg_in"), 16)
            act.wait_ge(S_("par_in"), 16)
            nc_a.activation(small[:, 64:80], pcol("cond", 0, 16), ACT.Tanh, scale=0.5).then_inc(S_("cond_tanh"), 1)
            n_mix0.scalar_square(act)
            act.wait_ge(S_("table"), 1)
            act.dma_start(table.ap(), wtab[0:HEADS, :, :].rearrange("h g n -> h (g n)").unsqueeze(1)
                          .to_broadcast([HEADS, P, GROUPS * WLEN])).then_inc(S_("table_out"), 16)
            act.wait_ge(S_("table_out"), 16)
            for h in range(HEADS):
                copies = GROUPS * WLEN
                skew = bass.AP(table, P - 1 + h * P * copies, [[copies - 1, P], [WLEN, GROUPS], [1, S]])
                act.dma_start(bias[:, h, :, :], skew).then_inc(S_("bias_in"), 16)
            n_mix0.evacuate(act, 0)

            for kind, a, g in ORDER:
                if kind in "VK":
                    for n in range(2):
                        unit = UNIT[(kind, a, g)] + n
                        if n == 0:
                            act.wait_ge(S_("proj"), unit // 2 + 1)
                        else:
                            chunk_done(act, (kind, a, g))
                        src = ps[:, unit % 3, :]
                        if kind == "V":
                            if a == 1:
                                act.wait_ge(S_("head_out"), 4)
                            dst = V[:, n, g, :, :].rearrange("p a b -> p (a b)")
                        else:
                            if a >= 2:
                                act.wait_ge(S_("scores"), 2 * a - 2)
                            dst = QKb[a % 2][:, g, 2 * n:2 * n + 2, :].rearrange("p a b -> p (a b)")
                        nc_a.activation(dst, src, ACT.Copy).then_inc(S_("proj_out"), 1)
                elif kind == "S":
                    act.wait_ge(S_("logits"), a + 1)
                    for t, c in ((1, slice(0, 256)), (0, slice(256, 384))):
                        last = nc_a.activation(L[a % 2][:, :, c], L[a % 2][:, :, c], ACT.Exp, bias=small[:, 80 + t:81 + t],
                                               accum_out=small[:, 82 + t:83 + t])
                        last.then_inc(S_("exps"), 1)
                elif kind == "T":
                    if a:
                        act.wait_ge(S_("head_out"), a)
                    for n, m in ((0, 4), (1, 4), (2, 1)):
                        act.wait_ge(S_("pT"), 3 * a + n + 1)
                        src = ps[:, 6 + n % 2, 0:m * P].rearrange("p (a b) -> p a b", a=m)
                        nc_a.activation(PT[:, 4 * n:4 * n + m, :], src, ACT.Copy).then_inc(S_("pT_out"), 1)
                else:
                    act.wait_ge(S_("head_out"), a + 1)
                    nc_a.activation(oT[:, a, :].rearrange("p (t q) -> p t q", t=2), ps[:, 7, 0:S].rearrange("p (t q) -> p t q", t=2), ACT.Copy).then_inc(S_("oT"), 1)

            def ada_rows(i):
                chunk_done(act, ("ada", i, 0))
                if i >= 2:
                    act.wait_ge(S_("ada_t"), i - 1)
                nc_a.activation(row[:, i % 2, :], ps[0:2, 5 + i % 2, :], ACT.Copy).then_inc(S_("ada_row_out"), 1)

            def gated_ffn(layer):
                for j in range(12):
                    chunk_done(act, ("up", layer, j))
                    if j >= 2:
                        act.wait_ge(S_("aT"), 12 * layer + j - 1)
                    for n in range(4):
                        ft = 2 * j + n % 2 + FT * (n // 2)
                        src = ps[:, 4 + 2 * (j % 2) + n // 2, (n % 2) * S:(n % 2 + 1) * S]
                        last = nc_a.activation(u[j % 2][:, n, :], src, ACT.Identity,
                                               scale=pcol("ffn_conv_w", (layer * 3 + 2) * 48 + ft), bias=pcol("ffn_conv_b", layer * 48 + ft))
                    last.then_inc(S_("tap"), 1)
                    act.wait_ge(S_("conv"), 12 * layer + j + 1)
                    nc_a.activation(gl[j % 2][:, :, :], u[j % 2][:, 0:2, :], ACT.Gelu_apprx_tanh).then_inc(S_("gelu"), 1)

            r_mix0.scalar(act)
            for i in range(0, 3):
                ada_rows(i)
            n_ffn0.scalar_square(act)
            n_ffn0.evacuate(act, 0)
            act.dma_start(lgw[:, :, :, :, :], A["gate_w"]).then_inc(S_("gate_w_in"), 16)
            act.wait_ge(S_("lam_abs"), 1)
            nc_a.activation(tmpc[:, 0:8], tmpc[:, 0:8], ACT.Exp).then_inc(S_("lam_exp"), 1)
            gated_ffn(0)
            r_ffn0.scalar(act)
            for i in range(3, 6):
                ada_rows(i)
            n_mix1.scalar_square(act)
            n_mix1.evacuate(act, 0)

            act.wait_ge(S_("lru_consts"), 1)

            def lru_taps(i):
                chunk_done(act, ("lin", i, 0))
                for n in range(2):
                    ft = 2 * i + n
                    nc_a.activation(xc[:, ft, :], ps[:, 4 + 2 * (i % 2), n * S:(n + 1) * S], ACT.Identity,
                                    scale=pcol("lru_conv_w", 24 + ft), bias=pcol("lru_conv_b", ft)).then_inc(S_("lru_tap"), 1)
                nc_a.activation(gb[:, 2 * i:2 * i + 2, :].rearrange("p a b -> p (a b)"), ps[:, 5 + 2 * (i % 2), :], ACT.Copy).then_inc(S_("lru_gb"), 1)

            def lru_gates(i):
                act.wait_ge(S_("lgate"), i + 1)
                for n in range(2):
                    ft = 2 * i + n
                    nc_a.activation(tr[:, ft, :], ps[:, 2 * (i % 2), n * S:(n + 1) * S], ACT.Tanh, scale=0.5, bias=small[:, 112 + ft:113 + ft])
                    nc_a.activation(ti[:, ft, :], ps[:, 2 * (i % 2) + 1, n * S:(n + 1) * S], ACT.Tanh, scale=0.5, bias=small[:, 120 + ft:121 + ft]).then_inc(S_("lru_tanh"), 1)
                for n in range(2):
                    ft = 2 * i + n
                    act.wait_ge(S_("lru_tanh"), ft + 1)
                    nc_a.activation(av[:, ft, :], tr[:, ft, :], ACT.Exp, scale=small[:, 128 + ft:129 + ft], bias=small[:, 128 + ft:129 + ft])
                    nc_a.activation(th[:, ft, :], tr[:, ft, :], ACT.Tanh, scale=small[:, 136 + ft:137 + ft], bias=small[:, 136 + ft:137 + ft]).then_inc(S_("lru_exp"), 1)

            lru_taps(0)
            for i in range(1, 4):
                lru_taps(i)
                lru_gates(i - 1)
            lru_gates(3)
            act.wait_ge(S_("lru_sq"), 1)
            nc_a.activation(mu[:, :, :], mu[:, :, :], ACT.Sqrt).then_inc(S_("lru_mult"), 1)
            nc_a.activation(gb[:, :, :], gb[:, :, :], ACT.Gelu_apprx_tanh).then_inc(S_("lru_gelu"), 1)

            r_mix1.scalar(act)
            for i in range(6, 9):
                ada_rows(i)
            n_ffn1.scalar_square(act)
            n_ffn1.evacuate(act, 0)
            gated_ffn(1)
            r_ffn1.scalar(act)
            act.dma_start(ctxx[:, :, :], A["ctx"].rearrange("(t p) d -> p t d", p=P)).then_inc(S_("ctx_in"), 16)
            act.dma_start(rope[:, :, :, :], A["rope"]).then_inc(S_("rope_in"), 16)
            act.dma_start(lvl[:, :, :, :], A["cst"][:, 6:, :].rearrange("p (d l) m -> p d l m", d=2)).then_inc(S_("lvl_in"), 16)
            act.dma_start(wab[:, :, :], A["wab"]).then_inc(S_("wab_in"), 16)
            act.dma_start(normg2[:, :, :], A["normg2"].unsqueeze(0).to_broadcast([P, 2, P])).then_inc(S_("normg2_in"), 16)
            act.dma_start(absc[:, 7, 0:24], A["head_vec"].to_broadcast([P, 24])).then_inc(S_("headv_in"), 16)
            n_ctx.scalar_square(act)
            for i in range(9, 12):
                ada_rows(i)
            n_ctx.evacuate(act, 0)
            n_lat.scalar_square(act)
            n_lat.evacuate(act, 0)

            def conv_taps(n):
                if n % 4 < 3:
                    act.wait_ge(S_("qkv"), n // 4 * 3 + n % 4 + 1)
                else:
                    chunk_done(act, ("win", n // 4, 0))
                if n >= 2:
                    act.wait_ge(S_("qkv_silu"), n - 1)
                w = S if n < H4 else 2 * S
                nc_a.activation(cu[n % 2][:, 0:w], ps[:, n % 8, 0:w], ACT.Identity, scale=hw2[:, 2 * 12 + n:2 * 12 + n + 1]).then_inc(S_("qkv_tap"), 1)

            def conv_tanh(n):
                w = S if n < H4 else 2 * S
                act.wait_ge(S_("qkv_conv"), n + 1)
                nc_a.activation(ct[n % 2][:, 0:w], cu[n % 2][:, 0:w], ACT.Tanh).then_inc(S_("qkv_tanh"), 1)

            act.wait_ge(S_("half_w"), 1)
            for n in range(12):
                conv_taps(n)
                conv_tanh(n)
            for n, (what, t) in enumerate(TOKU):
                unit_done(act, n)
                src = ps[:, (12 + n) % 8, :]
                if what in ("z", "rg"):
                    dst = (zt if what == "z" else rgt)[:, t - TT, :]
                    nc_a.activation(dst, src, ACT.Tanh, scale=0.5).then_inc(S_("tok_act"), 1)
                elif what == "rv":
                    nc_a.activation(rv[:, t, :, :].rearrange("p a b -> p (a b)"), src, ACT.Copy).then_inc(S_("tok_act"), 1)
            act.wait_ge(S_("ab"), 1)
            act.wait_ge(S_("headv_in"), 16)
            nc_a.activation(beta[:, :, :], AB[:, :, 8:16], ACT.Tanh, scale=0.5).then_inc(S_("beta_tanh"), 1)
            nc_a.activation(absc[:, 6, 0:8], absc[:, 7, 0:8], ACT.Exp).then_inc(S_("a_exp"), 1)
            act.wait_ge(S_("sp_in"), 1)
            nc_a.activation(absc[:, 1, 0:40], absc[:, 1, 0:40], ACT.Exp).then_inc(S_("sp_exp"), 1)
            act.wait_ge(S_("qkv_silu"), 12)
            nc_a.activation(sqk[:, 0:1024], qT.rearrange("p a b -> p (a b)"), ACT.Square)
            nc_a.activation(sqk[:, 1024:3072], kT.rearrange("p a b -> p (a b)"), ACT.Square).then_inc(S_("qk_sq"), 1)
            act.wait_ge(S_("sums"), 1)
            nc_a.activation(EX[:, :, :, :].rearrange("p a b c -> p (a b c)"), ps[:, 0, 0:320], ACT.Exp).then_inc(S_("EX"), 1)

            for n in range(len(TRANS)):
                what, t = TRANS[n]
                if what in ("rqT", "rkT", "knT", "qnT"):
                    act.wait_ge(S_("trans"), n + 1)
                    dst = {"rqT": rqT, "rkT": rkT, "knT": kT, "qnT": qT}[what]
                    tt = t - TT if what in ("rqT", "qnT") else t
                    sc = HD_SCALE if what in ("rqT", "qnT") else 1.0
                    nc_a.activation(dst[:, :, tt * P:(tt + 1) * P], TB(n), ACT.Copy, scale=sc).then_inc(S_("trans_a"), 1)

            for n, (kind, dr, t) in enumerate(GROUPLIST):
                lat = t >= TT
                first = n % 4 == 0
                if kind == 0 or lat:
                    act.wait_ge(S_("diff"), DIFFS[n] + 1)
                if kind == 0:
                    nc_a.activation(E[:, :, :], B4(0), ACT.Exp).then_inc(S_("E"), 1)
                if lat:
                    nc_a.activation(ET[:, :, :], B4(1), ACT.Exp).then_inc(S_("ET"), 1)
                if kind == 0:
                    act.wait_ge(S_("wT"), DELTAS[n] + 1)
                    nc_a.activation(wT[:, :, :], B4(2), ACT.Copy, scale=-1.0).then_inc(S_("wT_out"), 1)
                    act.wait_ge(S_("vnew"), DELTAS[n] + 1)
                    nc_a.activation(vnew[:, :, :], B4(3), ACT.Copy).then_inc(S_("vnew_out"), 1)

            act.wait_ge(S_("centred"), 1)
            for t in range(TT):
                for m in range(8):
                    nc_a.activation(kn[:, t * 2 + m // 4, m % 4, :], y2[m // 4][:, t, m % 4, :], ACT.Square,
                                    accum_out=small[:, 144 + t * 8 + m:145 + t * 8 + m]).then_inc(S_("head_sq"), 1)
            for b in (0, 2):
                act.wait_ge(S_("yT"), b + 1)
                nc_a.activation(yT[:, 2 * b:2 * b + 2, :].rearrange("p a b -> p (a b)"), ps[:, 4 + b, :], ACT.Copy).then_inc(S_("yT_a"), 1)
            n_ffn2.scalar_square(act)
            n_ffn2.evacuate(act, 0)
            for j in range(11):
                chunk_done(act, ("up2", j, 0))
                if j >= 2:
                    act.wait_ge(S_("aT2"), j - 1)
                nc_a.activation(gl[j % 2].rearrange("p a b -> p (a b)"), ps[:, 4 + 2 * (j % 2), :], ACT.Tanh, scale=0.5).then_inc(S_("tanh2"), 1)
            for t in range(TT):
                r_ffn2.x_ready(act, t)
                nc_a.activation(xn[:, t, :], x[:, t, :], ACT.Square, accum_out=small[:, 26 + t:27 + t]).then_inc(S_("last_squared"), 1)

        @block.vector
        def _(dve):
            v = nc.vector
            steps = [0]

            def link(ins):
                steps[0] += 1
                ins.then_inc(S_("vector_step"), 1)
                dve.wait_ge(S_("vector_step"), steps[0])

            n_mix0.vector_scale(dve)
            dve.wait_ge(S_("cond_tanh"), 1)
            link(v.scalar_tensor_tensor(small[:, 64:80], small[:, 64:80], 1.0, pcol("cond", 0, 16), ALU.add, ALU.mult))
            v.tensor_scalar(small[:, 64:80], small[:, 64:80], 0.5, None, ALU.mult).then_inc(S_("cond"), 1)
            dve.wait_ge(S_("neg_in"), 16)
            dve.wait_ge(S_("tables"), 1)
            v.tensor_tensor(wtab[0:HEADS, :, :], ps[0:HEADS, 0:3, 0:WLEN], negm[0:HEADS, :, :], ALU.add).then_inc(S_("table"), 1)
            n_mix0.evacuate(dve, 1)
            dve.wait_ge(S_("bias_in"), 16 * HEADS)
            for kind, h, _ in ORDER:
                if kind == "S":
                    Lh = L[h % 2]
                    dve.wait_ge(S_("scores"), h + 1)
                    if h >= 2:
                        dve.wait_ge(S_("pT"), 3 * (h - 1))
                    v.scalar_tensor_tensor(Lh[:, :, 0:256], ps[:, 3:6, 0:256], HD_SCALE, bias[:, h, :, :], ALU.mult, ALU.add)
                    link(v.scalar_tensor_tensor(Lh[:, :, 256:384], ps[:, 3:6, 256:384], HD_SCALE, bias[:, h, :, 128:256], ALU.mult, ALU.add))
                    if h:
                        dve.wait_ge(S_("exps"), 2 * h)
                    v.tensor_reduce(small[:, 81:82], Lh[:, :, 0:256], AX.XY, ALU.max, negate=True)
                    v.tensor_reduce(small[:, 80:81], Lh[:, :, 256:384], AX.XY, ALU.max, negate=True).then_inc(S_("logits"), 1)
                    dve.wait_ge(S_("exps"), 2 * h + 2)
                    link(v.reciprocal(small[:, 84:86], small[:, 82:84]))
                    v.tensor_scalar(Lh[:, :, 0:256], Lh[:, :, 0:256], small[:, 85:86], None, ALU.mult)
                    v.tensor_scalar(Lh[:, :, 256:384], Lh[:, :, 256:384], small[:, 84:85], None, ALU.mult).then_inc(S_("probs"), 1)

            def ada_out(i):
                dve.wait_ge(S_("ada_t"), i + 1)
                if i // 2 in (2, 5):
                    dve.wait_ge(S_("gate_bias_in"), 32)
                    gg = gates[:, (i // 2) // 3, (i % 2) * 512:(i % 2 + 1) * 512]
                    v.tensor_tensor(gg, gg, ps[:, 7, :], ALU.add).then_inc(S_("ada_out"), 1)
                else:
                    v.tensor_tensor(modT[:, 4 * i:4 * i + 4, :], ps[:, 7, 0:8].rearrange("p (a b) -> p a b", a=4),
                                    pcol("ada_b", 4 * i, 4).unsqueeze(2).to_broadcast([P, 4, 2]), ALU.add).then_inc(S_("ada_out"), 1)

            def gated_ffn(layer):
                for j in range(12):
                    dve.wait_ge(S_("tap"), 12 * layer + j + 1)
                    for tap, sh in ((1, 1), (0, 2)):
                        for n in range(4):
                            ft = 2 * j + n % 2 + FT * (n // 2)
                            src = ps[:, 4 + 2 * (j % 2) + n // 2, (n % 2) * S:(n % 2 + 1) * S - sh]
                            dst = u[j % 2][:, n, sh:S]
                            last = v.scalar_tensor_tensor(dst, src, pcol("ffn_conv_w", (layer * 3 + tap) * 48 + ft), dst, ALU.mult, ALU.add)
                        if tap:
                            link(last)
                    last.then_inc(S_("conv"), 1)
                    dve.wait_ge(S_("gelu"), 12 * layer + j + 1)
                    v.tensor_tensor(aT[:, 2 * j:2 * j + 2, :], gl[j % 2][:, :, :], u[j % 2][:, 2:4, :], ALU.mult).then_inc(S_("aT"), 1)

            def log1p_exp_neg(e, w, w2, acc, n):
                link(v.tensor_scalar(w, e, 2.0, None, ALU.add))
                link(v.reciprocal(w, w))
                link(v.tensor_tensor(w, w, e, ALU.mult))
                link(v.tensor_tensor(w2, w, w, ALU.mult))
                link(v.tensor_scalar(acc, w2, 2.0 / 15, 2.0 / 13, ALU.mult, ALU.add))
                for c in (11, 9, 7, 5, 3, 1):
                    link(v.tensor_tensor(acc, acc, w2, ALU.mult))
                    link(v.tensor_scalar(acc, acc, 2.0 / c, None, ALU.add))
                link(v.tensor_tensor(acc, acc, w, ALU.mult))

            r_mix0.vector(dve)
            for i in range(0, 3):
                ada_out(i)
            n_ffn0.vector_scale(dve)
            n_ffn0.evacuate(dve, 1)
            dve.wait_ge(S_("par_in"), 16)
            v.tensor_scalar(small[:, 112:128], pcol("ga_b", 0, 16), 0.5, None, ALU.mult)
            lam = pcol("lam", 0, 8)
            link(v.tensor_scalar(tmpc[:, 0:8], lam, -1.0, None, ALU.mult))
            v.tensor_tensor(tmpc[:, 0:8], tmpc[:, 0:8], lam, ALU.min).then_inc(S_("lam_abs"), 1)
            dve.wait_ge(S_("lam_exp"), 1)
            log1p_exp_neg(tmpc[:, 0:8], tmpc[:, 8:16], tmpc[:, 16:24], tmpc[:, 24:32], 8)
            link(v.tensor_scalar(tmpc[:, 0:8], lam, 0.0, None, ALU.min))
            link(v.tensor_tensor(tmpc[:, 0:8], tmpc[:, 0:8], tmpc[:, 24:32], ALU.subtract))
            v.tensor_scalar(small[:, 128:136], tmpc[:, 0:8], 4.0, None, ALU.mult)
            v.tensor_scalar(small[:, 136:144], tmpc[:, 0:8], -4.0, None, ALU.mult).then_inc(S_("lru_consts"), 1)
            gated_ffn(0)
            r_ffn0.vector(dve)
            for i in range(3, 6):
                ada_out(i)
            n_mix1.vector_scale(dve)
            n_mix1.evacuate(dve, 1)

            def lru_conv(i):
                dve.wait_ge(S_("lru_tap"), 2 * i + 2)
                for sh in (1, 2, 3):
                    for n in range(2):
                        ft = 2 * i + n
                        dst = xc[:, ft, sh:S]
                        src = ps[:, 4 + 2 * (i % 2), n * S:(n + 1) * S - sh]
                        last = v.scalar_tensor_tensor(dst, src, pcol("lru_conv_w", (3 - sh) * 8 + ft), dst, ALU.mult, ALU.add)
                    if sh < 3:
                        link(last)
                last.then_inc(S_("lru_xc"), 1)

            def lru_in(i):
                b2 = slice(2 * i, 2 * i + 2)
                dve.wait_ge(S_("lru_exp"), 2 * i + 2)
                link(v.tensor_tensor(mu[:, b2, :], av[:, b2, :], av[:, b2, :], ALU.mult))
                last = v.scalar_tensor_tensor(mu[:, b2, :], mu[:, b2, :], 1.0, th[:, b2, :], ALU.add, ALU.mult)
                if i == 3:
                    last.then_inc(S_("lru_sq"), 1)
                link(v.scalar_tensor_tensor(ti[:, b2, :], ti[:, b2, :], 1.0, xc[:, b2, :], ALU.add, ALU.mult))

            lru_conv(0)
            for i in range(1, 4):
                lru_conv(i)
                lru_in(i - 1)
            lru_in(3)
            dve.wait_ge(S_("lru_mult"), 1)
            link(v.scalar_tensor_tensor(ti[:, :, :], ti[:, :, :], 0.5, mu[:, :, :], ALU.mult, ALU.mult))
            for ft in range(KT):
                last = v.tensor_tensor_scan(th[:, ft, :], av[:, ft, :], ti[:, ft, :], 0.0, ALU.mult, ALU.add)
            link(last)
            dve.wait_ge(S_("lru_gelu"), 1)
            v.tensor_tensor(lT[:, :, :], th[:, :, :], gb[:, :, :], ALU.mult).then_inc(S_("lT"), 1)

            r_mix1.vector(dve)
            for i in range(6, 9):
                ada_out(i)
            n_ffn1.vector_scale(dve)
            n_ffn1.evacuate(dve, 1)
            gated_ffn(1)
            r_ffn1.vector(dve)
            n_ctx.vector_scale(dve)
            for i in range(9, 12):
                ada_out(i)
            for at, name, blk, which in ((0, "mix_g2", 8, 0), (8, "mix_g2", 8, 1), (16, "ffn_g2", 32, 0)):
                v.scalar_tensor_tensor(modc[:, at:at + 8], modT[:, blk:blk + 8, which:which + 1].rearrange("p a b -> p (a b)"),
                                       1.0, pcol(name, 0, 8), ALU.add, ALU.mult).then_inc(S_("modc"), 1)
            v.tensor_scalar(hw2[:, :], pcol("conv_w2", 0, 60), 0.5, None, ALU.mult).then_inc(S_("half_w"), 1)
            dve.wait_ge(S_("modc"), 3)
            dve.wait_ge(S_("half_w"), 1)
            n_ctx.evacuate(dve, 1)
            n_lat.vector_scale(dve)
            n_lat.evacuate(dve, 1)

            for n in range(12):
                dve.wait_ge(S_("qkv_tap"), n + 1)
                segs = 1 if n < H4 else 2
                src3 = ps[:, n % 8, 0:segs * S].rearrange("p (a b) -> p a b", a=segs)
                dst3 = cu[n % 2][:, 0:segs * S].rearrange("p (a b) -> p a b", a=segs)
                for tap in (0, 1, 3, 4):
                    d = tap - 2
                    if d < 0:
                        o_, i_ = dst3[:, :, -d:S], src3[:, :, 0:S + d]
                    else:
                        o_, i_ = dst3[:, :, 0:S - d], src3[:, :, d:S]
                    last = v.scalar_tensor_tensor(o_, i_, hw2[:, tap * 12 + n:tap * 12 + n + 1], o_, ALU.mult, ALU.add)
                    if tap < 4:
                        link(last)
                last.then_inc(S_("qkv_conv"), 1)
                dve.wait_ge(S_("qkv_tanh"), n + 1)
                w = segs * S
                dst = (qT[:, n, :] if n < 4 else kT[:, n - 4, :] if n < 8 else vT[:, n - 8, :])
                v.scalar_tensor_tensor(dst, ct[n % 2][:, 0:w], 1.0, cu[n % 2][:, 0:w], ALU.add, ALU.mult).then_inc(S_("qkv_silu"), 1)

            dve.wait_ge(S_("rope_in"), 16)
            for n, (what, t) in enumerate(TOKU):
                src = ps[:, (12 + n) % 8, :]
                s3 = src.rearrange("p (h d) -> p h d", h=H4)
                if what in ("z", "rg"):
                    dst = (zt if what == "z" else rgt)[:, t - TT, :]
                    dve.wait_ge(S_("tok_act"), TOKA[n] + 1)
                    v.scalar_tensor_tensor(dst, dst, 1.0, src, ALU.add, ALU.mult).then_inc(S_("tok_v"), 1)
                elif what in ("rq", "rk"):
                    unit_done(dve, n)
                    dst = rq[:, t - TT, :, :] if what == "rq" else rk[:, t, :, :]
                    cosb = rope[:, t, 0:1, :].to_broadcast([P, H4, P])
                    v.tensor_tensor(dst, s3, cosb, ALU.mult)
                    v.tensor_tensor(tmpr[:, :, 0:64], s3[:, :, 64:128], rope[:, t, 1:2, 0:64].to_broadcast([P, H4, 64]), ALU.mult)
                    link(v.tensor_tensor(tmpr[:, :, 64:128], s3[:, :, 0:64], rope[:, t, 1:2, 64:128].to_broadcast([P, H4, 64]), ALU.mult))
                    v.tensor_tensor(dst, dst, tmpr[:, :, :], ALU.add).then_inc(S_("tok_v"), 1)
                    dve.wait_ge(S_("tok_v"), TOKV[n] + 1)
            dve.wait_ge(S_("beta_tanh"), 1)
            dve.wait_ge(S_("headv_in"), 16)
            z0, z1, z2, z3, z4 = (absc[:, i, 0:40] for i in range(5))
            v.tensor_tensor(absc[:, 0, 0:32].rearrange("p (a b) -> p a b", a=TT2), AB[:, :, 0:8],
                            absc[:, 7:8, 8:16].to_broadcast([P, TT2, 8]), ALU.add)
            link(v.tensor_scalar(absc[:, 0, 32:40], absc[:, 7, 16:24], -1.0, None, ALU.mult))
            link(v.tensor_scalar(z1, z0, -1.0, None, ALU.mult))
            v.tensor_tensor(z1, z1, z0, ALU.min).then_inc(S_("sp_in"), 1)
            dve.wait_ge(S_("sp_exp"), 1)
            log1p_exp_neg(z1, z2, z3, z4, 40)
            link(v.tensor_scalar(z0, z0, 0.0, None, ALU.max))
            link(v.tensor_tensor(z0, z0, z4, ALU.add))
            link(v.tensor_scalar(z0, z0, -1.0, None, ALU.mult))
            dve.wait_ge(S_("a_exp"), 1)
            v.tensor_tensor(dec[:, :, 0:8], absc[:, 0, 0:32].rearrange("p (a b) -> p a b", a=TT2),
                            absc[:, 6:7, 0:8].to_broadcast([P, TT2, 8]), ALU.mult)
            v.tensor_copy(dec[:, :, 8:16], absc[:, 0:1, 32:40].to_broadcast([P, TT2, 8])).then_inc(S_("dec"), 1)
            dve.wait_ge(S_("beta_tanh"), 1)
            v.tensor_scalar(beta[:, :, :], beta[:, :, :], 0.5, 0.5, ALU.mult, ALU.add).then_inc(S_("beta"), 1)
            dve.wait_ge(S_("lens"), 1)
            v.tensor_scalar(rsq[:, 0:24], ps[:, 1, 0:24], EPS, None, ALU.add).then_inc(S_("lengths"), 1)
            dve.wait_ge(S_("lengths_r"), 1)
            for n in range(len(TRANS)):
                what, t = TRANS[n]
                if what in ("v", "kn", "qn"):
                    dve.wait_ge(S_("trans"), n + 1)
                    if what == "v":
                        v.tensor_copy(v_t[:, t, :, :], TB(n)).then_inc(S_("trans_v"), 1)
                    else:
                        c = 8 + t * 4 if what == "kn" else (t - TT) * 4
                        dst = kn[:, t, :, :] if what == "kn" else qn[:, t - TT, :, :]
                        v.tensor_tensor(dst, TB(n), rsq[:, c:c + 4].unsqueeze(2).to_broadcast([P, H4, P]), ALU.mult).then_inc(S_("trans_v"), 1)

            dve.wait_ge(S_("trans_v"), 10)
            dve.wait_ge(S_("EX"), 1)
            dve.wait_ge(S_("beta"), 1)
            dve.wait_ge(S_("lvl_in"), 16)
            for n, (kind, dr, t) in enumerate(GROUPLIST):
                lat = t >= TT
                first = n % 4 == 0
                last_of_dir = n % 4 == 3
                col = 8 * kind + 4 * dr
                kt_ = kn if kind == 0 else rk
                gi = DELTAS[n]
                eG = EX[:, C_LE if dr == 0 else C_GE, t, col:col + 4]
                eSuf = EX[:, C_GT if dr == 0 else C_LT, t, col:col + 4]
                bc = lambda a: a.unsqueeze(2).to_broadcast([P, H4, P])
                if DIFFS[n]:
                    dve.wait_ge(S_("diff"), DIFFS[n])
                smask = cst[:, C_GT if dr == 0 else C_LT, :]
                if kind == 0 or lat:
                    v.tensor_tensor(gS[:, :, :], smask.unsqueeze(1).to_broadcast([P, H4, P]), bc(dec[:, t, col:col + 4]), ALU.mult).then_inc(S_("gS"), 1)
                if UPDATES[n]:
                    dve.wait_ge(S_("dS"), UPDATES[n])
                v.tensor_tensor(kdec[:, :, :], kt_[:, t, :, :], bc(eSuf), ALU.mult).then_inc(S_("kdec"), 1)
                if kind == 0:
                    bt = beta[:, t, 4 * dr:4 * dr + 4]
                    if gi:
                        dve.wait_ge(S_("vnew"), gi)
                    v.tensor_tensor(small[:, 176:180], bt, eG, ALU.mult).then_inc(S_("beg"), 1)
                    v.tensor_tensor(Rv[:, :, :], v_t[:, t, :, :], bc(bt), ALU.mult)
                    dve.wait_ge(S_("beg"), gi + 1)
                    v.tensor_tensor(Rk[:, :, :], kn[:, t, :, :], bc(small[:, 176:180]), ALU.mult).then_inc(S_("R"), 1)
                    dve.wait_ge(S_("E"), gi + 1)
                    dve.wait_ge(S_("kk"), gi + 1)
                    link(v.tensor_tensor(Am[:, :, :], B4(4), E[:, :, :], ALU.mult))
                    v.tensor_tensor(Am[:, :, :], Am[:, :, :], bc(bt), ALU.mult)
                    v.tensor_copy(X[:, :, :], ident.unsqueeze(1).to_broadcast([P, H4, P]))
                    v.tensor_copy(XT[:, :, :], ident.unsqueeze(1).to_broadcast([P, H4, P])).then_inc(S_("A"), 1)
                    for l in range(LEVELS):
                        m = lvl[:, dr, l, :].unsqueeze(1).to_broadcast([P, H4, P])
                        dve.wait_ge(S_("Y"), gi * LEVELS + l + 1)
                        v.tensor_tensor(Yt[:, :, :], B4(5), m, ALU.mult).then_inc(S_("Y_out"), 1)
                        dve.wait_ge(S_("Z"), gi * LEVELS + l + 1)
                        v.tensor_tensor(XT[:, :, :], XT[:, :, :], B4(6), ALU.subtract)
                        v.tensor_tensor(X[:, :, :], X[:, :, :], B4(7), ALU.subtract).then_inc(S_("X_out"), 1)
                if lat:
                    dve.wait_ge(S_("ET"), LATER[n] + 1)
                    imask = cst[:, C_LE if dr == 0 else C_GE, :].unsqueeze(1).to_broadcast([P, H4, P])
                    link(v.tensor_tensor(ET[:, :, :], ET[:, :, :], imask, ALU.mult))
                    dve.wait_ge(S_("qk"), LATER[n] + 1)
                    v.tensor_tensor(Pm[:, :, :], B4(5), ET[:, :, :], ALU.mult).then_inc(S_("Pm"), 1)
                    dve.wait_ge(S_("o"), LATER[n] + 1)
                    o_ = y2[kind][:, t - TT, :, :]
                    if dr == 0:
                        v.tensor_tensor(tmp[:, :, :], B4(6), bc(eG), ALU.mult)
                        v.tensor_copy(o_, B4(7)).then_inc(S_("o_part"), 1)
                    else:
                        v.tensor_tensor(tmp[:, :, :], B4(6), bc(eG), ALU.mult)
                        v.tensor_tensor(o_, o_, B4(7), ALU.add).then_inc(S_("o_part"), 1)
                    dve.wait_ge(S_("o_part"), LATER[n] + 1)
                    v.tensor_tensor(o_, o_, tmp[:, :, :], ALU.add).then_inc(S_("o_out"), 1)
                    dve.wait_ge(S_("o_out"), LATER[n] + 1)
                if not last_of_dir:
                    dve.wait_ge(S_("dS"), UPDATES[n] + 1)
                    if first:
                        v.tensor_copy(St[:, :, :], B4(0)).then_inc(S_("state"), 1)
                    else:
                        for h in range(H4):
                            last = v.scalar_tensor_tensor(St[:, h, :], St[:, h, :], EX[:, C_ONE, t, col + h:col + h + 1],
                                                          ps[:, 0, h * P:(h + 1) * P], ALU.mult, ALU.add)
                        last.then_inc(S_("state"), 1)

            for t in range(TT):
                last = v.tensor_reduce(small[:, 180 + 4 * t:184 + 4 * t], y2[1][:, t, :, :], AX.X, ALU.add)
            link(last)
            link(v.tensor_scalar(tmpc[:, 0:8], small[:, 180:188], 1.0 / P, None, ALU.mult))
            for t in range(TT):
                last = v.tensor_tensor(y2[1][:, t, :, :], y2[1][:, t, :, :], tmpc[:, 4 * t:4 * t + 4].unsqueeze(2).to_broadcast([P, H4, P]), ALU.subtract)
            last.then_inc(S_("centred"), 1)
            dve.wait_ge(S_("head_sq"), 16)
            v.tensor_scalar(small[:, 160:176], small[:, 144:160], 1.0 / P, EPS, ALU.mult, ALU.add).then_inc(S_("head_var"), 1)
            dve.wait_ge(S_("head_rstd"), 1)
            dve.wait_ge(S_("normg2_in"), 16)
            for t in range(TT):
                for kind in range(2):
                    y = y2[kind][:, t, :, :]
                    c = 160 + t * 8 + kind * 4
                    link(v.tensor_tensor(y, y, small[:, c:c + 4].unsqueeze(2).to_broadcast([P, H4, P]), ALU.mult))
                    link(v.tensor_tensor(y, y, normg2[:, kind:kind + 1, :].to_broadcast([P, H4, P]), ALU.mult))
                    gt = (zt if kind == 0 else rgt)[:, t, :].rearrange("p (a b) -> p a b", a=H4)
                    v.scalar_tensor_tensor(y, y, 0.5, gt, ALU.mult, ALU.mult).then_inc(S_("mixed"), 1)
            for b in (1, 3):
                dve.wait_ge(S_("yT"), b + 1)
                v.tensor_copy(yT[:, 2 * b:2 * b + 2, :].rearrange("p a b -> p (a b)"), ps[:, 4 + b, :]).then_inc(S_("yT_v"), 1)
            r_mix2.vector(dve)
            n_ffn2.vector_scale(dve)
            n_ffn2.evacuate(dve, 1)
            for j in range(11):
                g_, u_ = ps[:, 4 + 2 * (j % 2), :], ps[:, 5 + 2 * (j % 2), :]
                glj = gl[j % 2].rearrange("p a b -> p (a b)")
                dve.wait_ge(S_("tanh2"), j + 1)
                link(v.scalar_tensor_tensor(glj, glj, 1.0, g_, ALU.add, ALU.mult))
                v.scalar_tensor_tensor(aT[:, 2 * j:2 * j + 2, :].rearrange("p a b -> p (a b)"), glj, 0.5, u_, ALU.mult, ALU.mult).then_inc(S_("aT2"), 1)
            r_ffn2.vector(dve)
            dve.wait_ge(S_("gain"), 16 * 5)
            for t in range(TT):
                dve.wait_ge(S_("last_rstd"), t + 1)
                v.scalar_tensor_tensor(xn[:, t, :], x[:, t, :], smallp[:, 26 + t:27 + t], gains[:, 0, :], ALU.mult, ALU.mult).then_inc(S_("final"), 1)

        @block.tensor
        def _(pe):
            pe.wait_ge(S_("cst_in"), 16)
            pe.wait_ge(S_("rel_in"), 32)
            for g in range(GROUPS):
                last = mm(ps[0:HEADS, g, 0:WLEN], relb[0:BUCKETS, HEADS * g:HEADS * (g + 1)], onehot[0:BUCKETS, g, :], True, True)
            last.then_inc(S_("tables"), 1)
            n_mix0.tensor(pe)
            n_mix0.done(pe)
            pe.wait_ge(S_("table"), 1)
            for kind, a, g in ORDER:
                if kind in "VK":
                    w = landed(pe, (kind, a, g)).rearrange("p (k n) -> p k n", k=KT)
                    for n in range(2):
                        unit = UNIT[(kind, a, g)] + n
                        if unit >= 3:
                            pe.wait_ge(S_("proj_out"), unit - 2)
                        if kind == "V":
                            for k in range(KT):
                                last = mm(ps[:, unit % 3, :], hT[:, k, n * P:(n + 1) * P], w[:, k, :], k == 0, k == KT - 1)
                        else:
                            for m in range(2):
                                for k in range(KT):
                                    last = mm(ps[:, unit % 3, m * S:(m + 1) * S], w[:, k, (2 * n + m) * P:(2 * n + m + 1) * P], hT[:, k, :],
                                              k == 0, k == KT - 1)
                        last.then_inc(S_("proj" if n == 0 else "chunk_used"), 1)
                elif kind == "S":
                    pe.wait_ge(S_("proj_out"), UNIT[("K", a // 2, 2)] + 2)
                    if a:
                        pe.wait_ge(S_("logits"), a)
                    q = QKb[(a // 2) % 2]
                    for gg in range(GROUPS):
                        mm(ps[:, 3 + gg, 0:256], q[:, gg, a % 2, P:2 * P], q[:, gg, 2 + a % 2, :], True, True)
                        last = mm(ps[:, 3 + gg, 256:384], q[:, gg, a % 2, 0:P], q[:, gg, 2 + a % 2, 0:P], True, True)
                    last.then_inc(S_("scores"), 1)
                elif kind == "T":
                    pe.wait_ge(S_("probs"), a + 1)
                    blocks = [(gg, c) for gg in range(GROUPS) for c in (256, 0)] + [(gg, 128) for gg in range(GROUPS)]
                    for i, (gg, c) in enumerate(blocks):
                        n = i // 4
                        if i == 0 and a:
                            pe.wait_ge(S_("pT_out"), 3 * a)
                        if i == 4 and a:
                            pe.wait_ge(S_("oT"), a)
                        if i == 8:
                            pe.wait_ge(S_("pT_out"), 3 * a + 1)
                        last = nc.tensor.transpose(ps[:, 6 + n % 2, (i % 4) * P:(i % 4 + 1) * P], L[a % 2][:, gg, c:c + P], ident)
                        if i % 4 == 3 or i == 8:
                            last.then_inc(S_("pT"), 1)
                else:
                    pe.wait_ge(S_("pT_out"), 3 * a + 3)
                    pe.wait_ge(S_("proj_out"), UNIT[("V", a // 4, 2)] + 2)
                    h4 = a % 4
                    for gg in range(GROUPS):
                        mm(ps[:, 7, 0:P], V[:, 0, gg, h4, :], PT[:, 2 * gg, :], gg == 0, gg == GROUPS - 1)
                    for gg in range(GROUPS):
                        mm(ps[:, 7, P:S], V[:, 0, gg, h4, :], PT[:, 2 * gg + 1, :], gg == 0, False)
                    for gg in range(GROUPS):
                        last = mm(ps[:, 7, P:S], V[:, 1, gg, h4, :], PT[:, 6 + gg, :], False, gg == GROUPS - 1)
                    last.then_inc(S_("head_out"), 1)

            def out_projection(chunks, src, tiles):
                for ci, chunk in enumerate(chunks):
                    w = landed(pe, chunk).rearrange("p (k n) -> p k n", k=4)
                    ks = [k for k in range(4) if 4 * ci + k < tiles]
                    for t in range(TT):
                        for n in range(2):
                            for k in ks:
                                kk = 4 * ci + k
                                last = mm(ps[:, 2 * t + n, :], src[:, kk, t * P:(t + 1) * P], w[:, k, n * 512:(n + 1) * 512],
                                          kk == 0, kk == tiles - 1)
                        if ci == len(chunks) - 1 and t == 0:
                            last.then_inc(S_("out_y"), 1)
                    last.then_inc(S_("chunk_used"), 1)

            def ada(i, first):
                w = landed(pe, ("ada", i, 0)).rearrange("p (k n) -> p k n", k=KT)
                pe.wait_ge(S_("cond"), 1)
                if i >= 2:
                    pe.wait_ge(S_("ada_row_out"), i - 1)
                for k in range(KT):
                    last = mm(ps[0:2, 5 + i % 2, :], condT[:, k, :], w[:, k, :], k == 0, k == KT - 1)
                last.then_inc(S_("chunk_used"), 1)
                if not first:
                    ada_turn(i - 1)

            def ada_turn(i):
                pe.wait_ge(S_("ada_row_out"), i + 1)
                if i:
                    pe.wait_ge(S_("ada_out"), i)
                if i // 2 in (2, 5):
                    last = mm(ps[:, 7, :], sel[:, :], row[:, i % 2, :], True, True)
                else:
                    for m in range(4):
                        last = nc.tensor.transpose(ps[:, 7, 2 * m:2 * m + 2], row[:, i % 2, m * P:(m + 1) * P], cst[0:2, C_ID, 0:2])
                last.then_inc(S_("ada_t"), 1)

            def ada_three(i):
                for n in range(3):
                    ada(i + n, n == 0)
                ada_turn(i + 2)
                pe.wait_ge(S_("ada_out"), i + 3)

            def gated_up(layer):
                for j in range(12):
                    w = landed(pe, ("up", layer, j)).rearrange("p (k n) -> p k n", k=KT)
                    if j >= 2:
                        pe.wait_ge(S_("conv"), 12 * layer + j - 1)
                    for n in range(4):
                        for k in range(KT):
                            last = mm(ps[:, 4 + 2 * (j % 2) + n // 2, (n % 2) * S:(n % 2 + 1) * S], w[:, k, n * P:(n + 1) * P], hT[:, k, :],
                                      k == 0, k == KT - 1)
                    last.then_inc(S_("chunk_used"), 1)
                pe.wait_ge(S_("aT"), 12 * layer + 12)

            pe.wait_ge(S_("oT"), HEADS)
            pe.wait_ge(S_("sel_in"), 16)
            out_projection([("wo", i, 0) for i in range(2)], oT, 8)
            ada_three(0)
            n_ffn0.tensor(pe)
            n_ffn0.done(pe)
            gated_up(0)
            out_projection([("down", 0, i) for i in range(6)], aT, FT)
            ada_three(3)
            n_mix1.tensor(pe)
            n_mix1.done(pe)

            def lru_proj(i):
                w = landed(pe, ("lin", i, 0)).rearrange("p (k n) -> p k n", k=KT)
                if i >= 2:
                    pe.wait_ge(S_("lru_xc"), i - 1)
                    pe.wait_ge(S_("lru_gb"), i - 1)
                for n in range(4):
                    for k in range(KT):
                        last = mm(ps[:, 4 + 2 * (i % 2) + n // 2, (n % 2) * S:(n % 2 + 1) * S], w[:, k, n * P:(n + 1) * P], hT[:, k, :],
                                  k == 0, k == KT - 1)
                last.then_inc(S_("chunk_used"), 1)

            def lru_gate(i, w):
                pe.wait_ge(S_("lru_xc"), i + 1)
                if i >= 2:
                    pe.wait_ge(S_("lru_tanh"), 2 * (i - 1))
                for which in range(2):
                    for n in range(2):
                        for k in range(2):
                            last = mm(ps[:, 2 * (i % 2) + which, n * S:(n + 1) * S], w[:, which, i, k, n * P:(n + 1) * P], xc[:, 2 * i + k, :],
                                      k == 0, k == 1)
                last.then_inc(S_("lgate"), 1)

            lru_proj(0)
            pe.wait_ge(S_("gate_w_in"), 16)
            for i in range(1, 4):
                lru_proj(i)
                lru_gate(i - 1, lgw)
            lru_gate(3, lgw)
            pe.wait_ge(S_("lT"), 1)
            out_projection([("lout", i, 0) for i in range(2)], lT, 8)
            ada_three(6)
            n_ffn1.tensor(pe)
            n_ffn1.done(pe)
            gated_up(1)
            out_projection([("down", 1, i) for i in range(6)], aT, FT)
            ada_three(9)
            pe.wait_ge(S_("modc"), 3)
            n_ctx.tensor(pe)
            n_ctx.done(pe)
            n_lat.tensor(pe)
            n_lat.done(pe)

            for c in range(3):
                w = landed(pe, ("win", c, 0)).rearrange("p (k n) -> p k n", k=KT)
                for m in range(H4):
                    n = 4 * c + m
                    if n >= 8:
                        pe.wait_ge(S_("qkv_conv"), n - 7)
                    t0 = S if c == 0 else 0
                    for k in range(KT):
                        last = mm(ps[:, n % 8, 0:2 * S - t0], w[:, k, m * P:(m + 1) * P], hT2[:, k, t0:2 * S], k == 0, k == KT - 1)
                    last.then_inc(S_("qkv" if m < 3 else "chunk_used"), 1)
            prev = None
            for n, (what, t) in enumerate(TOKU):
                if what != prev:
                    w = landed(pe, ("win", 3 + WHATS.index(what), 0)).rearrange("p (k n) -> p k n", k=KT)
                    prev = what
                b = 12 + n - 8
                if b < 12:
                    pe.wait_ge(S_("qkv_conv"), b + 1)
                else:
                    wait_unit(pe, b - 12)
                for k in range(KT):
                    last = mm(ps[:, (12 + n) % 8, :], hT2[:, k, t * P:(t + 1) * P], w[:, k, :], k == 0, k == KT - 1)
                last.then_inc(S_("tokproj" if t < 3 else "chunk_used"), 1)
            pe.wait_ge(S_("wab_in"), 16)
            wait_unit(pe, 6)
            for t in range(TT2):
                for k in range(KT):
                    last = mm(AB[:, t, :], hT2[:, k, t * P:(t + 1) * P], wab[:, k, :], k == 0, k == KT - 1)
            last.then_inc(S_("ab"), 1)
            for n in range(len(TOKU)):
                wait_unit(pe, n)
            pe.wait_ge(S_("qk_sq"), 1)
            for i in range(24):
                last = mm(ps[:, 1, i:i + 1], sqk[:, LENAT(i):LENAT(i) + P], cst[:, C_ONE, 0:1], True, True)
            last.then_inc(S_("lens"), 1)
            pe.wait_ge(S_("dec"), 1)
            for m in range(5):
                last = mm(ps[:, 0, 64 * m:64 * m + 64], cst[:, m, :], dec[:, :, :].rearrange("p a b -> p (a b)"), True, True)
            last.then_inc(S_("sums"), 1)
            pe.wait_ge(S_("qkv_silu"), 12)
            pe.wait_ge(S_("EX"), 1)
            pe.wait_ge(S_("lengths"), 1)
            pe.wait_ge(S_("beta"), 1)
            for n, (what, t) in enumerate(TRANS):
                if n >= 8:
                    trans_out(pe, n - 8)
                src = {"v": vT, "kn": kT, "qn": qT}.get(what)
                if what in ("rqT", "rkT"):
                    s_ = rq[:, t - TT, :, :] if what == "rqT" else rk[:, t, :, :]
                elif what in ("knT", "qnT"):
                    trans_out(pe, TRANS.index((what[0:2], t)))
                    s_ = kn[:, t, :, :] if what == "knT" else qn[:, t - TT, :, :]
                else:
                    c0 = (t - TT if what == "qn" else t) * P
                    s_ = src[:, :, c0:c0 + P]
                for h in range(H4):
                    last = nc.tensor.transpose(ps[:, n % 8, h * P:(h + 1) * P], s_[:, h, :], ident)
                last.then_inc(S_("trans"), 1)
            for n in range(len(TRANS)):
                trans_out(pe, n)

            for n, (kind, dr, t) in enumerate(GROUPLIST):
                lat = t >= TT
                first = n % 4 == 0
                last_of_dir = n % 4 == 3
                gi = DELTAS[n]
                lemask = cst[:, C_LE if dr == 0 else C_GE, :]
                kT_ = kT if kind == 0 else rkT
                qT_ = qT if kind == 0 else rqT
                kcol = slice(t * P, (t + 1) * P)
                qcol = slice((t - TT) * P, (t - TT + 1) * P)
                if kind == 0 or lat:
                    pe.wait_ge(S_("gS"), DIFFS[n] + 1)
                if n:
                    pe.wait_ge(S_("state"), UPDATES[n])
                if lat and LATER[n]:
                    pe.wait_ge(S_("ET"), LATER[n])
                if kind == 0:
                    last = mm(ps[:, 0, :], lemask, gS[:, :, :].rearrange("p a b -> p (a b)"), True, True)
                if lat:
                    for h in range(H4):
                        last = mm(ps[:, 1, h * P:(h + 1) * P], gS[:, h, :], lemask, True, True)
                if kind == 0 or lat:
                    last.then_inc(S_("diff"), 1)
                if kind == 0:
                    if gi:
                        pe.wait_ge(S_("A"), gi)
                    for h in range(H4):
                        last = mm(ps[:, 4, h * P:(h + 1) * P], kT[:, h, kcol], kT[:, h, kcol], True, True)
                    last.then_inc(S_("kk"), 1)
                if kind == 0:
                    pe.wait_ge(S_("A"), gi + 1)
                    if LATER[n]:
                        pe.wait_ge(S_("o_out"), LATER[n])
                    for l in range(LEVELS):
                        if l:
                            pe.wait_ge(S_("X_out"), gi * LEVELS + l)
                        for h in range(H4):
                            last = mm(ps[:, 5, h * P:(h + 1) * P], Am[:, h, :], XT[:, h, :], True, True)
                        last.then_inc(S_("Y"), 1)
                        pe.wait_ge(S_("Y_out"), gi * LEVELS + l + 1)
                        for h in range(H4):
                            mm(ps[:, 6, h * P:(h + 1) * P], X[:, h, :], Yt[:, h, :], True, True)
                        for h in range(H4):
                            last = mm(ps[:, 7, h * P:(h + 1) * P], Yt[:, h, :], X[:, h, :], True, True)
                        last.then_inc(S_("Z"), 1)
                    pe.wait_ge(S_("X_out"), (gi + 1) * LEVELS)
                    pe.wait_ge(S_("R"), gi + 1)
                    for h in range(H4):
                        last = mm(ps[:, 2, h * P:(h + 1) * P], Rk[:, h, :], XT[:, h, :], True, True)
                    last.then_inc(S_("wT"), 1)
                    pe.wait_ge(S_("wT_out"), gi + 1)
                    if gi:
                        pe.wait_ge(S_("vnew_out"), gi)
                    for h in range(H4):
                        last = mm(ps[:, 3, h * P:(h + 1) * P], XT[:, h, :], Rv[:, h, :], True, first)
                        if not first:
                            last = mm(ps[:, 3, h * P:(h + 1) * P], wT[:, h, :], St[:, h, :], False, True)
                    last.then_inc(S_("vnew"), 1)
                    pe.wait_ge(S_("vnew_out"), gi + 1)
                    vals = vnew
                else:
                    vals = rv[:, t, :, :]
                if lat:
                    if LATER[n]:
                        pe.wait_ge(S_("o_out"), LATER[n])
                    for h in range(H4):
                        last = mm(ps[:, 5, h * P:(h + 1) * P], kT_[:, h, kcol], qT_[:, h, qcol], True, True)
                    last.then_inc(S_("qk"), 1)
                    for h in range(H4):
                        mm(ps[:, 6, h * P:(h + 1) * P], qT_[:, h, qcol], St[:, h, :], True, True)
                    pe.wait_ge(S_("Pm"), LATER[n] + 1)
                    for h in range(H4):
                        last = mm(ps[:, 7, h * P:(h + 1) * P], Pm[:, h, :], vals[:, h, :], True, True)
                    last.then_inc(S_("o"), 1)
                if not last_of_dir:
                    pe.wait_ge(S_("kdec"), n + 1)
                    if kind == 0:
                        pe.wait_ge(S_("E"), gi + 1)
                    for h in range(H4):
                        last = mm(ps[:, 0, h * P:(h + 1) * P], kdec[:, h, :], vals[:, h, :], True, True)
                    last.then_inc(S_("dS"), 1)

            pe.wait_ge(S_("mixed"), 4)
            for k in range(KT):
                for t in range(TT):
                    last = nc.tensor.transpose(ps[:, 4 + k // 2, (k % 2) * S + t * P:(k % 2) * S + (t + 1) * P],
                                               y2[k // 4][:, t, k % 4, :], ident)
                if k % 2:
                    last.then_inc(S_("yT"), 1)
            pe.wait_ge(S_("yT_a"), 2)
            pe.wait_ge(S_("yT_v"), 2)
            out_projection([("wo2", i, 0) for i in range(2)], yT, 8)
            n_ffn2.tensor(pe)
            n_ffn2.done(pe)
            for j in range(11):
                w = landed(pe, ("up2", j, 0)).rearrange("p (k n) -> p k n", k=KT)
                if j >= 2:
                    pe.wait_ge(S_("aT2"), j - 1)
                for n in range(4):
                    for k in range(KT):
                        last = mm(ps[:, 4 + 2 * (j % 2) + n // 2, (n % 2) * S:(n % 2 + 1) * S], w[:, k, n * P:(n + 1) * P], hT[:, k, :],
                                  k == 0, k == KT - 1)
                last.then_inc(S_("chunk_used"), 1)
            pe.wait_ge(S_("aT2"), 11)
            out_projection([("down2", i, 0) for i in range(6)], aT, FT2)


def cols(a):
    return np.ascontiguousarray(a.reshape(-1, P).T)


def tiles(w):
    k, n = w.shape[0] // P, w.shape[1]
    return w.reshape(k, P, n).transpose(1, 0, 2).reshape(P, k * n)


def weight_stream(i):
    qkv, lin, win = i["attn_w_qkv"][0], i["lru_w_in"][0], i["w_in_2"][0]
    halves = lambda w, half, n: np.concatenate([w[:, n * 256:(n + 1) * 256], w[:, half + n * 256:half + (n + 1) * 256]], 1)
    W = np.zeros((NCH, P, SLOT), np.float32)
    starts = {0: 0, 1: 512, 2: 1024, 3: 1536, 4: 2064, 5: 2576, 6: 3088, 7: 3600}
    for c, (kind, a, b) in enumerate(STREAM):
        if kind == "V":
            at = ((b * 3 + 2) * HEADS + 4 * a) * P
            w = qkv[:, at:at + 512]
        elif kind == "K":
            q, k = ((b * 3 + s) * HEADS * P + 2 * a * P for s in range(2))
            w = np.concatenate([qkv[:, q:q + 256], qkv[:, k:k + 256]], 1)
        elif kind == "wo":
            w = i["attn_w_o"][0][a * 512:(a + 1) * 512]
        elif kind == "ada":
            w = i["ada_w_2"][0][:, a * 512:(a + 1) * 512]
        elif kind == "up":
            w = halves(i["ffn_w_up"][a], FF, b)
        elif kind == "down":
            w = i["ffn_w_down"][a][b * 512:(b + 1) * 512]
        elif kind == "lin":
            w = halves(lin, D, a)
        elif kind == "lout":
            w = i["lru_w_out"][0][a * 512:(a + 1) * 512]
        elif kind == "win":
            w = win[:, starts[a]:starts[a] + 512]
        elif kind == "wo2":
            w = i["w_out_2"][0][a * 512:(a + 1) * 512]
        elif kind == "up2":
            w = halves(i["w_ffn_in_2"][0], FF2, a)
        else:
            w = i["w_ffn_out_2"][0][a * 512:(a + 1) * 512]
        t = tiles(w)
        W[c, :, :t.shape[1]] = t
    return W


def constants():
    r = np.arange(P)
    l, m = r[:, None], r[None, :]
    cst = np.zeros((P, NCONST, P), np.float32)
    for n, mask in enumerate((l <= m, l >= m, l > m, l < m, l >= 0 * m, l == m)):
        cst[:, n, :] = mask
    for n in range(LEVELS):
        w = 1 << n
        same = l // (2 * w) == m // (2 * w)
        cst[:, 6 + n, :] = same & (l // w % 2 == 0) & (m // w % 2 == 1)
        cst[:, 6 + LEVELS + n, :] = same & (l // w % 2 == 1) & (m // w % 2 == 0)
    dist = S - 1 - np.arange(WLEN)
    exact = BUCKETS // 2
    dd = np.maximum(dist, 1).astype(np.float64)
    large = exact + (np.log(dd / exact) / np.log(MAX_DISTANCE / exact) * (BUCKETS - exact)).astype(np.int32)
    bucket = np.where(dist < exact, dist, np.minimum(large, BUCKETS - 1))
    onehot = np.zeros((BUCKETS, GROUPS, WLEN), np.float32)
    negm = np.full((HEADS, GROUPS, WLEN), NEG, np.float32)
    for g, dil in enumerate(DILATIONS):
        for n, d in enumerate(dist):
            if d >= 0 and d % dil == 0 and d // dil <= BAND:
                onehot[bucket[n], g, n] = 1
                negm[:, g, n] = 0
    f = np.float32
    t = np.arange(S)
    zero, ctx_len = np.zeros(S), np.full(S, float(S))
    pos = [np.concatenate(p).astype(f) for p in ((t, ctx_len), (zero, t // 64), (zero, t % 64))]
    ang = []
    for p, n in zip(pos, (16, 24, 24)):
        inv = (f(10000.0) ** (-np.arange(n, dtype=f) / f(n))).astype(f)
        ang.append(p[:, None] * inv[None, :])
    ang = np.concatenate(ang, 1).astype(f)
    c, s = np.cos(ang).astype(f), np.sin(ang).astype(f)
    rope = np.stack([np.concatenate([c, c], 1), np.concatenate([-s, s], 1)], 1)
    rope = np.ascontiguousarray(rope.reshape(TT2, P, 2, P).transpose(1, 0, 2, 3))
    sel = np.zeros((2, P), f)
    sel[0] = 1
    return {"cst": cst, "onehot": onehot, "negm": negm, "rope": rope, "sel": sel}


def kernel(**inputs):
    import concourse.bacc as bacc
    from concourse.bass_utils import run_bass_kernel_spmd

    i = {k: np.asarray(v) for k, v in inputs.items()}
    par = np.concatenate([
        cols(i["norm_mix_pre"]), cols(i["norm_ffn_pre"]), cols(i["lru_conv_w"]), cols(i["lru_conv_b"]),
        cols(i["lru_ga_b"]), cols(i["lru_gx_b"]), cols(i["lru_lambda"]), cols(i["norm_mix_g_2"]),
        cols(i["norm_ffn_g_2"]), cols(i["ffn_conv_w"]), cols(i["ffn_conv_b"]), cols(i["conv_w_2"]), cols(i["ada_b_2"]),
        np.stack([cols(i["c_2"]), cols(i["c_ctx_2"])], 2).reshape(P, 16)], 1)
    gate_w = np.stack([i[n][0].reshape(4, 2, P, 256).transpose(2, 0, 1, 3) for n in ("lru_ga_w", "lru_gx_w")], 1)
    ada_b = i["ada_b_2"][0]
    arrays = {
        "x": i["x"][0], "ctx": i["ctx_2"][0], "W": weight_stream(i), "par": par, "gate_w": gate_w,
        "rel_bias": i["rel_bias"],
        "gains": np.concatenate([i["norm_mix_post"][0:1], i["norm_ffn_post"][0:1], i["norm_mix_post"][1:2],
                                 i["norm_ffn_post"][1:2], i["final_g_2"][None]], 0),
        "ada_gate_b": np.stack([ada_b[2 * D:3 * D], ada_b[5 * D:6 * D]], 0),
        "wab": i["w_in_2"][0][:, 2048:2064].reshape(KT, P, 16).transpose(1, 0, 2),
        "normg2": np.concatenate([i["gdn_norm_g_2"], i["ret_norm_g_2"]], 0),
        "head_vec": np.concatenate([i["gdn_a_log_2"].reshape(1, 8), i["gdn_dt_bias_2"].reshape(1, 8),
                                    i["ret_decay_logit_2"].reshape(1, 8)], 1),
        **constants(),
    }
    arrays = {k: np.ascontiguousarray(a) for k, a in arrays.items()}
    nc = bacc.Bacc("TRN2", target_bir_lowering=False, num_devices=1)
    aps = {k: nc.dram_tensor(f"in_{k}", a.shape, F32, kind="ExternalInput").ap() for k, a in arrays.items()}
    out = nc.dram_tensor("out_x", (S, D), F32, kind="ExternalOutput").ap()
    build_program(nc, aps, out)
    r = run_bass_kernel_spmd(nc, [{f"in_{k}": a for k, a in arrays.items()}], core_ids=[0])
    return r.results[0]["out_x"].reshape(1, S, D)
```

```python
from contextlib import ExitStack

import numpy as np

import concourse.bass as bass
from concourse import mybir

F32 = mybir.dt.float32
ALU = mybir.AluOpType
ACT = mybir.ActivationFunctionType
AX = mybir.AxisListType

P = 128
D = 1024
KT = D // P
TT = 2
S = TT * P
EPS = 1e-6
NS = 3
SLOT = 4096
HD_SCALE = float(P) ** -0.5

GROUPS = 3
HEADS = 8
DILATIONS = (1, 4, 16)
BAND = 128
BUCKETS = 32
MAX_DISTANCE = 2048
NEG = -1e30
WLEN = 384

FF = 3 * D
FT = FF // P
FF2 = 2816
FT2 = FF2 // P

H4 = 4
NG = 16
TT2 = 4
BLK = 16
NB = P // BLK
LEVELS = 3

PC = {}
_at = 0
for _name, _n in (("mix_pre", 16), ("ffn_pre", 16), ("lru_conv_w", 32), ("lru_conv_b", 8),
                  ("ga_b", 8), ("gx_b", 8), ("lam", 8), ("mix_g2", 8), ("ffn_g2", 8),
                  ("ffn_conv_w", 288), ("ffn_conv_b", 96), ("conv_w2", 60), ("ada_b", 48),
                  ("cond", 16)):
    PC[_name] = _at
    _at += _n
NPC = _at
CONV2_K = 5

C_LE, C_GE, C_GT, C_LT, C_ONE, C_ID = range(6)
C_LEVEL = 6
NCONST = 6 + 2 * LEVELS + 1


def attention_order():
    k = lambda hp, g: ("K", hp, g)
    v = lambda q, g: ("V", q, g)
    s = lambda h: ("S", h, 0)
    t = lambda h: ("T", h, 0)
    o = lambda h: ("O", h, 0)
    return [v(0, 0), v(0, 1), v(0, 2), k(0, 0), k(0, 1), k(0, 2),
            s(0), k(1, 0), t(0), s(1), k(1, 1), o(0), t(1), k(1, 2),
            o(1), s(2), k(2, 0), t(2), s(3), k(2, 1), o(2), t(3), k(2, 2),
            o(3), s(4), v(1, 0), t(4), s(5), v(1, 1), v(1, 2),
            o(4), t(5), k(3, 0), o(5), k(3, 1), k(3, 2),
            s(6), t(6), s(7), o(6), t(7), o(7)]


def stream_order():
    ada = [("ada", i, 0) for i in range(12)]
    return ([c for c in attention_order() if c[0] in "VK"]
            + [("wo", i, 0) for i in range(2)] + ada[0:3]
            + [("up", 0, i) for i in range(12)] + [("down", 0, i) for i in range(6)] + ada[3:6]
            + [("lin", i, 0) for i in range(4)] + [("lout", i, 0) for i in range(2)] + ada[6:9]
            + [("up", 1, i) for i in range(12)] + [("down", 1, i) for i in range(6)] + ada[9:12]
            + [("win", i, 0) for i in range(8)] + [("wo2", i, 0) for i in (1, 0)]
            + [("up2", i, 0) for i in range(11)] + [("down2", i, 0) for i in range(6)])


STREAM = stream_order()
NCH = len(STREAM)
POSITION = {c: i for i, c in enumerate(STREAM)}


def build_program(nc, A, out):
    ctx = ExitStack()
    with ctx:
        def sb(name, shape):
            return ctx.enter_context(nc.sbuf_tensor(name, shape, F32))

        sems = {}

        def S_(name):
            if name not in sems:
                sems[name] = ctx.enter_context(nc.semaphore(name))
            return sems[name]

        ring = sb("ring", [P, NS, SLOT])
        x = sb("x", [P, TT, D])
        gains = sb("gains", [P, 2, D])
        gates = sb("gates", [P, 2, D])
        par = sb("par", [P, NPC])
        row = sb("row", [2, 2, 512])
        sel = sb("sel", [2, P])
        cst = sb("cst", [P, 6, P])
        modT = sb("modT", [P, 48, 2])
        small = sb("small", [P, 192])
        smallp = sb("smallp", [P, 64])
        arena = sb("arena", [P, 31744])
        ps = ctx.enter_context(nc.psum_tensor("ps", [P, 8, 512], F32))
        table = nc.dram_tensor("distance_tables", [HEADS, P, GROUPS * WLEN], F32)
        matrices = nc.dram_tensor("matrices", [2, P, TT2, H4, P], F32)
        block_inverses = nc.dram_tensor("block_inverses", [NB, TT2 * H4, 2, BLK, BLK], F32)

        ident = cst[:, C_ID, :]
        def region(start, *shape):
            n = int(np.prod(shape))
            assert start + n <= 31744, (start, shape)
            v = arena[:, start:start + n]
            if len(shape) == 1:
                return v
            names = "abcd"[:len(shape)]
            return v.rearrange(f"p ({' '.join(names)}) -> p {' '.join(names)}",
                               **{k: m for k, m in zip(names, shape)})

        def pcol(name, i=0, n=1):
            return par[:, PC[name] + i:PC[name] + i + n]

        xn = region(0, TT, D)
        hT = region(2048, KT, S)
        bias = region(4096, HEADS, GROUPS, S)
        V = region(10240, TT, GROUPS, 4, P)
        QKb = [region(13312 + 3072 * b, GROUPS, 4, S) for b in range(2)]
        L = [region(19456 + 1152 * b, GROUPS, 384) for b in range(2)]
        PT = region(21760, 9, P)
        oT = region(22912, HEADS, S)
        onehot = region(24960, GROUPS, WLEN)
        negm = region(26112, GROUPS, WLEN)
        wtab = region(27264, GROUPS, WLEN)
        relb = region(28416, 24)
        aT = region(4096, FT, S)
        u = [region(10240 + 1024 * b, 4, S) for b in range(2)]
        gl = [region(12288 + 512 * b, 2, S) for b in range(2)]
        xc = region(4096, KT, S)
        gb = region(6144, KT, S)
        tr = region(8192, KT, S)
        ti = region(10240, KT, S)
        av = region(12288, KT, S)
        th = region(14336, KT, S)
        mu = region(16384, KT, S)
        lT = region(18432, KT, S)
        lgw = region(20480, 2, 4, 2, S)

        def mm(o, l, r, start, stop):
            return nc.tensor.matmul(o, l, r, start=start, stop=stop)

        def landed(pe, chunk):
            i = POSITION[chunk]
            pe.wait_ge(S_(f"landed{i % NS}"), 16 * (i // NS + 1))
            return ring[:, i % NS, :]

        def chunk_done(eng, chunk):
            eng.wait_ge(S_("chunk_used"), POSITION[chunk] + 1)

        class Norm:

            def __init__(self, index, col, src, scaled, dst, gain, shift, ready, banks=(4, 5, 6, 7)):
                self.index, self.col, self.src, self.scaled, self.dst = index, col, src, scaled, dst
                self.gain, self.shift, self.ready, self.banks = gain, shift, ready, banks

            def scalar_square(self, act):
                for t in range(TT):
                    self.ready(act, t)
                    nc.scalar.activation(xn[:, t, :], self.src[:, t, :], ACT.Square,
                                         accum_out=small[:, self.col + t:self.col + t + 1]).then_inc(S_("norm_squared"), 1)

            def pool(self, pool):
                rstd(pool, "norm", self.index, self.col)

            def vector_scale(self, dve):
                for t in range(TT):
                    dve.wait_ge(S_("norm_rstd"), TT * self.index + t + 1)
                    nc.vector.tensor_scalar(self.scaled[:, t, :], self.src[:, t, :],
                                            smallp[:, self.col + t:self.col + t + 1], None, ALU.mult).then_inc(S_("norm_scaled"), 1)

            def tensor(self, pe):
                for t in range(TT):
                    pe.wait_ge(S_("norm_scaled"), TT * self.index + t + 1)
                    for k in range(KT):
                        o = ps[:, self.banks[k // 2], (k % 2) * S + t * P:(k % 2) * S + (t + 1) * P]
                        last = nc.tensor.transpose(o, self.scaled[:, t, k * P:(k + 1) * P], ident)
                        if t == TT - 1 and k % 2:
                            last.then_inc(S_("norm_transposed"), 1)

            def evacuate(self, eng, which):
                for k in range(KT):
                    if k // 2 % 2 != which:
                        continue
                    eng.wait_ge(S_("norm_transposed"), KT // 2 * self.index + k // 2 + 1)
                    src = ps[:, self.banks[k // 2], (k % 2) * S:(k % 2 + 1) * S]
                    done = S_(("norm_out_scalar", "norm_out_vector")[which])
                    if which == 0:
                        b = self.shift(k) if self.shift else 0.0
                        nc.scalar.activation(self.dst[:, k, :], src, ACT.Identity, scale=self.gain(k), bias=b).then_inc(done, 1)
                    elif self.shift:
                        nc.vector.tensor_scalar(self.dst[:, k, :], src, self.gain(k), self.shift(k), ALU.mult, ALU.add).then_inc(done, 1)
                    else:
                        nc.vector.tensor_scalar(self.dst[:, k, :], src, self.gain(k), None, ALU.mult).then_inc(done, 1)

            def done(self, eng):
                eng.wait_ge(S_("norm_out_scalar"), KT // 2 * (self.index + 1))
                eng.wait_ge(S_("norm_out_vector"), KT // 2 * (self.index + 1))

        def rstd(pool, name, index, col):
            for t in range(TT):
                pool.wait_ge(S_(name + "_squared"), TT * index + t + 1)
                c = slice(col + t, col + t + 1)
                nc.gpsimd.tensor_scalar(smallp[:, 32 + col + t:33 + col + t], small[:, c], 1.0 / D, EPS, ALU.mult, ALU.add).then_inc(S_("pool_step"), 1)
                pool_steps[0] += 1
                pool.wait_ge(S_("pool_step"), pool_steps[0])
                nc.gpsimd.tensor_tensor(smallp[:, c], smallp[:, 32 + col + t:33 + col + t], smallp[:, 31:32], ALU.pow).then_inc(S_(name + "_rstd"), 1)

        pool_steps = [0]

        class Residual:

            def __init__(self, index, col, gain, chunk, normed=True, gain_ready=None):
                self.index, self.col, self.gain, self.normed, self.gain_ready = index, col, gain, normed, gain_ready
                self.chunk = chunk

            def y_ready(self, eng, t):
                if t == 0:
                    eng.wait_ge(S_("out_y"), self.index + 1)
                else:
                    chunk_done(eng, self.chunk)

            def y(self, t):
                return ps[:, 2 * t:2 * t + 2, :]

            def scalar(self, act):
                if not self.normed:
                    return
                for t in range(TT):
                    self.y_ready(act, t)
                    nc.scalar.activation(xn[:, t, :].rearrange("p (a b) -> p a b", a=2), self.y(t), ACT.Square,
                                         accum_out=small[:, self.col + t:self.col + t + 1]).then_inc(S_("out_squared"), 1)

            def pool(self, pool):
                if self.normed:
                    rstd(pool, "out", self.index, self.col)

            def vector(self, dve):
                self.gain_ready(dve)
                g = self.gain.rearrange("p (a b) -> p a b", a=2)
                for t in range(TT):
                    tmp = xn[:, t, :].rearrange("p (a b) -> p a b", a=2)
                    if self.normed:
                        dve.wait_ge(S_("out_rstd"), TT * self.index + t + 1)
                        nc.vector.scalar_tensor_tensor(tmp, self.y(t), smallp[:, self.col + t:self.col + t + 1], g, ALU.mult, ALU.mult).then_inc(S_("out_gained"), 1)
                    else:
                        self.y_ready(dve, t)
                        nc.vector.tensor_tensor(tmp, self.y(t), g, ALU.mult).then_inc(S_("out_gained"), 1)
                    dve.wait_ge(S_("out_gained"), TT * self.index + t + 1)
                    nc.vector.tensor_tensor(x[:, t, :], x[:, t, :], xn[:, t, :], ALU.add).then_inc(S_("out_x"), 1)

            def x_ready(self, eng, t):
                eng.wait_ge(S_("out_x"), TT * self.index + t + 1)

        def gain_ready(i):
            return lambda dve: dve.wait_ge(S_("gain"), 16 * (i + 1))

        r_mix0 = Residual(0, 2, gains[:, 0, :], ("wo", 1, 0), gain_ready=gain_ready(0))
        r_ffn0 = Residual(1, 6, gains[:, 1, :], ("down", 0, 5), gain_ready=gain_ready(1))
        r_mix1 = Residual(2, 10, gains[:, 0, :], ("lout", 1, 0), gain_ready=gain_ready(2))
        r_ffn1 = Residual(3, 14, gains[:, 1, :], ("down", 1, 5), gain_ready=gain_ready(3))
        r_mix2 = Residual(4, 20, gates[:, 0, :], ("wo2", 0, 0), normed=False, gain_ready=lambda e: e.wait_ge(S_("ada_out"), 12))
        r_ffn2 = Residual(5, 24, gates[:, 1, :], ("down2", 5, 0), normed=False, gain_ready=lambda e: e.wait_ge(S_("ada_out"), 12))
        n_mix0 = Norm(0, 0, x, xn, hT, lambda k: pcol("mix_pre", k), None, lambda e, t: e.wait_ge(S_("x_in"), 16))
        n_ffn0 = Norm(1, 4, x, xn, hT, lambda k: pcol("ffn_pre", k), None, r_mix0.x_ready)
        n_mix1 = Norm(2, 8, x, xn, hT, lambda k: pcol("mix_pre", 8 + k), None, r_ffn0.x_ready)
        n_ffn1 = Norm(3, 12, x, xn, hT, lambda k: pcol("ffn_pre", 8 + k), None, r_mix1.x_ready)

        hT2 = region(2048, KT, 2 * S)
        ctxx = region(6144, TT, D)
        modc = small[:, 96:96 + 24]
        rope = region(8192, TT2, 2, P)
        lvl = region(9216, 2 * LEVELS + 1, P)
        qT = region(11008, H4, S)
        kT = region(12032, H4, 2 * S)
        vT = region(14080, H4, 2 * S)
        zt = region(16128, TT, 512)
        rgt = region(17152, TT, 512)
        rv = region(18176, TT2, H4, P)
        rk = region(20224, TT2, H4, P)
        rq = region(22272, TT, H4, P)
        cu = [region(23296 + 512 * b, 512) for b in range(2)]
        ct = [region(24320 + 512 * b, 512) for b in range(2)]
        wab = region(25344, KT, 16)
        normg2 = region(25472, 2, P)
        dec = region(25728, TT2, NG)
        beta = region(25792, TT2, 8)
        EX = region(25824, 5, TT2, NG)
        absc = region(26144, 8, 64)
        kn = region(0, TT2, H4, P)
        v_t = region(2048, TT2, H4, P)
        qn = region(4096, TT, H4, P)
        rqT = region(5120, H4, S)
        rkT = region(6144, H4, 2 * S)
        free = ([region(14080 + 512 * i, H4, P) for i in range(4)]
                + [region(23296 + 512 * i, H4, P) for i in range(4)]
                + [region(26656 + 512 * i, H4, P) for i in range(7)]
                + [region(o, H4, P) for o in (8704, 8192, 30720, 31232)]
                + [gains[:, 1, 512 * i:512 * (i + 1)].rearrange("p (a b) -> p a b", a=H4) for i in range(2)])
        Am = free[0:8]
        blocks = region(22272, 2, BLK, BLK)
        inverses = region(22784, 2, BLK, BLK)
        block_tmp = region(10112, 2, BLK * BLK)
        inverse_rows = region(26144, 2, TT2 * H4, BLK)
        gS = free[8:10]
        E = free[10:12]
        rET, rkdec, rPm, rSt = free[12:14], free[14:16], free[16:18], free[18:20]
        St, kdec, ET = free[12:14], free[14:16], free[16:18]
        left = [region(o + 512 * i, H4, P) for o, m in ((20224, 4), (18176, 4), (6144, 4), (5120, 2)) for i in range(m)]
        X, XT, Yt, Rk, Rv, wT, vnew = (left[2 * i:2 * i + 2] for i in range(7))
        tmp = region(29728, H4, P)
        rsq = region(8704, 32)
        sqk = region(26656, 3072)
        hw2 = region(30240, 60)
        tmpr = tmp
        AB = ps[:, 2, 0:64].rearrange("p (t c) -> p t c", t=TT2)
        condT = small[:, 64:80].rearrange("p (k c) -> p k c", k=KT)
        tmpc = sb("tmpc", [P, 40])

        TOKU = ([("z", t) for t in (2, 3)] + [("rq", t) for t in (2, 3)] + [("rk", t) for t in range(4)]
                + [("rv", t) for t in range(4)] + [("rg", t) for t in (2, 3)])
        TOKA = [sum(w in ("z", "rg", "rv") for w, _ in TOKU[:n]) for n in range(len(TOKU))]
        TOKV = [sum(w != "rv" for w, _ in TOKU[:n]) for n in range(len(TOKU))]

        WHATS = ("z", "rq", "rk", "rv", "rg")
        TOKP = [sum(t < 3 for _, t in TOKU[:n]) for n in range(len(TOKU))]

        def unit_done(eng, n):
            what, t = TOKU[n]
            if t < 3:
                eng.wait_ge(S_("tokproj"), TOKP[n] + 1)
            else:
                chunk_done(eng, ("win", 3 + WHATS.index(what), 0))

        def wait_unit(pe, n):
            if TOKU[n][0] == "rv":
                pe.wait_ge(S_("tok_act"), TOKA[n] + 1)
            else:
                pe.wait_ge(S_("tok_v"), TOKV[n] + 1)

        TRANS = ([("v", t) for t in range(4)] + [("kn", t) for t in range(4)] + [("qn", t) for t in (2, 3)]
                 + [("rkT", t) for t in range(4)] + [("rqT", t) for t in (2, 3)]
                 + [("knT", t) for t in range(4)] + [("qnT", t) for t in (2, 3)])
        ON_VECTOR = ("v", "kn", "qn")

        def trans_out(pe, n):
            mine = TRANS[n][0] in ON_VECTOR
            before = sum((w in ON_VECTOR) == mine for w, _ in TRANS[:n])
            pe.wait_ge(S_("trans_v" if mine else "trans_a"), before + 1)

        def B4(b):
            return ps[:, b, :].rearrange("p (h d) -> p h d", h=H4)

        def TB(n):
            return B4(n % 8)

        def LENAT(i):
            return (i % 4) * S + (i // 4) * P if i < 8 else 1024 + (i % 4) * 2 * S + ((i - 8) // 4) * P

        TILE_OF = ((0, 1, 2, 3), (1, 0, 3, 2))
        STEPS = len(TILE_OF[0])
        DIRS = (0, 1)

        def nth(step, d):
            return 2 * step + d + 1

        def later(step, d):
            return nth(step - 2, d)

        def level(step, l, d):
            return nth(step * LEVELS + l, d)

        y2 = [region(22272, TT, H4, P), region(4096, TT, H4, P)]
        yT = region(2048, KT, S)

        n_ctx = Norm(4, 16, ctxx, ctxx, hT2[:, :, 0:S], lambda k: modc[:, 8 + k:9 + k], lambda k: modT[:, k, 1:2],
                     lambda e, t: (e.wait_ge(S_("ctx_in"), 16), r_ffn1.x_ready(e, t)))
        n_lat = Norm(5, 18, x, xn, hT2[:, :, S:2 * S], lambda k: modc[:, k:k + 1], lambda k: modT[:, k, 0:1], r_ffn1.x_ready)
        n_ffn2 = Norm(6, 22, x, xn, hT, lambda k: modc[:, 16 + k:17 + k], lambda k: modT[:, 24 + k, 0:1], r_mix2.x_ready)

        ORDER = attention_order()
        proj = [c for c in ORDER if c[0] in "VK"]
        UNIT = {c: 2 * i for i, c in enumerate(proj)}

        block = ctx.enter_context(nc.Block())

        @block.sync
        def _(sp):
            sp.dma_start(x[:, :, :], A["x"].rearrange("(t p) d -> p t d", p=P)).then_inc(S_("x_in"), 16)
            sp.dma_start(cst[:, :, :], A["cst"][:, 0:6, :]).then_inc(S_("cst_in"), 16)
            for s in range(NS):
                sp.dma_start(ring[:, s, :], A["W"][s]).then_inc(S_(f"landed{s}"), 16)
            with sp.Fori(1, NCH // NS) as r:
                for s in range(NS):
                    sp.wait_ge(S_("chunk_used"), NS * (r - 1) + s + 1)
                    sp.dma_start(ring[:, s, :], A["W"][r * NS + s]).then_inc(S_(f"landed{s}"), 16)
            for i in range(NCH // NS * NS, NCH):
                sp.wait_ge(S_("chunk_used"), i - NS + 1)
                sp.dma_start(ring[:, i % NS, :], A["W"][i]).then_inc(S_(f"landed{i % NS}"), 16)
            for t in range(TT):
                sp.wait_ge(S_("final"), t + 1)
                sp.dma_start(out[t * P:(t + 1) * P, :], xn[:, t, :]).then_inc(S_("stored"), 16)
            sp.wait_ge(S_("stored"), 16 * TT)

        @block.gpsimd
        def _(pool):
            nc.gpsimd.memset(smallp[:, 31:32], -0.5).then_inc(S_("pool_step"), 1)
            pool_steps[0] += 1
            pool.wait_ge(S_("pool_step"), 1)

            def load_gain(i):
                if i >= 2:
                    pool.wait_ge(S_("out_gained"), TT * (i - 1))
                pool.dma_start(gains[:, i % 2, :], A["gains"][i:i + 1, :].to_broadcast([P, D])).then_inc(S_("gain"), 16)
                pool.wait_ge(S_("gain"), 16 * (i + 1))

            n_mix0.pool(pool)
            for i in range(2):
                pool.dma_start(gates[:, i, :], A["ada_gate_b"][i:i + 1, :].to_broadcast([P, D])).then_inc(S_("gate_bias_in"), 16)
            load_gain(0)
            load_gain(1)
            r_mix0.pool(pool)
            n_ffn0.pool(pool)
            load_gain(2)
            r_ffn0.pool(pool)
            n_mix1.pool(pool)
            load_gain(3)
            r_mix1.pool(pool)
            n_ffn1.pool(pool)
            load_gain(4)
            r_ffn1.pool(pool)
            n_ctx.pool(pool)
            n_lat.pool(pool)
            pool.wait_ge(S_("lengths"), 1)
            nc.gpsimd.tensor_tensor(rsq[:, 0:24], rsq[:, 0:24], smallp[:, 31:32].to_broadcast([P, 24]), ALU.pow).then_inc(S_("lengths_r"), 1)
            for i, (c, n) in enumerate(((168, 8), (164, 4), (160, 4))):
                pool.wait_ge(S_("head_var"), i + 1)
                nc.gpsimd.tensor_tensor(small[:, c:c + n], small[:, c:c + n], smallp[:, 31:32].to_broadcast([P, n]), ALU.pow).then_inc(S_("head_rstd"), 1)
            n_ffn2.pool(pool)
            rstd(pool, "last", 0, 26)

        @block.scalar
        def _(act):
            nc_a = nc.scalar
            act.dma_start(par[:, :], A["par"]).then_inc(S_("par_in"), 16)
            act.dma_start(onehot[0:BUCKETS, :, :], A["onehot"]).then_inc(S_("rel_in"), 16)
            act.dma_start(relb[0:BUCKETS, :], A["rel_bias"]).then_inc(S_("rel_in"), 16)
            act.dma_start(negm[0:HEADS, :, :], A["negm"]).then_inc(S_("neg_in"), 16)
            act.dma_start(sel[:, :], A["sel"]).then_inc(S_("sel_in"), 16)
            n_mix0.scalar_square(act)
            act.wait_ge(S_("par_in"), 16)
            nc_a.activation(small[:, 64:80], pcol("cond", 0, 16), ACT.Tanh, scale=0.5).then_inc(S_("cond_tanh"), 1)
            n_mix0.evacuate(act, 0)
            copies = GROUPS * WLEN
            act.wait_ge(S_("table"), 1)
            act.dma_start(table.ap(), wtab[0:HEADS, :, :].rearrange("h g n -> h (g n)").unsqueeze(1)
                          .to_broadcast([HEADS, P, copies])).then_inc(S_("table_out"), 16)

            for kind, a, g in ORDER:
                if kind in "VK":
                    for n in range(2):
                        unit = UNIT[(kind, a, g)] + n
                        if n == 0:
                            act.wait_ge(S_("proj"), unit // 2 + 1)
                        else:
                            chunk_done(act, (kind, a, g))
                        src = ps[:, unit % 3, :]
                        if kind == "V":
                            if a == 1:
                                act.wait_ge(S_("head_out"), 4)
                            dst = V[:, n, g, :, :].rearrange("p a b -> p (a b)")
                        else:
                            if a >= 2:
                                act.wait_ge(S_("scores"), 2 * a - 2)
                            dst = QKb[a % 2][:, g, 2 * n:2 * n + 2, :].rearrange("p a b -> p (a b)")
                        nc_a.activation(dst, src, ACT.Copy).then_inc(S_("proj_out"), 1)
                    if (kind, a, g) == ("V", 0, 2):
                        act.wait_ge(S_("table_out"), 16)
                        for h in range(HEADS):
                            skew = bass.AP(table, P - 1 + h * P * copies, [[copies - 1, P], [WLEN, GROUPS], [1, S]])
                            act.dma_start(bias[:, h, :, :], skew).then_inc(S_("bias_in"), 16)
                elif kind == "S":
                    act.wait_ge(S_("logits"), a + 1)
                    for t, c in ((1, slice(0, 256)), (0, slice(256, 384))):
                        last = nc_a.activation(L[a % 2][:, :, c], L[a % 2][:, :, c], ACT.Exp, bias=small[:, 80 + t:81 + t],
                                               accum_out=small[:, 82 + t:83 + t])
                        last.then_inc(S_("exps"), 1)
                elif kind == "T":
                    if a:
                        act.wait_ge(S_("head_out"), a)
                    for n, m in ((0, 4), (1, 4), (2, 1)):
                        act.wait_ge(S_("pT"), 3 * a + n + 1)
                        src = ps[:, 6 + n % 2, 0:m * P].rearrange("p (a b) -> p a b", a=m)
                        nc_a.activation(PT[:, 4 * n:4 * n + m, :], src, ACT.Copy).then_inc(S_("pT_out"), 1)
                else:
                    act.wait_ge(S_("head_out"), a + 1)
                    nc_a.activation(oT[:, a, :].rearrange("p (t q) -> p t q", t=2), ps[:, 7, 0:S].rearrange("p (t q) -> p t q", t=2), ACT.Copy).then_inc(S_("oT"), 1)

            def ada_rows(i):
                chunk_done(act, ("ada", i, 0))
                if i >= 2:
                    act.wait_ge(S_("ada_t"), i - 1)
                nc_a.activation(row[:, i % 2, :], ps[0:2, 5 + i % 2, :], ACT.Copy).then_inc(S_("ada_row_out"), 1)

            def gated_ffn(layer):
                for j in range(12):
                    chunk_done(act, ("up", layer, j))
                    if j >= 2:
                        act.wait_ge(S_("aT"), 12 * layer + j - 1)
                    for n in range(4):
                        ft = 2 * j + n % 2 + FT * (n // 2)
                        src = ps[:, 4 + 2 * (j % 2) + n // 2, (n % 2) * S:(n % 2 + 1) * S]
                        last = nc_a.activation(u[j % 2][:, n, :], src, ACT.Identity,
                                               scale=pcol("ffn_conv_w", (layer * 3 + 2) * 48 + ft), bias=pcol("ffn_conv_b", layer * 48 + ft))
                    last.then_inc(S_("tap"), 1)
                    act.wait_ge(S_("conv"), 12 * layer + j + 1)
                    nc_a.activation(gl[j % 2][:, :, :], u[j % 2][:, 0:2, :], ACT.Gelu_apprx_tanh).then_inc(S_("gelu"), 1)

            r_mix0.scalar(act)
            for i in range(0, 3):
                ada_rows(i)
            n_ffn0.scalar_square(act)
            n_ffn0.evacuate(act, 0)
            act.dma_start(lgw[:, :, :, :, :], A["gate_w"]).then_inc(S_("gate_w_in"), 16)
            act.wait_ge(S_("lam_abs"), 1)
            nc_a.activation(tmpc[:, 0:8], tmpc[:, 0:8], ACT.Exp).then_inc(S_("lam_exp"), 1)
            gated_ffn(0)
            r_ffn0.scalar(act)
            for i in range(3, 6):
                ada_rows(i)
            n_mix1.scalar_square(act)
            n_mix1.evacuate(act, 0)

            act.wait_ge(S_("lru_consts"), 1)

            def lru_taps(i):
                chunk_done(act, ("lin", i, 0))
                for n in range(2):
                    ft = 2 * i + n
                    nc_a.activation(xc[:, ft, :], ps[:, 4 + 2 * (i % 2), n * S:(n + 1) * S], ACT.Identity,
                                    scale=pcol("lru_conv_w", 24 + ft), bias=pcol("lru_conv_b", ft)).then_inc(S_("lru_tap"), 1)
                nc_a.activation(gb[:, 2 * i:2 * i + 2, :].rearrange("p a b -> p (a b)"), ps[:, 5 + 2 * (i % 2), :], ACT.Copy).then_inc(S_("lru_gb"), 1)

            def lru_gates(i):
                act.wait_ge(S_("lgate"), i + 1)
                for n in range(2):
                    ft = 2 * i + n
                    nc_a.activation(tr[:, ft, :], ps[:, 2 * (i % 2), n * S:(n + 1) * S], ACT.Tanh, scale=0.5, bias=small[:, 112 + ft:113 + ft])
                    nc_a.activation(ti[:, ft, :], ps[:, 2 * (i % 2) + 1, n * S:(n + 1) * S], ACT.Tanh, scale=0.5, bias=small[:, 120 + ft:121 + ft]).then_inc(S_("lru_tanh"), 1)
                for n in range(2):
                    ft = 2 * i + n
                    act.wait_ge(S_("lru_tanh"), ft + 1)
                    nc_a.activation(av[:, ft, :], tr[:, ft, :], ACT.Exp, scale=small[:, 128 + ft:129 + ft], bias=small[:, 128 + ft:129 + ft])
                    nc_a.activation(th[:, ft, :], tr[:, ft, :], ACT.Tanh, scale=small[:, 136 + ft:137 + ft], bias=small[:, 136 + ft:137 + ft]).then_inc(S_("lru_exp"), 1)

            lru_taps(0)
            for i in range(1, 4):
                lru_taps(i)
                lru_gates(i - 1)
            lru_gates(3)
            act.wait_ge(S_("lru_sq"), 1)
            nc_a.activation(mu[:, :, :], mu[:, :, :], ACT.Sqrt).then_inc(S_("lru_mult"), 1)
            nc_a.activation(gb[:, :, :], gb[:, :, :], ACT.Gelu_apprx_tanh).then_inc(S_("lru_gelu"), 1)

            r_mix1.scalar(act)
            for i in range(6, 9):
                ada_rows(i)
            n_ffn1.scalar_square(act)
            n_ffn1.evacuate(act, 0)
            gated_ffn(1)
            r_ffn1.scalar(act)
            act.dma_start(ctxx[:, :, :], A["ctx"].rearrange("(t p) d -> p t d", p=P)).then_inc(S_("ctx_in"), 16)
            act.dma_start(rope[:, :, :, :], A["rope"]).then_inc(S_("rope_in"), 16)
            act.dma_start(lvl[:, :, :], A["cst"][:, 6:, :]).then_inc(S_("lvl_in"), 16)
            act.dma_start(wab[:, :, :], A["wab"]).then_inc(S_("wab_in"), 16)
            act.dma_start(normg2[:, :, :], A["normg2"].unsqueeze(0).to_broadcast([P, 2, P])).then_inc(S_("normg2_in"), 16)
            act.dma_start(absc[:, 7, 0:24], A["head_vec"].to_broadcast([P, 24])).then_inc(S_("headv_in"), 16)
            n_ctx.scalar_square(act)
            for i in range(9, 12):
                ada_rows(i)
            n_ctx.evacuate(act, 0)
            n_lat.scalar_square(act)
            n_lat.evacuate(act, 0)

            def conv_taps(n):
                if n % 4 < 3:
                    act.wait_ge(S_("qkv"), n // 4 * 3 + n % 4 + 1)
                else:
                    chunk_done(act, ("win", n // 4, 0))
                if n >= 2:
                    act.wait_ge(S_("qkv_silu"), n - 1)
                w = S if n < H4 else 2 * S
                nc_a.activation(cu[n % 2][:, 0:w], ps[:, n % 8, 0:w], ACT.Identity, scale=hw2[:, 2 * 12 + n:2 * 12 + n + 1]).then_inc(S_("qkv_tap"), 1)

            def conv_tanh(n):
                w = S if n < H4 else 2 * S
                act.wait_ge(S_("qkv_conv"), n + 1)
                nc_a.activation(ct[n % 2][:, 0:w], cu[n % 2][:, 0:w], ACT.Tanh).then_inc(S_("qkv_tanh"), 1)

            act.wait_ge(S_("half_w"), 1)
            for n in range(12):
                conv_taps(n)
                conv_tanh(n)
            for n, (what, t) in enumerate(TOKU):
                unit_done(act, n)
                src = ps[:, (12 + n) % 8, :]
                if what in ("z", "rg"):
                    dst = (zt if what == "z" else rgt)[:, t - TT, :]
                    nc_a.activation(dst, src, ACT.Tanh, scale=0.5).then_inc(S_("tok_act"), 1)
                elif what == "rv":
                    nc_a.activation(rv[:, t, :, :].rearrange("p a b -> p (a b)"), src, ACT.Copy).then_inc(S_("tok_act"), 1)
            act.wait_ge(S_("ab"), 1)
            act.wait_ge(S_("headv_in"), 16)
            nc_a.activation(beta[:, :, :], AB[:, :, 8:16], ACT.Tanh, scale=0.5).then_inc(S_("beta_tanh"), 1)
            nc_a.activation(absc[:, 6, 0:8], absc[:, 7, 0:8], ACT.Exp).then_inc(S_("a_exp"), 1)
            act.wait_ge(S_("sp_in"), 1)
            nc_a.activation(absc[:, 1, 0:40], absc[:, 1, 0:40], ACT.Exp).then_inc(S_("sp_exp"), 1)
            act.wait_ge(S_("qkv_silu"), 12)
            nc_a.activation(sqk[:, 0:1024], qT.rearrange("p a b -> p (a b)"), ACT.Square)
            nc_a.activation(sqk[:, 1024:3072], kT.rearrange("p a b -> p (a b)"), ACT.Square).then_inc(S_("qk_sq"), 1)
            act.wait_ge(S_("sums"), 1)
            nc_a.activation(EX[:, :, :, :].rearrange("p a b c -> p (a b c)"), ps[:, 0, 0:320], ACT.Exp).then_inc(S_("EX"), 1)

            for n in range(len(TRANS)):
                what, t = TRANS[n]
                if what in ("rqT", "rkT", "knT", "qnT"):
                    act.wait_ge(S_("trans"), n + 1)
                    dst = {"rqT": rqT, "rkT": rkT, "knT": kT, "qnT": qT}[what]
                    tt = t - TT if what in ("rqT", "qnT") else t
                    sc = HD_SCALE if what in ("rqT", "qnT") else 1.0
                    nc_a.activation(dst[:, :, tt * P:(tt + 1) * P], TB(n), ACT.Copy, scale=sc).then_inc(S_("trans_a"), 1)

            def store_matrix(n):
                t, d = divmod(n, 2)
                act.wait_ge(S_("A"), n + 1)
                act.dma_start(matrices.ap()[d, :, t, :, :], Am[4 * d + t]).then_inc(S_("matrices_out"), 16)

            for n in range(2 * TT2):
                act.wait_ge(S_("diff"), n + 1)
                if n >= 2:
                    act.wait_ge(S_("A"), n - 1)
                nc_a.activation(E[n % 2], B4(n % 2), ACT.Exp).then_inc(S_("decay"), 1)
                if n >= 2:
                    store_matrix(n - 2)
            for d in DIRS:
                act.wait_ge(S_("diff"), 2 * TT2 + d + 1)
                nc_a.activation(rET[d], B4(4 + d), ACT.Exp).then_inc(S_("decay"), 1)
            store_matrix(2 * TT2 - 2)
            store_matrix(2 * TT2 - 1)
            act.wait_ge(S_("matrices_out"), 16 * 2 * TT2)
            row_words = TT2 * H4 * P
            for b in range(NB):
                for d in DIRS:
                    source = bass.AP(matrices, (d * P + b * BLK) * row_words + b * BLK, [[P, TT2 * H4], [row_words, BLK], [1, BLK]])
                    act.dma_start(blocks[b * BLK:(b + 1) * BLK, d, :, :], source).then_inc(S_("blocks_in"), 16)
            act.wait_ge(S_("inverses"), 1)
            act.dma_start(block_inverses.ap().rearrange("b n d i j -> (b n) d i j"), inverses[:, :, :, :]).then_inc(S_("inverses_out"), 16)
            act.wait_ge(S_("inverses_out"), 16)
            for b in range(NB):
                for d in DIRS:
                    act.dma_start(inverse_rows[b * BLK:(b + 1) * BLK, d, :, :],
                                  block_inverses.ap()[b, :, d, :, :].rearrange("n i j -> i n j")).then_inc(S_("inverse_rows_in"), 16)
            def head_squares(kind, t):
                for h in range(H4):
                    c = 144 + 8 * kind + 4 * t + h
                    nc_a.activation(E[t][:, h, :], y2[kind][:, t, h, :], ACT.Square, accum_out=small[:, c:c + 1]).then_inc(S_("head_sq"), 1)

            for step in range(STEPS):
                for d in DIRS:
                    act.wait_ge(S_("X_turned"), nth(step, d))
                    nc_a.activation(XT[d], B4(4 * d), ACT.Copy).then_inc(S_("XT_in"), 1)
                if step == 0:
                    act.wait_ge(S_("centred"), 1)
                    for t in range(TT):
                        head_squares(1, t)
                if step >= 2:
                    for d in DIRS:
                        act.wait_ge(S_("diff"), 2 * TT2 + 2 + later(step, d))
                        if step > 2:
                            act.wait_ge(S_("o"), later(step - 1, d))
                        nc_a.activation(ET[d], B4(4 * d + 3), ACT.Exp).then_inc(S_("decay"), 1)
                if step:
                    for d in DIRS:
                        act.wait_ge(S_("wT"), nth(step - 1, d))
                        nc_a.activation(wT[d], B4(4 * d), ACT.Copy, scale=-1.0).then_inc(S_("wT_out"), 1)
                for d in DIRS:
                    act.wait_ge(S_("vnew"), nth(step, d))
                    nc_a.activation(vnew[d], B4(4 * d + 1), ACT.Copy).then_inc(S_("vnew_out"), 1)

            for i, t in enumerate((1, 0)):
                act.wait_ge(S_("o_out"), 7 + i)
                head_squares(0, t)
            for bank, k in ((5, 4), (7, 6), (4, 0)):
                act.wait_ge(S_("yT"), {4: 1, 6: 2, 0: 3}[k])
                nc_a.activation(yT[:, k:k + 2, :].rearrange("p a b -> p (a b)"), ps[:, bank, :], ACT.Copy).then_inc(S_("yT_a"), 1)
            n_ffn2.scalar_square(act)
            n_ffn2.evacuate(act, 0)
            for j in range(11):
                chunk_done(act, ("up2", j, 0))
                if j >= 2:
                    act.wait_ge(S_("aT2"), j - 1)
                nc_a.activation(gl[j % 2].rearrange("p a b -> p (a b)"), ps[:, 4 + 2 * (j % 2), :], ACT.Tanh, scale=0.5).then_inc(S_("tanh2"), 1)
            for t in range(TT):
                r_ffn2.x_ready(act, t)
                nc_a.activation(xn[:, t, :], x[:, t, :], ACT.Square, accum_out=small[:, 26 + t:27 + t]).then_inc(S_("last_squared"), 1)

        @block.vector
        def _(dve):
            v = nc.vector
            steps = [0]

            def link(ins):
                steps[0] += 1
                ins.then_inc(S_("vector_step"), 1)
                dve.wait_ge(S_("vector_step"), steps[0])

            n_mix0.vector_scale(dve)
            dve.wait_ge(S_("cond_tanh"), 1)
            link(v.scalar_tensor_tensor(small[:, 64:80], small[:, 64:80], 1.0, pcol("cond", 0, 16), ALU.add, ALU.mult))
            v.tensor_scalar(small[:, 64:80], small[:, 64:80], 0.5, None, ALU.mult).then_inc(S_("cond"), 1)
            n_mix0.evacuate(dve, 1)
            dve.wait_ge(S_("neg_in"), 16)
            dve.wait_ge(S_("tables"), 1)
            v.tensor_tensor(wtab[0:HEADS, :, :], ps[0:HEADS, 0:3, 0:WLEN], negm[0:HEADS, :, :], ALU.add).then_inc(S_("table"), 1)
            for kind, h, _ in ORDER:
                if kind == "S":
                    Lh = L[h % 2]
                    if h == 0:
                        dve.wait_ge(S_("bias_in"), 16 * HEADS)
                    dve.wait_ge(S_("scores"), h + 1)
                    if h >= 2:
                        dve.wait_ge(S_("pT"), 3 * (h - 1))
                    v.scalar_tensor_tensor(Lh[:, :, 0:256], ps[:, 3:6, 0:256], HD_SCALE, bias[:, h, :, :], ALU.mult, ALU.add)
                    link(v.scalar_tensor_tensor(Lh[:, :, 256:384], ps[:, 3:6, 256:384], HD_SCALE, bias[:, h, :, 128:256], ALU.mult, ALU.add))
                    if h:
                        dve.wait_ge(S_("exps"), 2 * h)
                    v.tensor_reduce(small[:, 81:82], Lh[:, :, 0:256], AX.XY, ALU.max, negate=True)
                    v.tensor_reduce(small[:, 80:81], Lh[:, :, 256:384], AX.XY, ALU.max, negate=True).then_inc(S_("logits"), 1)
                    dve.wait_ge(S_("exps"), 2 * h + 2)
                    link(v.reciprocal(small[:, 84:86], small[:, 82:84]))
                    v.tensor_scalar(Lh[:, :, 0:256], Lh[:, :, 0:256], small[:, 85:86], None, ALU.mult)
                    v.tensor_scalar(Lh[:, :, 256:384], Lh[:, :, 256:384], small[:, 84:85], None, ALU.mult).then_inc(S_("probs"), 1)

            def ada_out(i):
                dve.wait_ge(S_("ada_t"), i + 1)
                if i // 2 in (2, 5):
                    dve.wait_ge(S_("gate_bias_in"), 32)
                    gg = gates[:, (i // 2) // 3, (i % 2) * 512:(i % 2 + 1) * 512]
                    v.tensor_tensor(gg, gg, ps[:, 7, :], ALU.add).then_inc(S_("ada_out"), 1)
                else:
                    v.tensor_tensor(modT[:, 4 * i:4 * i + 4, :], ps[:, 7, 0:8].rearrange("p (a b) -> p a b", a=4),
                                    pcol("ada_b", 4 * i, 4).unsqueeze(2).to_broadcast([P, 4, 2]), ALU.add).then_inc(S_("ada_out"), 1)

            def gated_ffn(layer):
                for j in range(12):
                    dve.wait_ge(S_("tap"), 12 * layer + j + 1)
                    for tap, sh in ((1, 1), (0, 2)):
                        for n in range(4):
                            ft = 2 * j + n % 2 + FT * (n // 2)
                            src = ps[:, 4 + 2 * (j % 2) + n // 2, (n % 2) * S:(n % 2 + 1) * S - sh]
                            dst = u[j % 2][:, n, sh:S]
                            last = v.scalar_tensor_tensor(dst, src, pcol("ffn_conv_w", (layer * 3 + tap) * 48 + ft), dst, ALU.mult, ALU.add)
                        if tap:
                            link(last)
                    last.then_inc(S_("conv"), 1)
                    dve.wait_ge(S_("gelu"), 12 * layer + j + 1)
                    v.tensor_tensor(aT[:, 2 * j:2 * j + 2, :], gl[j % 2][:, :, :], u[j % 2][:, 2:4, :], ALU.mult).then_inc(S_("aT"), 1)

            def log1p_exp_neg(e, w, w2, acc, n):
                link(v.tensor_scalar(w, e, 2.0, None, ALU.add))
                link(v.reciprocal(w, w))
                link(v.tensor_tensor(w, w, e, ALU.mult))
                link(v.tensor_tensor(w2, w, w, ALU.mult))
                link(v.tensor_scalar(acc, w2, 2.0 / 15, 2.0 / 13, ALU.mult, ALU.add))
                for c in (11, 9, 7, 5, 3, 1):
                    link(v.tensor_tensor(acc, acc, w2, ALU.mult))
                    link(v.tensor_scalar(acc, acc, 2.0 / c, None, ALU.add))
                link(v.tensor_tensor(acc, acc, w, ALU.mult))

            r_mix0.vector(dve)
            for i in range(0, 3):
                ada_out(i)
            n_ffn0.vector_scale(dve)
            n_ffn0.evacuate(dve, 1)
            dve.wait_ge(S_("par_in"), 16)
            v.tensor_scalar(small[:, 112:128], pcol("ga_b", 0, 16), 0.5, None, ALU.mult)
            lam = pcol("lam", 0, 8)
            link(v.tensor_scalar(tmpc[:, 0:8], lam, -1.0, None, ALU.mult))
            v.tensor_tensor(tmpc[:, 0:8], tmpc[:, 0:8], lam, ALU.min).then_inc(S_("lam_abs"), 1)
            dve.wait_ge(S_("lam_exp"), 1)
            log1p_exp_neg(tmpc[:, 0:8], tmpc[:, 8:16], tmpc[:, 16:24], tmpc[:, 24:32], 8)
            link(v.tensor_scalar(tmpc[:, 0:8], lam, 0.0, None, ALU.min))
            link(v.tensor_tensor(tmpc[:, 0:8], tmpc[:, 0:8], tmpc[:, 24:32], ALU.subtract))
            v.tensor_scalar(small[:, 128:136], tmpc[:, 0:8], 4.0, None, ALU.mult)
            v.tensor_scalar(small[:, 136:144], tmpc[:, 0:8], -4.0, None, ALU.mult).then_inc(S_("lru_consts"), 1)
            gated_ffn(0)
            r_ffn0.vector(dve)
            for i in range(3, 6):
                ada_out(i)
            n_mix1.vector_scale(dve)
            n_mix1.evacuate(dve, 1)

            def lru_conv(i):
                dve.wait_ge(S_("lru_tap"), 2 * i + 2)
                for sh in (1, 2, 3):
                    for n in range(2):
                        ft = 2 * i + n
                        dst = xc[:, ft, sh:S]
                        src = ps[:, 4 + 2 * (i % 2), n * S:(n + 1) * S - sh]
                        last = v.scalar_tensor_tensor(dst, src, pcol("lru_conv_w", (3 - sh) * 8 + ft), dst, ALU.mult, ALU.add)
                    if sh < 3:
                        link(last)
                last.then_inc(S_("lru_xc"), 1)

            def lru_in(i):
                b2 = slice(2 * i, 2 * i + 2)
                dve.wait_ge(S_("lru_exp"), 2 * i + 2)
                link(v.tensor_tensor(mu[:, b2, :], av[:, b2, :], av[:, b2, :], ALU.mult))
                last = v.scalar_tensor_tensor(mu[:, b2, :], mu[:, b2, :], 1.0, th[:, b2, :], ALU.add, ALU.mult)
                if i == 3:
                    last.then_inc(S_("lru_sq"), 1)
                link(v.scalar_tensor_tensor(ti[:, b2, :], ti[:, b2, :], 1.0, xc[:, b2, :], ALU.add, ALU.mult))

            lru_conv(0)
            for i in range(1, 4):
                lru_conv(i)
                lru_in(i - 1)
            lru_in(3)
            dve.wait_ge(S_("lru_mult"), 1)
            link(v.scalar_tensor_tensor(ti[:, :, :], ti[:, :, :], 0.5, mu[:, :, :], ALU.mult, ALU.mult))
            for ft in range(KT):
                last = v.tensor_tensor_scan(th[:, ft, :], av[:, ft, :], ti[:, ft, :], 0.0, ALU.mult, ALU.add)
            link(last)
            dve.wait_ge(S_("lru_gelu"), 1)
            v.tensor_tensor(lT[:, :, :], th[:, :, :], gb[:, :, :], ALU.mult).then_inc(S_("lT"), 1)

            r_mix1.vector(dve)
            for i in range(6, 9):
                ada_out(i)
            n_ffn1.vector_scale(dve)
            n_ffn1.evacuate(dve, 1)
            gated_ffn(1)
            r_ffn1.vector(dve)
            n_ctx.vector_scale(dve)
            for i in range(9, 12):
                ada_out(i)
            for at, name, blk, which in ((0, "mix_g2", 8, 0), (8, "mix_g2", 8, 1), (16, "ffn_g2", 32, 0)):
                v.scalar_tensor_tensor(modc[:, at:at + 8], modT[:, blk:blk + 8, which:which + 1].rearrange("p a b -> p (a b)"),
                                       1.0, pcol(name, 0, 8), ALU.add, ALU.mult).then_inc(S_("modc"), 1)
            v.tensor_scalar(hw2[:, :], pcol("conv_w2", 0, 60), 0.5, None, ALU.mult).then_inc(S_("half_w"), 1)
            dve.wait_ge(S_("modc"), 3)
            dve.wait_ge(S_("half_w"), 1)
            n_ctx.evacuate(dve, 1)
            n_lat.vector_scale(dve)
            n_lat.evacuate(dve, 1)

            for n in range(12):
                dve.wait_ge(S_("qkv_tap"), n + 1)
                segs = 1 if n < H4 else 2
                src3 = ps[:, n % 8, 0:segs * S].rearrange("p (a b) -> p a b", a=segs)
                dst3 = cu[n % 2][:, 0:segs * S].rearrange("p (a b) -> p a b", a=segs)
                for tap in (0, 1, 3, 4):
                    d = tap - 2
                    if d < 0:
                        o_, i_ = dst3[:, :, -d:S], src3[:, :, 0:S + d]
                    else:
                        o_, i_ = dst3[:, :, 0:S - d], src3[:, :, d:S]
                    last = v.scalar_tensor_tensor(o_, i_, hw2[:, tap * 12 + n:tap * 12 + n + 1], o_, ALU.mult, ALU.add)
                    if tap < 4:
                        link(last)
                last.then_inc(S_("qkv_conv"), 1)
                dve.wait_ge(S_("qkv_tanh"), n + 1)
                w = segs * S
                dst = (qT[:, n, :] if n < 4 else kT[:, n - 4, :] if n < 8 else vT[:, n - 8, :])
                v.scalar_tensor_tensor(dst, ct[n % 2][:, 0:w], 1.0, cu[n % 2][:, 0:w], ALU.add, ALU.mult).then_inc(S_("qkv_silu"), 1)

            dve.wait_ge(S_("rope_in"), 16)
            for n, (what, t) in enumerate(TOKU):
                src = ps[:, (12 + n) % 8, :]
                s3 = src.rearrange("p (h d) -> p h d", h=H4)
                if what in ("z", "rg"):
                    dst = (zt if what == "z" else rgt)[:, t - TT, :]
                    dve.wait_ge(S_("tok_act"), TOKA[n] + 1)
                    v.scalar_tensor_tensor(dst, dst, 1.0, src, ALU.add, ALU.mult).then_inc(S_("tok_v"), 1)
                elif what in ("rq", "rk"):
                    unit_done(dve, n)
                    dst = rq[:, t - TT, :, :] if what == "rq" else rk[:, t, :, :]
                    cosb = rope[:, t, 0:1, :].to_broadcast([P, H4, P])
                    v.tensor_tensor(dst, s3, cosb, ALU.mult)
                    v.tensor_tensor(tmpr[:, :, 0:64], s3[:, :, 64:128], rope[:, t, 1:2, 0:64].to_broadcast([P, H4, 64]), ALU.mult)
                    link(v.tensor_tensor(tmpr[:, :, 64:128], s3[:, :, 0:64], rope[:, t, 1:2, 64:128].to_broadcast([P, H4, 64]), ALU.mult))
                    v.tensor_tensor(dst, dst, tmpr[:, :, :], ALU.add).then_inc(S_("tok_v"), 1)
                    dve.wait_ge(S_("tok_v"), TOKV[n] + 1)
            dve.wait_ge(S_("beta_tanh"), 1)
            dve.wait_ge(S_("headv_in"), 16)
            z0, z1, z2, z3, z4 = (absc[:, i, 0:40] for i in range(5))
            v.tensor_tensor(absc[:, 0, 0:32].rearrange("p (a b) -> p a b", a=TT2), AB[:, :, 0:8],
                            absc[:, 7:8, 8:16].to_broadcast([P, TT2, 8]), ALU.add)
            link(v.tensor_scalar(absc[:, 0, 32:40], absc[:, 7, 16:24], -1.0, None, ALU.mult))
            link(v.tensor_scalar(z1, z0, -1.0, None, ALU.mult))
            v.tensor_tensor(z1, z1, z0, ALU.min).then_inc(S_("sp_in"), 1)
            dve.wait_ge(S_("sp_exp"), 1)
            log1p_exp_neg(z1, z2, z3, z4, 40)
            link(v.tensor_scalar(z0, z0, 0.0, None, ALU.max))
            link(v.tensor_tensor(z0, z0, z4, ALU.add))
            link(v.tensor_scalar(z0, z0, -1.0, None, ALU.mult))
            dve.wait_ge(S_("a_exp"), 1)
            v.tensor_tensor(dec[:, :, 0:8], absc[:, 0, 0:32].rearrange("p (a b) -> p a b", a=TT2),
                            absc[:, 6:7, 0:8].to_broadcast([P, TT2, 8]), ALU.mult)
            v.tensor_copy(dec[:, :, 8:16], absc[:, 0:1, 32:40].to_broadcast([P, TT2, 8])).then_inc(S_("dec"), 1)
            dve.wait_ge(S_("beta_tanh"), 1)
            v.tensor_scalar(beta[:, :, :], beta[:, :, :], 0.5, 0.5, ALU.mult, ALU.add).then_inc(S_("beta"), 1)
            dve.wait_ge(S_("lens"), 1)
            v.tensor_scalar(rsq[:, 0:24], ps[:, 1, 0:24], EPS, None, ALU.add).then_inc(S_("lengths"), 1)
            dve.wait_ge(S_("lengths_r"), 1)
            for n in range(len(TRANS)):
                what, t = TRANS[n]
                if what in ("v", "kn", "qn"):
                    dve.wait_ge(S_("trans"), n + 1)
                    if what == "v":
                        v.tensor_copy(v_t[:, t, :, :], TB(n)).then_inc(S_("trans_v"), 1)
                    else:
                        c = 8 + t * 4 if what == "kn" else (t - TT) * 4
                        dst = kn[:, t, :, :] if what == "kn" else qn[:, t - TT, :, :]
                        v.tensor_tensor(dst, TB(n), rsq[:, c:c + 4].unsqueeze(2).to_broadcast([P, H4, P]), ALU.mult).then_inc(S_("trans_v"), 1)

            dve.wait_ge(S_("trans_v"), 10)
            dve.wait_ge(S_("EX"), 1)
            dve.wait_ge(S_("beta"), 1)
            dve.wait_ge(S_("lvl_in"), 16)

            def bc(a):
                return a.unsqueeze(2).to_broadcast([P, H4, P])

            def bh(a):
                return a.unsqueeze(1).to_broadcast([P, H4, P])

            def decay_in(d, t, kind, dst):
                c = 8 * kind + 4 * d
                v.tensor_tensor(dst, bh(cst[:, C_LT if d else C_GT, :]), bc(dec[:, t, c:c + 4]), ALU.mult).then_inc(S_("gS"), 1)

            def output_part(kind, step, d, inter, inner):
                t = TILE_OF[d][step]
                c = 8 * kind + 4 * d
                o_ = y2[kind][:, t - TT, :, :]
                done = 4 * (kind == 0) + later(step, d)
                if step == 2:
                    link(v.tensor_copy(o_, B4(inner)))
                else:
                    dve.wait_ge(S_("o_out"), done - 1)
                    link(v.tensor_tensor(o_, o_, B4(inner), ALU.add))
                for h in range(H4):
                    last = v.scalar_tensor_tensor(o_[:, h, :], ps[:, inter, h * P:(h + 1) * P],
                                                  EX[:, C_GE if d else C_LE, t, c + h:c + h + 1], o_[:, h, :], ALU.mult, ALU.add)
                last.then_inc(S_("o_out"), 1)

            def update_state(state, kind, step, d, b, sem):
                t = TILE_OF[d][step]
                c = 8 * kind + 4 * d
                if step == 0:
                    v.tensor_copy(state, B4(b)).then_inc(sem, 1)
                else:
                    for h in range(H4):
                        last = v.scalar_tensor_tensor(state[:, h, :], state[:, h, :], EX[:, C_ONE, t, c + h:c + h + 1],
                                                      ps[:, b, h * P:(h + 1) * P], ALU.mult, ALU.add)
                    last.then_inc(sem, 1)

            for n in range(2):
                decay_in(n, 0, 0, gS[n])
            for n in range(2 * TT2):
                t, d = divmod(n, 2)
                dve.wait_ge(S_("decay"), n + 1)
                dve.wait_ge(S_("kk"), t + 1)
                for h in range(H4):
                    last = v.scalar_tensor_tensor(Am[4 * d + t][:, h, :], ps[:, 2 + t % 2, h * P:(h + 1) * P],
                                                  beta[:, t, 4 * d + h:4 * d + h + 1], E[d][:, h, :], ALU.mult, ALU.mult)
                last.then_inc(S_("A"), 1)
                dve.wait_ge(S_("diff"), n + 1)
                if t + 1 < TT2:
                    decay_in(d, t + 1, 0, gS[d])
                else:
                    decay_in(d, 0, 1, gS[d])
            for d in DIRS:
                dve.wait_ge(S_("decay"), 2 * TT2 + d + 1)
                link(v.tensor_tensor(rET[d], rET[d], bh(cst[:, C_GE if d else C_LE, :]), ALU.mult))
            def invert_blocks():
                dve.wait_ge(S_("blocks_in"), 16 * 2 * NB)
                for i in range(1, BLK):
                    for d in DIRS:
                        done = slice(BLK - i, BLK) if d else slice(0, i)
                        r = BLK - 1 - i if d else i
                        prod = block_tmp[:, d, 0:i * i].rearrange("p (c j) -> p c j", c=i)
                        last = v.tensor_tensor(prod, inverses[:, d, done, done].rearrange("p j c -> p c j"),
                                               blocks[:, d, r, done].unsqueeze(1).to_broadcast([P, i, i]), ALU.mult)
                    link(last)
                    for d in DIRS:
                        done = slice(BLK - i, BLK) if d else slice(0, i)
                        r = BLK - 1 - i if d else i
                        last = v.tensor_reduce(inverses[:, d, r, done], block_tmp[:, d, 0:i * i].rearrange("p (c j) -> p c j", c=i),
                                               AX.X, ALU.add, negate=True)
                    if i < BLK - 1:
                        link(last)
                last.then_inc(S_("inverses"), 1)

            def expand(step, d):
                t = TILE_OF[d][step]
                rows = inverse_rows[:, d, H4 * t:H4 * (t + 1), :].unsqueeze(2).to_broadcast([P, H4, NB, BLK])
                mask = lvl[:, 2 * LEVELS, :].rearrange("p (b j) -> p b j", b=NB).unsqueeze(1).to_broadcast([P, H4, NB, BLK])
                v.tensor_tensor(X[d].rearrange("p h (b j) -> p h b j", b=NB), rows, mask, ALU.mult).then_inc(S_("X_in"), 1)

            link(v.memset(inverses[:, :, :, :], 0.0))
            for d in DIRS:
                diagonal = inverses[:, d, :, :].rearrange("p i j -> p (i j)")[:, 0:BLK * BLK:BLK + 1]
                last = v.memset(diagonal, 1.0)
            link(last)
            for step in range(STEPS):
                if step == 2:
                    invert_blocks()
                if step < 3:
                    for d in DIRS:
                        t = TILE_OF[d][step]
                        if step:
                            dve.wait_ge(S_("rdS"), nth(step - 1, d))
                        v.tensor_tensor(rkdec[d], rk[:, t, :, :], bc(EX[:, C_LT if d else C_GT, t, 8 + 4 * d:12 + 4 * d]), ALU.mult).then_inc(S_("rkdec"), 1)
                if step >= 2:
                    for d in DIRS:
                        if step > 2:
                            dve.wait_ge(S_("ro"), later(step - 1, d))
                        dve.wait_ge(S_("rqk"), later(step, d))
                        v.tensor_tensor(rPm[d], B4(4 * d), rET[d], ALU.mult).then_inc(S_("rPm"), 1)
                if step < 3:
                    for d in DIRS:
                        dve.wait_ge(S_("rdS"), nth(step, d))
                        update_state(rSt[d], 1, step, d, 4 * d + 3, S_("rstate"))
                if step >= 2:
                    for d in DIRS:
                        dve.wait_ge(S_("ro"), later(step, d))
                        output_part(1, step, d, 4 * d + 1, 4 * d + 2)
            def retention_centre():
                for t in range(TT):
                    dve.wait_ge(S_("o_out"), 4)
                    last = v.tensor_reduce(tmpc[:, 8 + 4 * t:12 + 4 * t], y2[1][:, t, :, :], AX.X, ALU.add)
                link(last)
                link(v.tensor_scalar(tmpc[:, 0:8], tmpc[:, 8:16], 1.0 / P, None, ALU.mult))
                for t in range(TT):
                    last = v.tensor_tensor(y2[1][:, t, :, :], y2[1][:, t, :, :], bc(tmpc[:, 4 * t:4 * t + 4]), ALU.subtract)
                last.then_inc(S_("centred"), 1)

            def retention_variance():
                dve.wait_ge(S_("head_sq"), 8)
                v.tensor_scalar(small[:, 168:176], small[:, 152:160], 1.0 / P, EPS, ALU.mult, ALU.add).then_inc(S_("head_var"), 1)

            def retention_norm(t):
                dve.wait_ge(S_("head_rstd"), 1)
                dve.wait_ge(S_("normg2_in"), 16)
                y = y2[1][:, t, :, :]
                link(v.tensor_tensor(y, y, bc(small[:, 168 + 4 * t:172 + 4 * t]), ALU.mult))
                link(v.tensor_tensor(y, y, normg2[:, 1:2, :].to_broadcast([P, H4, P]), ALU.mult))
                v.scalar_tensor_tensor(y, y, 0.5, rgt[:, t, :].rearrange("p (a b) -> p a b", a=H4), ALU.mult, ALU.mult).then_inc(S_("mixed"), 1)

            def delta_gates(t):
                dve.wait_ge(S_("normg2_in"), 16)
                z = zt[:, t, :].rearrange("p (a b) -> p a b", a=H4)
                link(v.scalar_tensor_tensor(z, z, 0.5, normg2[:, 0:1, :].to_broadcast([P, H4, P]), ALU.mult, ALU.mult))

            beside = {(0, 0): retention_centre, (0, 2): retention_variance,
                      (1, 1): lambda: retention_norm(0), (1, 2): lambda: retention_norm(1),
                      (2, 0): lambda: delta_gates(0), (2, 2): lambda: delta_gates(1)}
            for step in range(STEPS):
                if step == 0:
                    dve.wait_ge(S_("inverse_rows_in"), 16 * 2 * NB)
                    for d in DIRS:
                        expand(step, d)
                if step >= 2:
                    for d in DIRS:
                        dve.wait_ge(S_("diff"), 2 * TT2 + (2 if step == 2 else 2 + later(step - 1, d)))
                        decay_in(d, TILE_OF[d][step], 0, gS[d])
                if step:
                    dve.wait_ge(S_("vnew"), 2 * step)
                    dve.wait_ge(S_("dS"), 2 * step)
                for l in range(LEVELS):
                    for d in DIRS:
                        dve.wait_ge(S_("Y"), level(step, l, d))
                        v.tensor_tensor(Yt[d], B4(4 * d), bh(lvl[:, d * LEVELS + l, :]), ALU.mult).then_inc(S_("Y_out"), 1)
                    if l == 0:
                        for d in DIRS:
                            t = TILE_OF[d][step]
                            bt = beta[:, t, 4 * d:4 * d + 4]
                            v.tensor_tensor(small[:, 176 + 4 * d:180 + 4 * d], bt, EX[:, C_GE if d else C_LE, t, 4 * d:4 * d + 4], ALU.mult).then_inc(S_("beg"), 1)
                            v.tensor_tensor(Rv[d], v_t[:, t, :, :], bc(bt), ALU.mult)
                            dve.wait_ge(S_("beg"), nth(step, d))
                            v.tensor_tensor(Rk[d], kn[:, t, :, :], bc(small[:, 176 + 4 * d:180 + 4 * d]), ALU.mult).then_inc(S_("R"), 1)
                    if (step, l) in beside:
                        beside[step, l]()
                    if l == 1 and step < 3:
                        for d in DIRS:
                            t = TILE_OF[d][step]
                            v.tensor_tensor(kdec[d], kn[:, t, :, :], bc(EX[:, C_LT if d else C_GT, t, 4 * d:4 * d + 4]), ALU.mult).then_inc(S_("kdec"), 1)
                    if l == 1 and step >= 2:
                        for d in DIRS:
                            dve.wait_ge(S_("decay"), 2 * TT2 + 2 + later(step, d))
                            v.tensor_tensor(ET[d], ET[d], bh(cst[:, C_GE if d else C_LE, :]), ALU.mult).then_inc(S_("ET"), 1)
                    for d in DIRS:
                        dve.wait_ge(S_("Z"), level(step, l, d))
                        last = v.tensor_tensor(XT[d], XT[d], B4(4 * d + 1), ALU.subtract)
                        if l < LEVELS - 1:
                            last = v.tensor_tensor(X[d], X[d], B4(4 * d + 2), ALU.subtract)
                        last.then_inc(S_("X_out"), 1)
                if step < 3:
                    for d in DIRS:
                        expand(step + 1, d)
                if step >= 2:
                    for d in DIRS:
                        dve.wait_ge(S_("ET"), later(step, d))
                        dve.wait_ge(S_("qk"), later(step, d))
                        v.tensor_tensor(ET[d], B4(4 * d + 2), ET[d], ALU.mult).then_inc(S_("Pm"), 1)
                if step < 3:
                    for d in DIRS:
                        dve.wait_ge(S_("dS"), nth(step, d))
                        update_state(St[d], 0, step, d, 4 * d + 3, S_("state"))
                if step >= 2:
                    for d in DIRS:
                        dve.wait_ge(S_("o"), later(step, d))
                        output_part(0, step, d, 4 * d, 4 * d + 2)
            for i, t in enumerate((1, 0)):
                dve.wait_ge(S_("head_sq"), 8 + 4 * (i + 1))
                c = 144 + 4 * t
                v.tensor_scalar(small[:, c + 16:c + 20], small[:, c:c + 4], 1.0 / P, EPS, ALU.mult, ALU.add).then_inc(S_("head_var"), 1)
            for i, t in enumerate((1, 0)):
                dve.wait_ge(S_("head_rstd"), i + 2)
                for h in range(H4):
                    last = v.scalar_tensor_tensor(y2[0][:, t, h, :], y2[0][:, t, h, :], small[:, 160 + 4 * t + h:161 + 4 * t + h],
                                                  zt[:, t, h * P:(h + 1) * P], ALU.mult, ALU.mult)
                last.then_inc(S_("mixed"), 1)
            dve.wait_ge(S_("yT"), 4)
            v.tensor_copy(yT[:, 2:4, :].rearrange("p a b -> p (a b)"), ps[:, 6, :]).then_inc(S_("yT_v"), 1)
            r_mix2.vector(dve)
            n_ffn2.vector_scale(dve)
            n_ffn2.evacuate(dve, 1)
            for j in range(11):
                g_, u_ = ps[:, 4 + 2 * (j % 2), :], ps[:, 5 + 2 * (j % 2), :]
                glj = gl[j % 2].rearrange("p a b -> p (a b)")
                dve.wait_ge(S_("tanh2"), j + 1)
                link(v.scalar_tensor_tensor(glj, glj, 1.0, g_, ALU.add, ALU.mult))
                v.scalar_tensor_tensor(aT[:, 2 * j:2 * j + 2, :].rearrange("p a b -> p (a b)"), glj, 0.5, u_, ALU.mult, ALU.mult).then_inc(S_("aT2"), 1)
            r_ffn2.vector(dve)
            dve.wait_ge(S_("gain"), 16 * 5)
            for t in range(TT):
                dve.wait_ge(S_("last_rstd"), t + 1)
                v.scalar_tensor_tensor(xn[:, t, :], x[:, t, :], smallp[:, 26 + t:27 + t], gains[:, 0, :], ALU.mult, ALU.mult).then_inc(S_("final"), 1)

        @block.tensor
        def _(pe):
            pe.wait_ge(S_("cst_in"), 16)
            n_mix0.tensor(pe)
            pe.wait_ge(S_("rel_in"), 32)
            for g in range(GROUPS):
                last = mm(ps[0:HEADS, g, 0:WLEN], relb[0:BUCKETS, HEADS * g:HEADS * (g + 1)], onehot[0:BUCKETS, g, :], True, True)
            last.then_inc(S_("tables"), 1)
            n_mix0.done(pe)
            pe.wait_ge(S_("table"), 1)
            for kind, a, g in ORDER:
                if kind in "VK":
                    w = landed(pe, (kind, a, g)).rearrange("p (k n) -> p k n", k=KT)
                    for n in range(2):
                        unit = UNIT[(kind, a, g)] + n
                        if unit >= 3:
                            pe.wait_ge(S_("proj_out"), unit - 2)
                        if kind == "V":
                            for k in range(KT):
                                last = mm(ps[:, unit % 3, :], hT[:, k, n * P:(n + 1) * P], w[:, k, :], k == 0, k == KT - 1)
                        else:
                            for m in range(2):
                                for k in range(KT):
                                    last = mm(ps[:, unit % 3, m * S:(m + 1) * S], w[:, k, (2 * n + m) * P:(2 * n + m + 1) * P], hT[:, k, :],
                                              k == 0, k == KT - 1)
                        last.then_inc(S_("proj" if n == 0 else "chunk_used"), 1)
                elif kind == "S":
                    pe.wait_ge(S_("proj_out"), UNIT[("K", a // 2, 2)] + 2)
                    if a:
                        pe.wait_ge(S_("logits"), a)
                    q = QKb[(a // 2) % 2]
                    for gg in range(GROUPS):
                        mm(ps[:, 3 + gg, 0:256], q[:, gg, a % 2, P:2 * P], q[:, gg, 2 + a % 2, :], True, True)
                        last = mm(ps[:, 3 + gg, 256:384], q[:, gg, a % 2, 0:P], q[:, gg, 2 + a % 2, 0:P], True, True)
                    last.then_inc(S_("scores"), 1)
                elif kind == "T":
                    pe.wait_ge(S_("probs"), a + 1)
                    blocks = [(gg, c) for gg in range(GROUPS) for c in (256, 0)] + [(gg, 128) for gg in range(GROUPS)]
                    for i, (gg, c) in enumerate(blocks):
                        n = i // 4
                        if i == 0 and a:
                            pe.wait_ge(S_("pT_out"), 3 * a)
                        if i == 4 and a:
                            pe.wait_ge(S_("oT"), a)
                        if i == 8:
                            pe.wait_ge(S_("pT_out"), 3 * a + 1)
                        last = nc.tensor.transpose(ps[:, 6 + n % 2, (i % 4) * P:(i % 4 + 1) * P], L[a % 2][:, gg, c:c + P], ident)
                        if i % 4 == 3 or i == 8:
                            last.then_inc(S_("pT"), 1)
                else:
                    pe.wait_ge(S_("pT_out"), 3 * a + 3)
                    pe.wait_ge(S_("proj_out"), UNIT[("V", a // 4, 2)] + 2)
                    h4 = a % 4
                    for gg in range(GROUPS):
                        mm(ps[:, 7, 0:P], V[:, 0, gg, h4, :], PT[:, 2 * gg, :], gg == 0, gg == GROUPS - 1)
                    for gg in range(GROUPS):
                        mm(ps[:, 7, P:S], V[:, 0, gg, h4, :], PT[:, 2 * gg + 1, :], gg == 0, False)
                    for gg in range(GROUPS):
                        last = mm(ps[:, 7, P:S], V[:, 1, gg, h4, :], PT[:, 6 + gg, :], False, gg == GROUPS - 1)
                    last.then_inc(S_("head_out"), 1)

            def out_projection(chunks, src, tiles, order=None, between=None):
                order = order or range(len(chunks))
                for ci in order:
                    chunk = chunks[ci]
                    w = landed(pe, chunk).rearrange("p (k n) -> p k n", k=4)
                    ks = [k for k in range(4) if 4 * ci + k < tiles]
                    for t in range(TT):
                        for n in range(2):
                            for k in ks:
                                kk = 4 * ci + k
                                last = mm(ps[:, 2 * t + n, :], src[:, kk, t * P:(t + 1) * P], w[:, k, n * 512:(n + 1) * 512],
                                          ci == order[0] and k == ks[0], ci == order[-1] and k == ks[-1])
                        if ci == order[-1] and t == 0:
                            last.then_inc(S_("out_y"), 1)
                    last.then_inc(S_("chunk_used"), 1)
                    if between and ci == order[0]:
                        between()

            def ada(i, first):
                w = landed(pe, ("ada", i, 0)).rearrange("p (k n) -> p k n", k=KT)
                pe.wait_ge(S_("cond"), 1)
                if i >= 2:
                    pe.wait_ge(S_("ada_row_out"), i - 1)
                for k in range(KT):
                    last = mm(ps[0:2, 5 + i % 2, :], condT[:, k, :], w[:, k, :], k == 0, k == KT - 1)
                last.then_inc(S_("chunk_used"), 1)
                if not first:
                    ada_turn(i - 1)

            def ada_turn(i):
                pe.wait_ge(S_("ada_row_out"), i + 1)
                if i:
                    pe.wait_ge(S_("ada_out"), i)
                if i // 2 in (2, 5):
                    last = mm(ps[:, 7, :], sel[:, :], row[:, i % 2, :], True, True)
                else:
                    for m in range(4):
                        last = nc.tensor.transpose(ps[:, 7, 2 * m:2 * m + 2], row[:, i % 2, m * P:(m + 1) * P], cst[0:2, C_ID, 0:2])
                last.then_inc(S_("ada_t"), 1)

            def ada_three(i):
                for n in range(3):
                    ada(i + n, n == 0)
                ada_turn(i + 2)
                pe.wait_ge(S_("ada_out"), i + 3)

            def gated_up(layer):
                for j in range(12):
                    w = landed(pe, ("up", layer, j)).rearrange("p (k n) -> p k n", k=KT)
                    if j >= 2:
                        pe.wait_ge(S_("conv"), 12 * layer + j - 1)
                    for n in range(4):
                        for k in range(KT):
                            last = mm(ps[:, 4 + 2 * (j % 2) + n // 2, (n % 2) * S:(n % 2 + 1) * S], w[:, k, n * P:(n + 1) * P], hT[:, k, :],
                                      k == 0, k == KT - 1)
                    last.then_inc(S_("chunk_used"), 1)
                pe.wait_ge(S_("aT"), 12 * layer + 12)

            pe.wait_ge(S_("oT"), HEADS)
            pe.wait_ge(S_("sel_in"), 16)
            out_projection([("wo", i, 0) for i in range(2)], oT, 8)
            ada_three(0)
            n_ffn0.tensor(pe)
            n_ffn0.done(pe)
            gated_up(0)
            out_projection([("down", 0, i) for i in range(6)], aT, FT)
            ada_three(3)
            n_mix1.tensor(pe)
            n_mix1.done(pe)

            def lru_proj(i):
                w = landed(pe, ("lin", i, 0)).rearrange("p (k n) -> p k n", k=KT)
                if i >= 2:
                    pe.wait_ge(S_("lru_xc"), i - 1)
                    pe.wait_ge(S_("lru_gb"), i - 1)
                for n in range(4):
                    for k in range(KT):
                        last = mm(ps[:, 4 + 2 * (i % 2) + n // 2, (n % 2) * S:(n % 2 + 1) * S], w[:, k, n * P:(n + 1) * P], hT[:, k, :],
                                  k == 0, k == KT - 1)
                last.then_inc(S_("chunk_used"), 1)

            def lru_gate(i, w):
                pe.wait_ge(S_("lru_xc"), i + 1)
                if i >= 2:
                    pe.wait_ge(S_("lru_tanh"), 2 * (i - 1))
                for which in range(2):
                    for n in range(2):
                        for k in range(2):
                            last = mm(ps[:, 2 * (i % 2) + which, n * S:(n + 1) * S], w[:, which, i, k, n * P:(n + 1) * P], xc[:, 2 * i + k, :],
                                      k == 0, k == 1)
                last.then_inc(S_("lgate"), 1)

            lru_proj(0)
            pe.wait_ge(S_("gate_w_in"), 16)
            for i in range(1, 4):
                lru_proj(i)
                lru_gate(i - 1, lgw)
            lru_gate(3, lgw)
            pe.wait_ge(S_("lT"), 1)
            out_projection([("lout", i, 0) for i in range(2)], lT, 8)
            ada_three(6)
            n_ffn1.tensor(pe)
            n_ffn1.done(pe)
            gated_up(1)
            out_projection([("down", 1, i) for i in range(6)], aT, FT)
            ada_three(9)
            pe.wait_ge(S_("modc"), 3)
            n_ctx.tensor(pe)
            n_ctx.done(pe)
            n_lat.tensor(pe)
            n_lat.done(pe)

            for c in range(3):
                w = landed(pe, ("win", c, 0)).rearrange("p (k n) -> p k n", k=KT)
                for m in range(H4):
                    n = 4 * c + m
                    if n >= 8:
                        pe.wait_ge(S_("qkv_conv"), n - 7)
                    t0 = S if c == 0 else 0
                    for k in range(KT):
                        last = mm(ps[:, n % 8, 0:2 * S - t0], w[:, k, m * P:(m + 1) * P], hT2[:, k, t0:2 * S], k == 0, k == KT - 1)
                    last.then_inc(S_("qkv" if m < 3 else "chunk_used"), 1)
            prev = None
            for n, (what, t) in enumerate(TOKU):
                if what != prev:
                    w = landed(pe, ("win", 3 + WHATS.index(what), 0)).rearrange("p (k n) -> p k n", k=KT)
                    prev = what
                b = 12 + n - 8
                if b < 12:
                    pe.wait_ge(S_("qkv_conv"), b + 1)
                else:
                    wait_unit(pe, b - 12)
                for k in range(KT):
                    last = mm(ps[:, (12 + n) % 8, :], hT2[:, k, t * P:(t + 1) * P], w[:, k, :], k == 0, k == KT - 1)
                last.then_inc(S_("tokproj" if t < 3 else "chunk_used"), 1)
            pe.wait_ge(S_("wab_in"), 16)
            wait_unit(pe, 6)
            for t in range(TT2):
                for k in range(KT):
                    last = mm(AB[:, t, :], hT2[:, k, t * P:(t + 1) * P], wab[:, k, :], k == 0, k == KT - 1)
            last.then_inc(S_("ab"), 1)
            for n in range(len(TOKU)):
                wait_unit(pe, n)
            pe.wait_ge(S_("qk_sq"), 1)
            for i in range(24):
                last = mm(ps[:, 1, i:i + 1], sqk[:, LENAT(i):LENAT(i) + P], cst[:, C_ONE, 0:1], True, True)
            last.then_inc(S_("lens"), 1)
            pe.wait_ge(S_("dec"), 1)
            for m in range(5):
                last = mm(ps[:, 0, 64 * m:64 * m + 64], cst[:, m, :], dec[:, :, :].rearrange("p a b -> p (a b)"), True, True)
            last.then_inc(S_("sums"), 1)
            pe.wait_ge(S_("qkv_silu"), 12)
            pe.wait_ge(S_("EX"), 1)
            pe.wait_ge(S_("lengths"), 1)
            pe.wait_ge(S_("beta"), 1)
            for n, (what, t) in enumerate(TRANS):
                if n >= 8:
                    trans_out(pe, n - 8)
                src = {"v": vT, "kn": kT, "qn": qT}.get(what)
                if what in ("rqT", "rkT"):
                    s_ = rq[:, t - TT, :, :] if what == "rqT" else rk[:, t, :, :]
                elif what in ("knT", "qnT"):
                    trans_out(pe, TRANS.index((what[0:2], t)))
                    s_ = kn[:, t, :, :] if what == "knT" else qn[:, t - TT, :, :]
                else:
                    c0 = (t - TT if what == "qn" else t) * P
                    s_ = src[:, :, c0:c0 + P]
                for h in range(H4):
                    last = nc.tensor.transpose(ps[:, n % 8, h * P:(h + 1) * P], s_[:, h, :], ident)
                last.then_inc(S_("trans"), 1)
            for n in range(len(TRANS)):
                trans_out(pe, n)

            def heads(bank, left_of, right_of, start=True, stop=True):
                for h in range(H4):
                    last = mm(ps[:, bank, h * P:(h + 1) * P], left_of[:, h, :], right_of[:, h, :], start, stop)
                return last

            def tile(a, t):
                return a[:, :, t * P:(t + 1) * P]

            def lemask(d):
                return cst[:, C_GE if d else C_LE, :]

            def decay_transposed(d, bank):
                for h in range(H4):
                    last = mm(ps[:, bank, h * P:(h + 1) * P], gS[d][:, h, :], lemask(d), True, True)
                last.then_inc(S_("diff"), 1)

            for n in range(2 * TT2):
                t, d = divmod(n, 2)
                pe.wait_ge(S_("gS"), n + 1)
                if n >= 2:
                    pe.wait_ge(S_("decay"), n - 1)
                mm(ps[:, n % 2, :], lemask(d), gS[d].rearrange("p a b -> p (a b)"), True, True).then_inc(S_("diff"), 1)
                if d == 0:
                    if t >= 2:
                        pe.wait_ge(S_("A"), 2 * (t - 1))
                    heads(2 + t % 2, tile(kT, t), tile(kT, t)).then_inc(S_("kk"), 1)
            for d in DIRS:
                pe.wait_ge(S_("gS"), 2 * TT2 + d + 1)
                decay_transposed(d, 4 + d)
            pe.wait_ge(S_("A"), 2 * TT2)
            pe.wait_ge(S_("decay"), 2 * TT2 + 2)
            for step in range(STEPS):
                if step >= 2:
                    for d in DIRS:
                        t = TILE_OF[d][step]
                        if step > 2:
                            pe.wait_ge(S_("rPm"), later(step - 1, d))
                        heads(4 * d, tile(rkT, t), tile(rqT, t - TT)).then_inc(S_("rqk"), 1)
                    for d in DIRS:
                        t = TILE_OF[d][step]
                        pe.wait_ge(S_("rstate"), nth(step - 1, d))
                        if step > 2:
                            pe.wait_ge(S_("o_out"), later(step - 1, d))
                        heads(4 * d + 1, tile(rqT, t - TT), rSt[d])
                if step < 3:
                    for d in DIRS:
                        pe.wait_ge(S_("rkdec"), nth(step, d))
                        if step:
                            pe.wait_ge(S_("rstate"), nth(step - 1, d))
                        heads(4 * d + 3, rkdec[d], rv[:, TILE_OF[d][step], :, :]).then_inc(S_("rdS"), 1)
                if step >= 2:
                    for d in DIRS:
                        pe.wait_ge(S_("rPm"), later(step, d))
                        heads(4 * d + 2, rPm[d], rv[:, TILE_OF[d][step], :, :]).then_inc(S_("ro"), 1)
            for step in range(STEPS):
                pe.wait_ge(S_("o_out"), 4 + max(step - 2, 0) * 2)
                if step:
                    pe.wait_ge(S_("vnew_out"), 2 * step)
                for d in DIRS:
                    pe.wait_ge(S_("X_in"), nth(step, d))
                    for h in range(H4):
                        last = nc.tensor.transpose(ps[:, 4 * d, h * P:(h + 1) * P], X[d][:, h, :], ident)
                    last.then_inc(S_("X_turned"), 1)
                if step >= 2:
                    for d in DIRS:
                        pe.wait_ge(S_("gS"), 2 * TT2 + 2 + later(step, d))
                        pe.wait_ge(S_("state"), nth(step - 1, d))
                        decay_transposed(d, 4 * d + 3)
                for l in range(LEVELS):
                    for d in DIRS:
                        t = TILE_OF[d][step]
                        if l:
                            pe.wait_ge(S_("X_out"), level(step, l - 1, d))
                        else:
                            pe.wait_ge(S_("XT_in"), nth(step, d))
                        heads(4 * d, Am[4 * d + t], XT[d]).then_inc(S_("Y"), 1)
                    if l == LEVELS - 1 and step >= 2:
                        for d in DIRS:
                            t = TILE_OF[d][step]
                            heads(4 * d + 2, tile(kT, t), tile(qT, t - TT)).then_inc(S_("qk"), 1)
                    for d in DIRS:
                        pe.wait_ge(S_("Y_out"), level(step, l, d))
                        last = heads(4 * d + 1, X[d], Yt[d])
                        if l < LEVELS - 1:
                            last = heads(4 * d + 2, Yt[d], X[d])
                        last.then_inc(S_("Z"), 1)
                if step:
                    for d in DIRS:
                        pe.wait_ge(S_("X_out"), level(step, LEVELS - 1, d))
                        pe.wait_ge(S_("R"), nth(step, d))
                        heads(4 * d, Rk[d], XT[d]).then_inc(S_("wT"), 1)
                for d in DIRS:
                    if step == 0:
                        pe.wait_ge(S_("X_out"), level(step, LEVELS - 1, d))
                        pe.wait_ge(S_("R"), nth(step, d))
                        heads(4 * d + 1, XT[d], Rv[d]).then_inc(S_("vnew"), 1)
                    else:
                        pe.wait_ge(S_("wT_out"), nth(step - 1, d))
                        pe.wait_ge(S_("state"), nth(step - 1, d))
                        for h in range(H4):
                            mm(ps[:, 4 * d + 1, h * P:(h + 1) * P], XT[d][:, h, :], Rv[d][:, h, :], True, False)
                            last = mm(ps[:, 4 * d + 1, h * P:(h + 1) * P], wT[d][:, h, :], St[d][:, h, :], False, True)
                        last.then_inc(S_("vnew"), 1)
                if step >= 2:
                    for d in DIRS:
                        heads(4 * d, tile(qT, TILE_OF[d][step] - TT), St[d])
                if step < 3:
                    for d in DIRS:
                        pe.wait_ge(S_("vnew_out"), nth(step, d))
                        pe.wait_ge(S_("kdec"), nth(step, d))
                        if step >= 2:
                            pe.wait_ge(S_("decay"), 2 * TT2 + 2 + later(step, d))
                        elif step:
                            pe.wait_ge(S_("state"), nth(step - 1, d))
                        heads(4 * d + 3, kdec[d], vnew[d]).then_inc(S_("dS"), 1)
                if step >= 2:
                    for d in DIRS:
                        pe.wait_ge(S_("Pm"), later(step, d))
                        pe.wait_ge(S_("vnew_out"), nth(step, d))
                        heads(4 * d + 2, ET[d], vnew[d]).then_inc(S_("o"), 1)

            def y_transposes(k, bank):
                for i in range(2):
                    for t in range(TT):
                        last = nc.tensor.transpose(ps[:, bank, i * S + t * P:i * S + (t + 1) * P], y2[(k + i) // 4][:, t, (k + i) % 4, :], ident)
                last.then_inc(S_("yT"), 1)

            def delta_transposes():
                pe.wait_ge(S_("mixed"), 4)
                y_transposes(0, 4)
                y_transposes(2, 6)
                pe.wait_ge(S_("yT_a"), 3)
                pe.wait_ge(S_("yT_v"), 1)

            pe.wait_ge(S_("mixed"), 2)
            pe.wait_ge(S_("vnew_out"), 8)
            y_transposes(4, 5)
            y_transposes(6, 7)
            pe.wait_ge(S_("yT_a"), 2)
            pe.wait_ge(S_("o_out"), 8)
            out_projection([("wo2", i, 0) for i in range(2)], yT, 8, order=(1, 0), between=delta_transposes)
            n_ffn2.tensor(pe)
            n_ffn2.done(pe)
            for j in range(11):
                w = landed(pe, ("up2", j, 0)).rearrange("p (k n) -> p k n", k=KT)
                if j >= 2:
                    pe.wait_ge(S_("aT2"), j - 1)
                for n in range(4):
                    for k in range(KT):
                        last = mm(ps[:, 4 + 2 * (j % 2) + n // 2, (n % 2) * S:(n % 2 + 1) * S], w[:, k, n * P:(n + 1) * P], hT[:, k, :],
                                  k == 0, k == KT - 1)
                last.then_inc(S_("chunk_used"), 1)
            pe.wait_ge(S_("aT2"), 11)
            out_projection([("down2", i, 0) for i in range(6)], aT, FT2)


def cols(a):
    return np.ascontiguousarray(a.reshape(-1, P).T)


def tiles(w):
    k, n = w.shape[0] // P, w.shape[1]
    return w.reshape(k, P, n).transpose(1, 0, 2).reshape(P, k * n)


def weight_stream(i):
    qkv, lin, win = i["attn_w_qkv"][0], i["lru_w_in"][0], i["w_in_2"][0]
    halves = lambda w, half, n: np.concatenate([w[:, n * 256:(n + 1) * 256], w[:, half + n * 256:half + (n + 1) * 256]], 1)
    W = np.zeros((NCH, P, SLOT), np.float32)
    starts = {0: 0, 1: 512, 2: 1024, 3: 1536, 4: 2064, 5: 2576, 6: 3088, 7: 3600}
    for c, (kind, a, b) in enumerate(STREAM):
        if kind == "V":
            at = ((b * 3 + 2) * HEADS + 4 * a) * P
            w = qkv[:, at:at + 512]
        elif kind == "K":
            q, k = ((b * 3 + s) * HEADS * P + 2 * a * P for s in range(2))
            w = np.concatenate([qkv[:, q:q + 256], qkv[:, k:k + 256]], 1)
        elif kind == "wo":
            w = i["attn_w_o"][0][a * 512:(a + 1) * 512]
        elif kind == "ada":
            w = i["ada_w_2"][0][:, a * 512:(a + 1) * 512]
        elif kind == "up":
            w = halves(i["ffn_w_up"][a], FF, b)
        elif kind == "down":
            w = i["ffn_w_down"][a][b * 512:(b + 1) * 512]
        elif kind == "lin":
            w = halves(lin, D, a)
        elif kind == "lout":
            w = i["lru_w_out"][0][a * 512:(a + 1) * 512]
        elif kind == "win":
            w = win[:, starts[a]:starts[a] + 512]
        elif kind == "wo2":
            w = i["w_out_2"][0][a * 512:(a + 1) * 512]
        elif kind == "up2":
            w = halves(i["w_ffn_in_2"][0], FF2, a)
        else:
            w = i["w_ffn_out_2"][0][a * 512:(a + 1) * 512]
        t = tiles(w)
        W[c, :, :t.shape[1]] = t
    return W


def constants():
    r = np.arange(P)
    l, m = r[:, None], r[None, :]
    cst = np.zeros((P, NCONST, P), np.float32)
    for n, mask in enumerate((l <= m, l >= m, l > m, l < m, l >= 0 * m, l == m)):
        cst[:, n, :] = mask
    for n in range(LEVELS):
        w = BLK << n
        same = l // (2 * w) == m // (2 * w)
        cst[:, 6 + n, :] = same & (l // w % 2 == 0) & (m // w % 2 == 1)
        cst[:, 6 + LEVELS + n, :] = same & (l // w % 2 == 1) & (m // w % 2 == 0)
    cst[:, 6 + 2 * LEVELS, :] = l // BLK == m // BLK
    dist = S - 1 - np.arange(WLEN)
    exact = BUCKETS // 2
    dd = np.maximum(dist, 1).astype(np.float64)
    large = exact + (np.log(dd / exact) / np.log(MAX_DISTANCE / exact) * (BUCKETS - exact)).astype(np.int32)
    bucket = np.where(dist < exact, dist, np.minimum(large, BUCKETS - 1))
    onehot = np.zeros((BUCKETS, GROUPS, WLEN), np.float32)
    negm = np.full((HEADS, GROUPS, WLEN), NEG, np.float32)
    for g, dil in enumerate(DILATIONS):
        for n, d in enumerate(dist):
            if d >= 0 and d % dil == 0 and d // dil <= BAND:
                onehot[bucket[n], g, n] = 1
                negm[:, g, n] = 0
    f = np.float32
    t = np.arange(S)
    zero, ctx_len = np.zeros(S), np.full(S, float(S))
    pos = [np.concatenate(p).astype(f) for p in ((t, ctx_len), (zero, t // 64), (zero, t % 64))]
    ang = []
    for p, n in zip(pos, (16, 24, 24)):
        inv = (f(10000.0) ** (-np.arange(n, dtype=f) / f(n))).astype(f)
        ang.append(p[:, None] * inv[None, :])
    ang = np.concatenate(ang, 1).astype(f)
    c, s = np.cos(ang).astype(f), np.sin(ang).astype(f)
    rope = np.stack([np.concatenate([c, c], 1), np.concatenate([-s, s], 1)], 1)
    rope = np.ascontiguousarray(rope.reshape(TT2, P, 2, P).transpose(1, 0, 2, 3))
    sel = np.zeros((2, P), f)
    sel[0] = 1
    return {"cst": cst, "onehot": onehot, "negm": negm, "rope": rope, "sel": sel}


def kernel(**inputs):
    import concourse.bacc as bacc
    from concourse.bass_utils import run_bass_kernel_spmd

    i = {k: np.asarray(v) for k, v in inputs.items()}
    par = np.concatenate([
        cols(i["norm_mix_pre"]), cols(i["norm_ffn_pre"]), cols(i["lru_conv_w"]), cols(i["lru_conv_b"]),
        cols(i["lru_ga_b"]), cols(i["lru_gx_b"]), cols(i["lru_lambda"]), cols(i["norm_mix_g_2"]),
        cols(i["norm_ffn_g_2"]), cols(i["ffn_conv_w"]), cols(i["ffn_conv_b"]), cols(i["conv_w_2"]), cols(i["ada_b_2"]),
        np.stack([cols(i["c_2"]), cols(i["c_ctx_2"])], 2).reshape(P, 16)], 1)
    gate_w = np.stack([i[n][0].reshape(4, 2, P, 256).transpose(2, 0, 1, 3) for n in ("lru_ga_w", "lru_gx_w")], 1)
    ada_b = i["ada_b_2"][0]
    arrays = {
        "x": i["x"][0], "ctx": i["ctx_2"][0], "W": weight_stream(i), "par": par, "gate_w": gate_w,
        "rel_bias": i["rel_bias"],
        "gains": np.concatenate([i["norm_mix_post"][0:1], i["norm_ffn_post"][0:1], i["norm_mix_post"][1:2],
                                 i["norm_ffn_post"][1:2], i["final_g_2"][None]], 0),
        "ada_gate_b": np.stack([ada_b[2 * D:3 * D], ada_b[5 * D:6 * D]], 0),
        "wab": i["w_in_2"][0][:, 2048:2064].reshape(KT, P, 16).transpose(1, 0, 2),
        "normg2": np.concatenate([i["gdn_norm_g_2"], i["ret_norm_g_2"]], 0),
        "head_vec": np.concatenate([i["gdn_a_log_2"].reshape(1, 8), i["gdn_dt_bias_2"].reshape(1, 8),
                                    i["ret_decay_logit_2"].reshape(1, 8)], 1),
        **constants(),
    }
    arrays = {k: np.ascontiguousarray(a) for k, a in arrays.items()}
    nc = bacc.Bacc("TRN2", target_bir_lowering=False, num_devices=1)
    aps = {k: nc.dram_tensor(f"in_{k}", a.shape, F32, kind="ExternalInput").ap() for k, a in arrays.items()}
    out = nc.dram_tensor("out_x", (S, D), F32, kind="ExternalOutput").ap()
    build_program(nc, aps, out)
    r = run_bass_kernel_spmd(nc, [{f"in_{k}": a for k, a in arrays.items()}], core_ids=[0])
    return r.results[0]["out_x"].reshape(1, S, D)
```

```python
from contextlib import ExitStack

import numpy as np

import concourse.bass as bass
from concourse import mybir

F32 = mybir.dt.float32
F32R = mybir.dt.float32r
ALU = mybir.AluOpType
ACT = mybir.ActivationFunctionType
AX = mybir.AxisListType

P = 128
D = 1024
KT = D // P
TT = 2
S = TT * P
EPS = 1e-6
NS = 3
SLOT = 4096
HD_SCALE = float(P) ** -0.5

GROUPS = 3
HEADS = 8
DILATIONS = (1, 4, 16)
BAND = 128
BUCKETS = 32
MAX_DISTANCE = 2048
NEG = -1e30
WLEN = 384

FF = 3 * D
FT = FF // P
FF2 = 2816
FT2 = FF2 // P

H4 = 4
NG = 16
TT2 = 4
BLK = 16
NB = P // BLK
NPARTS, PARTS_AT = 3, 13312
LEVELS = 3

PC = {}
_at = 0
for _name, _n in (("mix_pre", 16), ("ffn_pre", 16), ("lru_conv_w", 32), ("lru_conv_b", 8),
                  ("ga_b", 8), ("gx_b", 8), ("lam", 8), ("mix_g2", 8), ("ffn_g2", 8),
                  ("ffn_conv_w", 288), ("ffn_conv_b", 96), ("conv_w2", 60), ("ada_b", 48),
                  ("cond", 16)):
    PC[_name] = _at
    _at += _n
NPC = _at

C_LE, C_GE, C_GT, C_LT, C_ONE, C_ID = range(6)
C_LEVEL = 6
NCONST = 6 + 2 * LEVELS + 1


def attention_order():
    k = lambda hp, g: ("K", hp, g)
    v = lambda q, g: ("V", q, g)
    s = lambda h: ("S", h, 0)
    t = lambda h: ("T", h, 0)
    o = lambda h: ("O", h, 0)
    return [v(0, 0), v(0, 1), v(0, 2), k(0, 0), k(0, 1), k(0, 2),
            s(0), k(1, 0), t(0), s(1), k(1, 1), o(0), t(1), k(1, 2),
            o(1), s(2), k(2, 0), t(2), s(3), k(2, 1), o(2), t(3), k(2, 2),
            o(3), s(4), v(1, 0), t(4), s(5), v(1, 1), v(1, 2),
            o(4), t(5), k(3, 0), o(5), k(3, 1), k(3, 2),
            s(6), t(6), s(7), o(6), t(7), o(7)]


def stream_order():
    ada = [("ada", i, 0) for i in range(12)]
    return ([c for c in attention_order() if c[0] in "VK"]
            + [("wo", i, 0) for i in range(2)] + ada[0:3]
            + [("up", 0, i) for i in range(12)] + [("down", 0, i) for i in range(6)] + ada[3:6]
            + [("lin", i, 0) for i in range(4)] + [("lout", i, 0) for i in range(2)] + ada[6:9]
            + [("up", 1, i) for i in range(12)] + [("down", 1, i) for i in range(6)] + ada[9:12]
            + [("win", i, 0) for i in range(8)] + [("wo2", i, 0) for i in (1, 0)]
            + [("up2", i, 0) for i in range(11)] + [("down2", i, 0) for i in range(6)])


STREAM = stream_order()
NCH = len(STREAM)
POSITION = {c: i for i, c in enumerate(STREAM)}


def build_program(nc, A, out):
    ctx = ExitStack()
    with ctx:
        def sb(name, shape):
            return ctx.enter_context(nc.sbuf_tensor(name, shape, F32))

        sems = {}

        def S_(name):
            if name not in sems:
                sems[name] = ctx.enter_context(nc.semaphore(name))
            return sems[name]

        ring = sb("ring", [P, NS, SLOT])
        x = sb("x", [P, TT, D])
        gains = sb("gains", [P, 2, D])
        gates = sb("gates", [P, 2, D])
        par = sb("par", [P, NPC])
        row = sb("row", [2, 2, 512])
        sel = sb("sel", [2, P])
        cst = sb("cst", [P, 6, P])
        modT = sb("modT", [P, 48, 2])
        small = sb("small", [P, 192])
        smallp = sb("smallp", [P, 64])
        tmpc = sb("tmpc", [P, 40])
        arena_space = nc.sbuf_tensor("arena", [P, 31744], F32)
        arena = arena_space.__enter__()
        arena_space.__exit__(None, None, None)
        sb("below_parts", [P, PARTS_AT])
        parts = ctx.enter_context(nc.sbuf_tensor("parts", [P, NPARTS, 2, D + S], F32R))
        hparts = ctx.enter_context(nc.sbuf_tensor("hparts", [P, 2, KT, S], F32R))
        ps = ctx.enter_context(nc.psum_tensor("ps", [P, 8, 512], F32))
        table = nc.dram_tensor("distance_tables", [HEADS, P, GROUPS * WLEN], F32)
        matrices = nc.dram_tensor("matrices", [2, P, TT2, H4, P], F32)
        block_inverses = nc.dram_tensor("block_inverses", [NB, TT2 * H4, 2, BLK, BLK], F32)

        ident = cst[:, C_ID, :]
        def region(start, *shape):
            n = int(np.prod(shape))
            assert start + n <= 31744, (start, shape)
            v = arena[:, start:start + n]
            if len(shape) == 1:
                return v
            names = "abcd"[:len(shape)]
            return v.rearrange(f"p ({' '.join(names)}) -> p {' '.join(names)}",
                               **{k: m for k, m in zip(names, shape)})

        def pcol(name, i=0, n=1):
            return par[:, PC[name] + i:PC[name] + i + n]

        xn = region(0, TT, D)
        hT = region(2048, KT, S)
        bias = region(4096, HEADS, GROUPS, S)
        V = region(10240, TT, GROUPS, 4, P)
        QKb = [region(13312 + 3072 * b, GROUPS, 4, S) for b in range(2)]
        L = [region(19456 + 1152 * b, GROUPS, 384) for b in range(2)]
        PT = region(21760, 9, P)
        oT = region(22912, HEADS, S)
        onehot = region(24960, GROUPS, WLEN)
        negm = region(26112, GROUPS, WLEN)
        wtab = region(27264, GROUPS, WLEN)
        relb = region(28416, 24)
        aT = region(4096, FT, S)
        u = [region(10240 + 1024 * b, 4, S) for b in range(2)]
        gl = [region(12288 + 512 * b, 2, S) for b in range(2)]
        xc = region(4096, KT, S)
        gb = region(6144, KT, S)
        tr = region(8192, KT, S)
        ti = region(10240, KT, S)
        av = region(23552, KT, S)
        th = region(25600, KT, S)
        mu = region(0, KT, S)
        lT = region(21504, KT, S)
        lgw = region(27648, 2, 4, 2, S)

        def mm(o, l, r, start, stop):
            return nc.tensor.matmul(o, l, r, start=start, stop=stop)

        def landed(pe, chunk):
            i = POSITION[chunk]
            pe.wait_ge(S_(f"landed{i % NS}"), 16 * (i // NS + 1))
            return ring[:, i % NS, :]

        def chunk_done(eng, chunk):
            eng.wait_ge(S_("chunk_used"), POSITION[chunk] + 1)

        class Norm:

            def __init__(self, index, col, src, scaled, dst, gain, shift, ready, banks=(4, 5, 6, 7), split=False):
                self.split = split
                self.index, self.col, self.src, self.scaled, self.dst = index, col, src, scaled, dst
                self.gain, self.shift, self.ready, self.banks = gain, shift, ready, banks

            def scalar_square(self, act):
                for t in range(TT):
                    self.ready(act, t)
                    nc.scalar.activation(xn[:, t, :], self.src[:, t, :], ACT.Square,
                                         accum_out=small[:, self.col + t:self.col + t + 1]).then_inc(S_("norm_squared"), 1)

            def pool(self, pool):
                rstd(pool, "norm", self.index, self.col)

            def vector_scale(self, dve):
                for t in range(TT):
                    dve.wait_ge(S_("norm_rstd"), TT * self.index + t + 1)
                    nc.vector.tensor_scalar(self.scaled[:, t, :], self.src[:, t, :],
                                            smallp[:, self.col + t:self.col + t + 1], None, ALU.mult).then_inc(S_("norm_scaled"), 1)

            def tensor(self, pe):
                for t in range(TT):
                    pe.wait_ge(S_("norm_scaled"), TT * self.index + t + 1)
                    for k in range(KT):
                        o = ps[:, self.banks[k // 2], (k % 2) * S + t * P:(k % 2) * S + (t + 1) * P]
                        last = nc.tensor.transpose(o, self.scaled[:, t, k * P:(k + 1) * P], ident)
                        if t == TT - 1 and k % 2:
                            last.then_inc(S_("norm_transposed"), 1)

            def evacuate_parts(self, eng, which):
                for b in range(KT // 2):
                    if which == 0:
                        eng.wait_ge(S_("norm_transposed"), KT // 2 * self.index + b + 1)
                        for k in (2 * b, 2 * b + 1):
                            last = nc.scalar.activation(hparts[:, 0, k, :], ps[:, self.banks[b], (k % 2) * S:(k % 2 + 1) * S], ACT.Identity,
                                                        scale=self.gain(k), bias=self.shift(k) if self.shift else 0.0)
                        last.then_inc(S_("norm_out_scalar"), 1)
                    else:
                        eng.wait_ge(S_("norm_out_scalar"), KT // 2 * self.index + b + 1)
                        for k in (2 * b, 2 * b + 1):
                            src = ps[:, self.banks[b], (k % 2) * S:(k % 2 + 1) * S]
                            if self.shift:
                                last = nc.vector.tensor_scalar(self.dst[:, k, :], src, self.gain(k), self.shift(k), ALU.mult, ALU.add)
                            else:
                                last = nc.vector.scalar_tensor_tensor(hparts[:, 1, k, :], src, self.gain(k), hparts[:, 0, k, :],
                                                                      ALU.mult, ALU.subtract)
                        if self.shift:
                            last.then_inc(S_("shifted"), 1)
                            eng.wait_ge(S_("shifted"), b + 1)
                            last = nc.vector.tensor_tensor(hparts[:, 1, 2 * b:2 * b + 2, :], self.dst[:, 2 * b:2 * b + 2, :],
                                                           hparts[:, 0, 2 * b:2 * b + 2, :], ALU.subtract)
                        last.then_inc(S_("norm_out_vector"), 1)

            def evacuate(self, eng, which):
                if self.split:
                    return self.evacuate_parts(eng, which)
                for k in range(KT):
                    if k // 2 % 2 != which:
                        continue
                    eng.wait_ge(S_("norm_transposed"), KT // 2 * self.index + k // 2 + 1)
                    src = ps[:, self.banks[k // 2], (k % 2) * S:(k % 2 + 1) * S]
                    done = S_(("norm_out_scalar", "norm_out_vector")[which])
                    if which == 0:
                        b = self.shift(k) if self.shift else 0.0
                        nc.scalar.activation(self.dst[:, k, :], src, ACT.Identity, scale=self.gain(k), bias=b).then_inc(done, 1)
                    elif self.shift:
                        nc.vector.tensor_scalar(self.dst[:, k, :], src, self.gain(k), self.shift(k), ALU.mult, ALU.add).then_inc(done, 1)
                    else:
                        nc.vector.tensor_scalar(self.dst[:, k, :], src, self.gain(k), None, ALU.mult).then_inc(done, 1)

            def done(self, eng):
                eng.wait_ge(S_("norm_out_scalar"), KT // 2 * (self.index + 1))
                eng.wait_ge(S_("norm_out_vector"), KT // 2 * (self.index + 1))

        def rstd(pool, name, index, col):
            for t in range(TT):
                pool.wait_ge(S_(name + "_squared"), TT * index + t + 1)
                c = slice(col + t, col + t + 1)
                nc.gpsimd.tensor_scalar(smallp[:, 32 + col + t:33 + col + t], small[:, c], 1.0 / D, EPS, ALU.mult, ALU.add).then_inc(S_("pool_step"), 1)
                pool_steps[0] += 1
                pool.wait_ge(S_("pool_step"), pool_steps[0])
                nc.gpsimd.tensor_tensor(smallp[:, c], smallp[:, 32 + col + t:33 + col + t], smallp[:, 31:32], ALU.pow).then_inc(S_(name + "_rstd"), 1)

        pool_steps = [0]

        UNITS = []
        units_split = {"high": 0, "low": 0}

        def high_parts(act, end):
            for n in range(units_split["high"], end):
                chunk, weights, inputs, ready = UNITS[n]
                if n == 0 or UNITS[n - 1][0] != chunk:
                    landed(act, chunk)
                if inputs is not None:
                    ready(act)
                if n >= NPARTS:
                    act.wait_ge(S_("parts_used"), n - NPARTS + 1)
                last = nc.scalar.activation(unit_weights(n, 0, weights), weights, ACT.Copy)
                if inputs is not None:
                    last = nc.scalar.activation(parts[:, n % NPARTS, 0, D:D + S], inputs, ACT.Copy)
                last.then_inc(S_("high_parts"), 1)
            units_split["high"] = max(units_split["high"], end)

        def low_parts(dve, end):
            for n in range(units_split["low"], end):
                _, weights, inputs, _ = UNITS[n]
                dve.wait_ge(S_("high_parts"), n + 1)
                last = nc.vector.tensor_tensor(unit_weights(n, 1, weights), weights, unit_weights(n, 0, weights), ALU.subtract)
                if inputs is not None:
                    last = nc.vector.tensor_tensor(parts[:, n % NPARTS, 1, D:D + S], inputs, parts[:, n % NPARTS, 0, D:D + S], ALU.subtract)
                last.then_inc(S_("low_parts"), 1)
            units_split["low"] = max(units_split["low"], end)

        def unit_weights(n, part, like):
            w = parts[:, n % NPARTS, part, 0:D]
            return w if len(like.shape) == 2 else w.rearrange("p (k n) -> p k n", n=P)

        def slot(chunk):
            return ring[:, POSITION[chunk] % NS, :]

        class SplitUp:

            def __init__(self, chunks, out_waits):
                self.chunks, self.out_waits = chunks, out_waits
                self.first = len(UNITS)
                for c in chunks:
                    for n in range(4):
                        UNITS.append((c, slot(c).rearrange("p (k n) -> p k n", k=KT)[:, :, n * P:(n + 1) * P], None, None))

            def upto(self, j):
                return self.first + 4 * (j + 1) + NPARTS

            def done(self, eng, j):
                eng.wait_ge(S_("parts_used"), self.first + 4 * (j + 1))

            def tensor(self, pe):
                for j in range(len(self.chunks)):
                    if j >= 2:
                        self.out_waits(pe, j - 2)
                    for n in range(4):
                        u = self.first + 4 * j + n
                        pe.wait_ge(S_("low_parts"), u + 1)
                        for k in range(KT):
                            for w_part, x_part in ((0, 1), (0, 0), (1, 0)):
                                last = nc.tensor.matmul(ps[:, 4 + 2 * (j % 2) + n // 2, (n % 2) * S:(n % 2 + 1) * S],
                                                        parts[:, u % NPARTS, w_part, k * P:(k + 1) * P], hparts[:, x_part, k, :],
                                                        start=k == 0 and x_part == 1, stop=k == KT - 1 and w_part == 1)
                                if n == 3 and k == 0 and x_part == 1:
                                    last.then_inc(S_("chunk_used"), 1)
                        last.then_inc(S_("parts_used"), 1)

        class SplitProjection:

            def __init__(self, chunks, src, tiles, ready):
                self.tiles = tiles
                self.first = len(UNITS)
                for kk in range(tiles):
                    c = chunks[kk // 4]
                    UNITS.append((c, slot(c)[:, kk % 4 * D:(kk % 4 + 1) * D], src[:, kk, :], lambda e, kk=kk: ready(e, kk)))

            def scalar(self, act):
                high_parts(act, self.first + self.tiles)

            def vector(self, dve):
                low_parts(dve, self.first + self.tiles)

            def tensor(self, pe):
                for kk in range(self.tiles):
                    n = self.first + kk
                    pe.wait_ge(S_("low_parts"), n + 1)
                    frees = kk % 4 == 3 or kk == self.tiles - 1
                    for t in range(TT):
                        for x_part, w_part in ((1, 0), (0, 0), (0, 1)):
                            for half in range(2):
                                w0 = half * 512
                                last = nc.tensor.matmul(ps[:, 2 * t + half, :], parts[:, n % NPARTS, x_part, D + t * P:D + (t + 1) * P],
                                                        parts[:, n % NPARTS, w_part, w0:w0 + 512],
                                                        start=kk == 0 and x_part == 1, stop=kk == self.tiles - 1 and w_part == 1)
                                if frees:
                                    last.then_inc(S_("chunk_used"), 1)
                                    frees = False
                    last.then_inc(S_("parts_used"), 1)

            def done(self, eng):
                eng.wait_ge(S_("parts_used"), self.first + self.tiles)

        class Residual:

            def __init__(self, index, col, gain, product, normed=True, gain_ready=None):
                self.index, self.col, self.gain, self.normed, self.gain_ready = index, col, gain, normed, gain_ready
                self.product = product

            def y_ready(self, eng, t):
                if isinstance(self.product, SplitProjection):
                    self.product.done(eng)
                elif t == 0:
                    eng.wait_ge(S_("out_y"), 1)
                else:
                    chunk_done(eng, self.product)

            def y(self, t):
                return ps[:, 2 * t:2 * t + 2, :]

            def scalar(self, act):
                if not self.normed:
                    return
                for t in range(TT):
                    self.y_ready(act, t)
                    nc.scalar.activation(xn[:, t, :].rearrange("p (a b) -> p a b", a=2), self.y(t), ACT.Square,
                                         accum_out=small[:, self.col + t:self.col + t + 1]).then_inc(S_("out_squared"), 1)

            def pool(self, pool):
                if self.normed:
                    rstd(pool, "out", self.index, self.col)

            def vector(self, dve):
                self.gain_ready(dve)
                g = self.gain.rearrange("p (a b) -> p a b", a=2)
                for t in range(TT):
                    tmp = xn[:, t, :].rearrange("p (a b) -> p a b", a=2)
                    if self.normed:
                        dve.wait_ge(S_("out_rstd"), TT * self.index + t + 1)
                        nc.vector.scalar_tensor_tensor(tmp, self.y(t), smallp[:, self.col + t:self.col + t + 1], g, ALU.mult, ALU.mult).then_inc(S_("out_gained"), 1)
                    else:
                        self.y_ready(dve, t)
                        nc.vector.tensor_tensor(tmp, self.y(t), g, ALU.mult).then_inc(S_("out_gained"), 1)
                    dve.wait_ge(S_("out_gained"), TT * self.index + t + 1)
                    nc.vector.tensor_tensor(x[:, t, :], x[:, t, :], xn[:, t, :], ALU.add).then_inc(S_("out_x"), 1)

            def x_ready(self, eng, t):
                eng.wait_ge(S_("out_x"), TT * self.index + t + 1)

        def gain_ready(i):
            return lambda dve: dve.wait_ge(S_("gain"), 16 * (i + 1))

        p_mix0 = SplitProjection([("wo", i, 0) for i in range(2)], oT, KT, lambda e, kk: e.wait_ge(S_("oT"), HEADS))
        up_ffn0 = SplitUp([("up", 0, j) for j in range(12)], lambda e, j: e.wait_ge(S_("conv"), j + 1))
        p_ffn0 = SplitProjection([("down", 0, i) for i in range(6)], aT, FT, lambda e, kk: e.wait_ge(S_("aT"), kk // 2 + 1))
        p_mix1 = SplitProjection([("lout", i, 0) for i in range(2)], lT, KT, lambda e, kk: e.wait_ge(S_("lT"), kk // 2 + 1))
        up_ffn1 = SplitUp([("up", 1, j) for j in range(12)], lambda e, j: e.wait_ge(S_("conv"), 12 + j + 1))
        p_ffn1 = SplitProjection([("down", 1, i) for i in range(6)], aT, FT, lambda e, kk: e.wait_ge(S_("aT"), 12 + kk // 2 + 1))
        up_ffn2 = SplitUp([("up2", j, 0) for j in range(11)], lambda e, j: e.wait_ge(S_("aT2"), j + 1))
        p_ffn2 = SplitProjection([("down2", i, 0) for i in range(6)], aT, FT2, lambda e, kk: e.wait_ge(S_("aT2"), kk // 2 + 1))
        r_mix0 = Residual(0, 2, gains[:, 0, :], p_mix0, gain_ready=gain_ready(0))
        r_ffn0 = Residual(1, 6, gains[:, 1, :], p_ffn0, gain_ready=gain_ready(1))
        r_mix1 = Residual(2, 10, gains[:, 0, :], p_mix1, gain_ready=gain_ready(2))
        r_ffn1 = Residual(3, 14, gains[:, 1, :], p_ffn1, gain_ready=gain_ready(3))
        r_mix2 = Residual(4, 20, gates[:, 0, :], ("wo2", 0, 0), normed=False, gain_ready=lambda e: e.wait_ge(S_("ada_out"), 12))
        r_ffn2 = Residual(5, 24, gates[:, 1, :], p_ffn2, normed=False, gain_ready=lambda e: e.wait_ge(S_("ada_out"), 12))
        n_mix0 = Norm(0, 0, x, xn, hT, lambda k: pcol("mix_pre", k), None, lambda e, t: e.wait_ge(S_("x_in"), 16))
        n_ffn0 = Norm(1, 4, x, xn, hT, lambda k: pcol("ffn_pre", k), None, r_mix0.x_ready, split=True)
        n_mix1 = Norm(2, 8, x, xn, hT, lambda k: pcol("mix_pre", 8 + k), None, r_ffn0.x_ready)
        n_ffn1 = Norm(3, 12, x, xn, hT, lambda k: pcol("ffn_pre", 8 + k), None, r_mix1.x_ready, split=True)

        hT2 = region(2048, KT, 2 * S)
        ctxx = region(6144, TT, D)
        modc = small[:, 96:96 + 24]
        rope = region(8192, TT2, 2, P)
        lvl = region(9216, 2 * LEVELS + 1, P)
        qT = region(11008, H4, S)
        kT = region(12032, H4, 2 * S)
        vT = region(14080, H4, 2 * S)
        zt = region(16128, TT, 512)
        rgt = region(17152, TT, 512)
        rv = region(18176, TT2, H4, P)
        rk = region(20224, TT2, H4, P)
        rq = region(22272, TT, H4, P)
        cu = [region(23296 + 512 * b, 512) for b in range(2)]
        ct = [region(24320 + 512 * b, 512) for b in range(2)]
        wab = region(25344, KT, 16)
        normg2 = region(25472, 2, P)
        dec = region(25728, TT2, NG)
        beta = region(25792, TT2, 8)
        EX = region(25824, 5, TT2, NG)
        absc = region(26144, 8, 64)
        kn = region(0, TT2, H4, P)
        v_t = region(2048, TT2, H4, P)
        qn = region(4096, TT, H4, P)
        rqT = region(5120, H4, S)
        rkT = region(6144, H4, 2 * S)
        free = ([region(14080 + 512 * i, H4, P) for i in range(4)]
                + [region(23296 + 512 * i, H4, P) for i in range(4)]
                + [region(26656 + 512 * i, H4, P) for i in range(7)]
                + [region(o, H4, P) for o in (8704, 8192, 30720, 31232)]
                + [gains[:, 1, 512 * i:512 * (i + 1)].rearrange("p (a b) -> p a b", a=H4) for i in range(2)])
        Am = free[0:8]
        blocks = region(22272, 2, BLK, BLK)
        inverses = region(22784, 2, BLK, BLK)
        block_tmp = region(10112, 2, BLK * BLK)
        inverse_rows = region(26144, 2, TT2 * H4, BLK)
        gS = free[8:10]
        E = free[10:12]
        rET, rkdec, rPm, rSt = free[12:14], free[14:16], free[16:18], free[18:20]
        St, kdec, ET = free[12:14], free[14:16], free[16:18]
        left = [region(o + 512 * i, H4, P) for o, m in ((20224, 4), (18176, 4), (6144, 4), (5120, 2)) for i in range(m)]
        X, XT, Yt, Rk, Rv, wT, vnew = (left[2 * i:2 * i + 2] for i in range(7))
        tmpr = region(29728, H4, P)
        rsq = region(8704, 32)
        sqk = region(26656, 3072)
        hw2 = region(30240, 60)
        AB = ps[:, 2, 0:64].rearrange("p (t c) -> p t c", t=TT2)
        condT = small[:, 64:80].rearrange("p (k c) -> p k c", k=KT)

        TOKU = ([("z", t) for t in (2, 3)] + [("rq", t) for t in (2, 3)] + [("rk", t) for t in range(4)]
                + [("rv", t) for t in range(4)] + [("rg", t) for t in (2, 3)])
        TOKA = [sum(w in ("z", "rg", "rv") for w, _ in TOKU[:n]) for n in range(len(TOKU))]
        TOKV = [sum(w != "rv" for w, _ in TOKU[:n]) for n in range(len(TOKU))]

        WHATS = ("z", "rq", "rk", "rv", "rg")
        TOKP = [sum(t < 3 for _, t in TOKU[:n]) for n in range(len(TOKU))]

        def unit_done(eng, n):
            what, t = TOKU[n]
            if t < 3:
                eng.wait_ge(S_("tokproj"), TOKP[n] + 1)
            else:
                chunk_done(eng, ("win", 3 + WHATS.index(what), 0))

        def wait_unit(pe, n):
            if TOKU[n][0] == "rv":
                pe.wait_ge(S_("tok_act"), TOKA[n] + 1)
            else:
                pe.wait_ge(S_("tok_v"), TOKV[n] + 1)

        TRANS = ([("v", t) for t in range(4)] + [("kn", t) for t in range(4)] + [("qn", t) for t in (2, 3)]
                 + [("rkT", t) for t in range(4)] + [("rqT", t) for t in (2, 3)]
                 + [("knT", t) for t in range(4)] + [("qnT", t) for t in (2, 3)])
        ON_VECTOR = ("v", "kn", "qn")

        def trans_out(pe, n):
            mine = TRANS[n][0] in ON_VECTOR
            before = sum((w in ON_VECTOR) == mine for w, _ in TRANS[:n])
            pe.wait_ge(S_("trans_v" if mine else "trans_a"), before + 1)

        def B4(b):
            return ps[:, b, :].rearrange("p (h d) -> p h d", h=H4)

        def TB(n):
            return B4(n % 8)

        def LENAT(i):
            return (i % 4) * S + (i // 4) * P if i < 8 else 1024 + (i % 4) * 2 * S + ((i - 8) // 4) * P

        TILE_OF = ((0, 1, 2, 3), (1, 0, 3, 2))
        STEPS = len(TILE_OF[0])
        DIRS = (0, 1)

        def nth(step, d):
            return 2 * step + d + 1

        def later(step, d):
            return nth(step - 2, d)

        def level(step, l, d):
            return nth(step * LEVELS + l, d)

        y2 = [region(22272, TT, H4, P), region(4096, TT, H4, P)]
        yT = region(2048, KT, S)

        n_ctx = Norm(4, 16, ctxx, ctxx, hT2[:, :, 0:S], lambda k: modc[:, 8 + k:9 + k], lambda k: modT[:, k, 1:2],
                     lambda e, t: (e.wait_ge(S_("ctx_in"), 16), r_ffn1.x_ready(e, t)))
        n_lat = Norm(5, 18, x, xn, hT2[:, :, S:2 * S], lambda k: modc[:, k:k + 1], lambda k: modT[:, k, 0:1], r_ffn1.x_ready)
        n_ffn2 = Norm(6, 22, x, xn, hT, lambda k: modc[:, 16 + k:17 + k], lambda k: modT[:, 24 + k, 0:1], r_mix2.x_ready, split=True)

        ORDER = attention_order()
        proj = [c for c in ORDER if c[0] in "VK"]
        UNIT = {c: 2 * i for i, c in enumerate(proj)}

        block = ctx.enter_context(nc.Block())

        @block.sync
        def _(sp):
            sp.dma_start(x[:, :, :], A["x"].rearrange("(t p) d -> p t d", p=P)).then_inc(S_("x_in"), 16)
            sp.dma_start(cst[:, :, :], A["cst"][:, 0:6, :]).then_inc(S_("cst_in"), 16)
            for s in range(NS):
                sp.dma_start(ring[:, s, :], A["W"][s]).then_inc(S_(f"landed{s}"), 16)
            with sp.Fori(1, NCH // NS) as r:
                for s in range(NS):
                    sp.wait_ge(S_("chunk_used"), NS * (r - 1) + s + 1)
                    sp.dma_start(ring[:, s, :], A["W"][r * NS + s]).then_inc(S_(f"landed{s}"), 16)
            for i in range(NCH // NS * NS, NCH):
                sp.wait_ge(S_("chunk_used"), i - NS + 1)
                sp.dma_start(ring[:, i % NS, :], A["W"][i]).then_inc(S_(f"landed{i % NS}"), 16)
            for t in range(TT):
                sp.wait_ge(S_("final"), t + 1)
                sp.dma_start(out[t * P:(t + 1) * P, :], xn[:, t, :]).then_inc(S_("stored"), 16)
            sp.wait_ge(S_("stored"), 16 * TT)

        @block.gpsimd
        def _(pool):
            nc.gpsimd.memset(smallp[:, 31:32], -0.5).then_inc(S_("pool_step"), 1)
            pool_steps[0] += 1
            pool.wait_ge(S_("pool_step"), 1)

            def load_gain(i):
                if i >= 2:
                    pool.wait_ge(S_("out_gained"), TT * (i - 1))
                pool.dma_start(gains[:, i % 2, :], A["gains"][i:i + 1, :].to_broadcast([P, D])).then_inc(S_("gain"), 16)
                pool.wait_ge(S_("gain"), 16 * (i + 1))

            n_mix0.pool(pool)
            for i in range(2):
                pool.dma_start(gates[:, i, :], A["ada_gate_b"][i:i + 1, :].to_broadcast([P, D])).then_inc(S_("gate_bias_in"), 16)
            load_gain(0)
            load_gain(1)
            r_mix0.pool(pool)
            n_ffn0.pool(pool)
            load_gain(2)
            r_ffn0.pool(pool)
            n_mix1.pool(pool)
            load_gain(3)
            r_mix1.pool(pool)
            n_ffn1.pool(pool)
            load_gain(4)
            r_ffn1.pool(pool)
            n_ctx.pool(pool)
            n_lat.pool(pool)
            pool.wait_ge(S_("lengths"), 1)
            nc.gpsimd.tensor_tensor(rsq[:, 0:24], rsq[:, 0:24], smallp[:, 31:32].to_broadcast([P, 24]), ALU.pow).then_inc(S_("lengths_r"), 1)
            pool.wait_ge(S_("trans_v"), 10)
            pool.wait_ge(S_("dec"), 1)
            pool.wait_ge(S_("EX"), 1)

            def by_head(a):
                return a.unsqueeze(2).to_broadcast([P, H4, P])

            def decay_in(d, t, kind):
                c = 8 * kind + 4 * d
                mask = cst[:, C_LT if d else C_GT, :].unsqueeze(1).to_broadcast([P, H4, P])
                nc.gpsimd.tensor_tensor(gS[d], mask, by_head(dec[:, t, c:c + 4]), ALU.mult).then_inc(S_("gS"), 1)

            def decayed_keys(kind, step, d, dst, keys, sem):
                t = TILE_OF[d][step]
                c = 8 * kind + 4 * d
                factor = by_head(EX[:, C_LT if d else C_GT, t, c:c + 4])
                nc.gpsimd.tensor_tensor(dst[d], keys[:, t, :, :], factor, ALU.mult).then_inc(sem, 1)

            def heads_rstd(i, c, n):
                pool.wait_ge(S_("head_var"), i)
                nc.gpsimd.tensor_tensor(small[:, c:c + n], small[:, c:c + n], smallp[:, 31:32].to_broadcast([P, n]), ALU.pow).then_inc(S_("head_rstd"), 1)

            for n in range(2 * TT2 + 2):
                if n >= 2:
                    pool.wait_ge(S_("diff"), n - 1)
                decay_in(n % 2, n // 2 % TT2, n // (2 * TT2))
            for step in range(STEPS - 1):
                for d in DIRS:
                    if step:
                        pool.wait_ge(S_("rdS"), nth(step - 1, d))
                    decayed_keys(1, step, d, rkdec, rk, S_("rkdec"))
            for step in range(STEPS):
                if step >= 2:
                    for d in DIRS:
                        pool.wait_ge(S_("diff"), 2 * TT2 + (2 if step == 2 else 2 + later(step - 1, d)))
                        decay_in(d, TILE_OF[d][step], 0)
                if step < STEPS - 1:
                    for d in DIRS:
                        if step == 0:
                            pool.wait_ge(S_("rdS"), nth(STEPS - 2, d))
                        else:
                            pool.wait_ge(S_("dS"), nth(step - 1, d))
                        decayed_keys(0, step, d, kdec, kn, S_("kdec"))
                if step == 0:
                    heads_rstd(1, 168, 8)
            heads_rstd(2, 164, 4)
            heads_rstd(3, 160, 4)
            n_ffn2.pool(pool)
            rstd(pool, "last", 0, 26)

        @block.scalar
        def _(act):
            nc_a = nc.scalar
            act.dma_start(par[:, :], A["par"]).then_inc(S_("par_in"), 16)
            act.dma_start(onehot[0:BUCKETS, :, :], A["onehot"]).then_inc(S_("rel_in"), 16)
            act.dma_start(relb[0:BUCKETS, :], A["rel_bias"]).then_inc(S_("rel_in"), 16)
            act.dma_start(negm[0:HEADS, :, :], A["negm"]).then_inc(S_("neg_in"), 16)
            act.dma_start(sel[:, :], A["sel"]).then_inc(S_("sel_in"), 16)
            n_mix0.scalar_square(act)
            act.wait_ge(S_("par_in"), 16)
            nc_a.activation(small[:, 64:80], pcol("cond", 0, 16), ACT.Tanh, scale=0.5).then_inc(S_("cond_tanh"), 1)
            n_mix0.evacuate(act, 0)
            copies = GROUPS * WLEN
            act.wait_ge(S_("table"), 1)
            act.dma_start(table.ap(), wtab[0:HEADS, :, :].rearrange("h g n -> h (g n)").unsqueeze(1)
                          .to_broadcast([HEADS, P, copies])).then_inc(S_("table_out"), 16)

            for kind, a, g in ORDER:
                if kind in "VK":
                    for n in range(2):
                        unit = UNIT[(kind, a, g)] + n
                        if n == 0:
                            act.wait_ge(S_("proj"), unit // 2 + 1)
                        else:
                            chunk_done(act, (kind, a, g))
                        src = ps[:, unit % 3, :]
                        if kind == "V":
                            if a == 1:
                                act.wait_ge(S_("head_out"), 4)
                            dst = V[:, n, g, :, :].rearrange("p a b -> p (a b)")
                        else:
                            if a >= 2:
                                act.wait_ge(S_("scores"), 2 * a - 2)
                            dst = QKb[a % 2][:, g, 2 * n:2 * n + 2, :].rearrange("p a b -> p (a b)")
                        nc_a.activation(dst, src, ACT.Copy).then_inc(S_("proj_out"), 1)
                    if (kind, a, g) == ("V", 0, 2):
                        act.wait_ge(S_("table_out"), 16)
                        for h in range(HEADS):
                            skew = bass.AP(table, P - 1 + h * P * copies, [[copies - 1, P], [WLEN, GROUPS], [1, S]])
                            act.dma_start(bias[:, h, :, :], skew).then_inc(S_("bias_in"), 16)
                elif kind == "S":
                    act.wait_ge(S_("logits"), a + 1)
                    for t, c in ((1, slice(0, 256)), (0, slice(256, 384))):
                        last = nc_a.activation(L[a % 2][:, :, c], L[a % 2][:, :, c], ACT.Exp, bias=small[:, 80 + t:81 + t],
                                               accum_out=small[:, 82 + t:83 + t])
                        last.then_inc(S_("exps"), 1)
                elif kind == "T":
                    if a:
                        act.wait_ge(S_("head_out"), a)
                    for n, m in ((0, 4), (1, 4), (2, 1)):
                        act.wait_ge(S_("pT"), 3 * a + n + 1)
                        src = ps[:, 6 + n % 2, 0:m * P].rearrange("p (a b) -> p a b", a=m)
                        nc_a.activation(PT[:, 4 * n:4 * n + m, :], src, ACT.Copy).then_inc(S_("pT_out"), 1)
                else:
                    act.wait_ge(S_("head_out"), a + 1)
                    nc_a.activation(oT[:, a, :].rearrange("p (t q) -> p t q", t=2), ps[:, 7, 0:S].rearrange("p (t q) -> p t q", t=2), ACT.Copy).then_inc(S_("oT"), 1)

            def ada_rows(i):
                chunk_done(act, ("ada", i, 0))
                if i >= 2:
                    act.wait_ge(S_("ada_t"), i - 1)
                nc_a.activation(row[:, i % 2, :], ps[0:2, 5 + i % 2, :], ACT.Copy).then_inc(S_("ada_row_out"), 1)

            def gated_ffn(layer, up):
                for j in range(12):
                    up.done(act, j)
                    if j >= 2:
                        act.wait_ge(S_("aT"), 12 * layer + j - 1)
                    for n in range(4):
                        ft = 2 * j + n % 2 + FT * (n // 2)
                        src = ps[:, 4 + 2 * (j % 2) + n // 2, (n % 2) * S:(n % 2 + 1) * S]
                        last = nc_a.activation(u[j % 2][:, n, :], src, ACT.Identity,
                                               scale=pcol("ffn_conv_w", (layer * 3 + 2) * 48 + ft), bias=pcol("ffn_conv_b", layer * 48 + ft))
                    last.then_inc(S_("tap"), 1)
                    high_parts(act, up.upto(j) + 1)
                    act.wait_ge(S_("conv"), 12 * layer + j + 1)
                    nc_a.activation(gl[j % 2][:, :, :], u[j % 2][:, 0:2, :], ACT.Gelu_apprx_tanh).then_inc(S_("gelu"), 1)
                    high_parts(act, up.upto(j + 1))

            p_mix0.scalar(act)
            r_mix0.scalar(act)
            for i in range(0, 3):
                ada_rows(i)
            n_ffn0.scalar_square(act)
            high_parts(act, up_ffn0.upto(-1))
            n_ffn0.evacuate(act, 0)
            high_parts(act, up_ffn0.upto(0))
            act.dma_start(lgw[:, :, :, :, :], A["gate_w"]).then_inc(S_("gate_w_in"), 16)
            act.wait_ge(S_("lam_abs"), 1)
            nc_a.activation(tmpc[:, 0:8], tmpc[:, 0:8], ACT.Exp).then_inc(S_("lam_exp"), 1)
            gated_ffn(0, up_ffn0)
            p_ffn0.scalar(act)
            r_ffn0.scalar(act)
            for i in range(3, 6):
                ada_rows(i)
            n_mix1.scalar_square(act)
            n_mix1.evacuate(act, 0)

            act.wait_ge(S_("lru_consts"), 1)

            def lru_taps(i):
                chunk_done(act, ("lin", i, 0))
                for n in range(2):
                    ft = 2 * i + n
                    nc_a.activation(xc[:, ft, :], ps[:, 4 + 2 * (i % 2), n * S:(n + 1) * S], ACT.Identity,
                                    scale=pcol("lru_conv_w", 24 + ft), bias=pcol("lru_conv_b", ft)).then_inc(S_("lru_tap"), 1)
                nc_a.activation(gb[:, 2 * i:2 * i + 2, :].rearrange("p a b -> p (a b)"), ps[:, 5 + 2 * (i % 2), :], ACT.Copy).then_inc(S_("lru_gb"), 1)

            def lru_gates(i):
                act.wait_ge(S_("lgate"), i + 1)
                for n in range(2):
                    ft = 2 * i + n
                    nc_a.activation(tr[:, ft, :], ps[:, 2 * (i % 2), n * S:(n + 1) * S], ACT.Tanh, scale=0.5, bias=small[:, 112 + ft:113 + ft])
                    nc_a.activation(ti[:, ft, :], ps[:, 2 * (i % 2) + 1, n * S:(n + 1) * S], ACT.Tanh, scale=0.5, bias=small[:, 120 + ft:121 + ft]).then_inc(S_("lru_tanh"), 1)
                for n in range(2):
                    ft = 2 * i + n
                    act.wait_ge(S_("lru_tanh"), ft + 1)
                    nc_a.activation(av[:, ft, :], tr[:, ft, :], ACT.Exp, scale=small[:, 128 + ft:129 + ft], bias=small[:, 128 + ft:129 + ft])
                    nc_a.activation(th[:, ft, :], tr[:, ft, :], ACT.Tanh, scale=small[:, 136 + ft:137 + ft], bias=small[:, 136 + ft:137 + ft]).then_inc(S_("lru_exp"), 1)

            lru_taps(0)
            for i in range(1, 4):
                lru_taps(i)
                lru_gates(i - 1)
            lru_gates(3)
            for i in range(4):
                b2 = slice(2 * i, 2 * i + 2)
                nc_a.activation(gb[:, b2, :], gb[:, b2, :], ACT.Gelu_apprx_tanh).then_inc(S_("lru_gelu"), 1)
            for i in range(4):
                b2 = slice(2 * i, 2 * i + 2)
                act.wait_ge(S_("lru_sq"), i + 1)
                nc_a.activation(mu[:, b2, :], mu[:, b2, :], ACT.Sqrt).then_inc(S_("lru_mult"), 1)

            p_mix1.scalar(act)
            r_mix1.scalar(act)
            for i in range(6, 9):
                ada_rows(i)
            n_ffn1.scalar_square(act)
            high_parts(act, up_ffn1.upto(-1))
            n_ffn1.evacuate(act, 0)
            high_parts(act, up_ffn1.upto(0))
            gated_ffn(1, up_ffn1)
            p_ffn1.scalar(act)
            r_ffn1.scalar(act)
            act.dma_start(ctxx[:, :, :], A["ctx"].rearrange("(t p) d -> p t d", p=P)).then_inc(S_("ctx_in"), 16)
            act.dma_start(rope[:, :, :, :], A["rope"]).then_inc(S_("rope_in"), 16)
            act.dma_start(lvl[:, :, :], A["cst"][:, 6:, :]).then_inc(S_("lvl_in"), 16)
            act.dma_start(wab[:, :, :], A["wab"]).then_inc(S_("wab_in"), 16)
            act.dma_start(normg2[:, :, :], A["normg2"].unsqueeze(0).to_broadcast([P, 2, P])).then_inc(S_("normg2_in"), 16)
            act.dma_start(absc[:, 7, 0:24], A["head_vec"].to_broadcast([P, 24])).then_inc(S_("headv_in"), 16)
            n_ctx.scalar_square(act)
            for i in range(9, 12):
                ada_rows(i)
            n_ctx.evacuate(act, 0)
            n_lat.scalar_square(act)
            n_lat.evacuate(act, 0)

            def conv_taps(n):
                if n % 4 < 3:
                    act.wait_ge(S_("qkv"), n // 4 * 3 + n % 4 + 1)
                else:
                    chunk_done(act, ("win", n // 4, 0))
                if n >= 2:
                    act.wait_ge(S_("qkv_silu"), n - 1)
                w = S if n < H4 else 2 * S
                nc_a.activation(cu[n % 2][:, 0:w], ps[:, n % 8, 0:w], ACT.Identity, scale=hw2[:, 2 * 12 + n:2 * 12 + n + 1]).then_inc(S_("qkv_tap"), 1)

            def conv_tanh(n):
                w = S if n < H4 else 2 * S
                act.wait_ge(S_("qkv_conv"), n + 1)
                nc_a.activation(ct[n % 2][:, 0:w], cu[n % 2][:, 0:w], ACT.Tanh).then_inc(S_("qkv_tanh"), 1)

            act.wait_ge(S_("half_w"), 1)
            for n in range(12):
                conv_taps(n)
                conv_tanh(n)
            for n, (what, t) in enumerate(TOKU):
                unit_done(act, n)
                src = ps[:, (12 + n) % 8, :]
                if what in ("z", "rg"):
                    dst = (zt if what == "z" else rgt)[:, t - TT, :]
                    nc_a.activation(dst, src, ACT.Tanh, scale=0.5).then_inc(S_("tok_act"), 1)
                elif what == "rv":
                    nc_a.activation(rv[:, t, :, :].rearrange("p a b -> p (a b)"), src, ACT.Copy).then_inc(S_("tok_act"), 1)
            act.wait_ge(S_("ab"), 1)
            act.wait_ge(S_("headv_in"), 16)
            nc_a.activation(beta[:, :, :], AB[:, :, 8:16], ACT.Tanh, scale=0.5).then_inc(S_("beta_tanh"), 1)
            nc_a.activation(absc[:, 6, 0:8], absc[:, 7, 0:8], ACT.Exp).then_inc(S_("a_exp"), 1)
            act.wait_ge(S_("sp_in"), 1)
            nc_a.activation(absc[:, 1, 0:40], absc[:, 1, 0:40], ACT.Exp).then_inc(S_("sp_exp"), 1)
            act.wait_ge(S_("qkv_silu"), 12)
            nc_a.activation(sqk[:, 0:1024], qT.rearrange("p a b -> p (a b)"), ACT.Square)
            nc_a.activation(sqk[:, 1024:3072], kT.rearrange("p a b -> p (a b)"), ACT.Square).then_inc(S_("qk_sq"), 1)
            act.wait_ge(S_("sums"), 1)
            nc_a.activation(EX[:, :, :, :].rearrange("p a b c -> p (a b c)"), ps[:, 0, 0:320], ACT.Exp).then_inc(S_("EX"), 1)

            for n in range(len(TRANS)):
                what, t = TRANS[n]
                if what in ("rqT", "rkT", "knT", "qnT"):
                    act.wait_ge(S_("trans"), n + 1)
                    dst = {"rqT": rqT, "rkT": rkT, "knT": kT, "qnT": qT}[what]
                    tt = t - TT if what in ("rqT", "qnT") else t
                    sc = HD_SCALE if what in ("rqT", "qnT") else 1.0
                    nc_a.activation(dst[:, :, tt * P:(tt + 1) * P], TB(n), ACT.Copy, scale=sc).then_inc(S_("trans_a"), 1)

            def store_matrix(n):
                t, d = divmod(n, 2)
                act.wait_ge(S_("A"), n + 1)
                act.dma_start(matrices.ap()[d, :, t, :, :], Am[4 * d + t]).then_inc(S_("matrices_out"), 16)

            for n in range(2 * TT2):
                act.wait_ge(S_("diff"), n + 1)
                if n >= 2:
                    act.wait_ge(S_("A"), n - 1)
                nc_a.activation(E[n % 2], B4(n % 2), ACT.Exp).then_inc(S_("decay"), 1)
                if n >= 2:
                    store_matrix(n - 2)
            for d in DIRS:
                act.wait_ge(S_("diff"), 2 * TT2 + d + 1)
                nc_a.activation(rET[d], B4(4 + d), ACT.Exp).then_inc(S_("decay"), 1)
            store_matrix(2 * TT2 - 2)
            store_matrix(2 * TT2 - 1)
            act.wait_ge(S_("matrices_out"), 16 * 2 * TT2)
            row_words = TT2 * H4 * P
            for b in range(NB):
                for d in DIRS:
                    source = bass.AP(matrices, (d * P + b * BLK) * row_words + b * BLK, [[P, TT2 * H4], [row_words, BLK], [1, BLK]])
                    act.dma_start(blocks[b * BLK:(b + 1) * BLK, d, :, :], source).then_inc(S_("blocks_in"), 16)
            act.wait_ge(S_("inverses"), 1)
            act.dma_start(block_inverses.ap().rearrange("b n d i j -> (b n) d i j"), inverses[:, :, :, :]).then_inc(S_("inverses_out"), 16)
            act.wait_ge(S_("inverses_out"), 16)
            for b in range(NB):
                for d in DIRS:
                    act.dma_start(inverse_rows[b * BLK:(b + 1) * BLK, d, :, :],
                                  block_inverses.ap()[b, :, d, :, :].rearrange("n i j -> i n j")).then_inc(S_("inverse_rows_in"), 16)
            def head_squares(kind, t):
                for h in range(H4):
                    c = 144 + 8 * kind + 4 * t + h
                    nc_a.activation(E[t][:, h, :], y2[kind][:, t, h, :], ACT.Square, accum_out=small[:, c:c + 1]).then_inc(S_("head_sq"), 1)

            for step in range(STEPS):
                for d in DIRS:
                    act.wait_ge(S_("X_turned"), nth(step, d))
                    nc_a.activation(XT[d], B4(4 * d), ACT.Copy).then_inc(S_("XT_in"), 1)
                if step == 0:
                    act.wait_ge(S_("centred"), 1)
                    for t in range(TT):
                        head_squares(1, t)
                if step >= 2:
                    for d in DIRS:
                        act.wait_ge(S_("diff"), 2 * TT2 + 2 + later(step, d))
                        if step > 2:
                            act.wait_ge(S_("o"), later(step - 1, d))
                        nc_a.activation(ET[d], B4(4 * d + 3), ACT.Exp).then_inc(S_("decay"), 1)
                if step:
                    for d in DIRS:
                        act.wait_ge(S_("wT"), nth(step - 1, d))
                        nc_a.activation(wT[d], B4(4 * d), ACT.Copy, scale=-1.0).then_inc(S_("wT_out"), 1)
                for d in DIRS:
                    act.wait_ge(S_("vnew"), nth(step, d))
                    nc_a.activation(vnew[d], B4(4 * d + 1), ACT.Copy).then_inc(S_("vnew_out"), 1)

            for i, t in enumerate((1, 0)):
                act.wait_ge(S_("o_out"), 7 + i)
                head_squares(0, t)
            for bank, k in ((5, 4), (7, 6), (4, 0)):
                act.wait_ge(S_("yT"), {4: 1, 6: 2, 0: 3}[k])
                nc_a.activation(yT[:, k:k + 2, :].rearrange("p a b -> p (a b)"), ps[:, bank, :], ACT.Copy).then_inc(S_("yT_a"), 1)
            n_ffn2.scalar_square(act)
            high_parts(act, up_ffn2.upto(-1))
            n_ffn2.evacuate(act, 0)
            high_parts(act, up_ffn2.upto(0))
            for j in range(11):
                up_ffn2.done(act, j)
                if j >= 2:
                    act.wait_ge(S_("aT2"), j - 1)
                nc_a.activation(gl[j % 2].rearrange("p a b -> p (a b)"), ps[:, 4 + 2 * (j % 2), :], ACT.Tanh, scale=0.5).then_inc(S_("tanh2"), 1)
                high_parts(act, up_ffn2.upto(j + 1))
            p_ffn2.scalar(act)
            for t in range(TT):
                r_ffn2.x_ready(act, t)
                nc_a.activation(xn[:, t, :], x[:, t, :], ACT.Square, accum_out=small[:, 26 + t:27 + t]).then_inc(S_("last_squared"), 1)

        @block.vector
        def _(dve):
            v = nc.vector
            steps = [0]

            def link(ins):
                steps[0] += 1
                ins.then_inc(S_("vector_step"), 1)
                dve.wait_ge(S_("vector_step"), steps[0])

            n_mix0.vector_scale(dve)
            dve.wait_ge(S_("cond_tanh"), 1)
            link(v.scalar_tensor_tensor(small[:, 64:80], small[:, 64:80], 1.0, pcol("cond", 0, 16), ALU.add, ALU.mult))
            v.tensor_scalar(small[:, 64:80], small[:, 64:80], 0.5, None, ALU.mult).then_inc(S_("cond"), 1)
            n_mix0.evacuate(dve, 1)
            dve.wait_ge(S_("neg_in"), 16)
            dve.wait_ge(S_("tables"), 1)
            v.tensor_tensor(wtab[0:HEADS, :, :], ps[0:HEADS, 0:3, 0:WLEN], negm[0:HEADS, :, :], ALU.add).then_inc(S_("table"), 1)
            for kind, h, _ in ORDER:
                if kind == "S":
                    Lh = L[h % 2]
                    if h == 0:
                        dve.wait_ge(S_("bias_in"), 16 * HEADS)
                    dve.wait_ge(S_("scores"), h + 1)
                    if h >= 2:
                        dve.wait_ge(S_("pT"), 3 * (h - 1))
                    v.scalar_tensor_tensor(Lh[:, :, 0:256], ps[:, 3:6, 0:256], HD_SCALE, bias[:, h, :, :], ALU.mult, ALU.add)
                    link(v.scalar_tensor_tensor(Lh[:, :, 256:384], ps[:, 3:6, 256:384], HD_SCALE, bias[:, h, :, 128:256], ALU.mult, ALU.add))
                    if h:
                        dve.wait_ge(S_("exps"), 2 * h)
                    v.tensor_reduce(small[:, 81:82], Lh[:, :, 0:256], AX.XY, ALU.max, negate=True)
                    v.tensor_reduce(small[:, 80:81], Lh[:, :, 256:384], AX.XY, ALU.max, negate=True).then_inc(S_("logits"), 1)
                    dve.wait_ge(S_("exps"), 2 * h + 2)
                    link(v.reciprocal(small[:, 84:86], small[:, 82:84]))
                    v.tensor_scalar(Lh[:, :, 0:256], Lh[:, :, 0:256], small[:, 85:86], None, ALU.mult)
                    v.tensor_scalar(Lh[:, :, 256:384], Lh[:, :, 256:384], small[:, 84:85], None, ALU.mult).then_inc(S_("probs"), 1)

            def ada_out(i):
                dve.wait_ge(S_("ada_t"), i + 1)
                if i // 2 in (2, 5):
                    dve.wait_ge(S_("gate_bias_in"), 32)
                    gg = gates[:, (i // 2) // 3, (i % 2) * 512:(i % 2 + 1) * 512]
                    v.tensor_tensor(gg, gg, ps[:, 7, :], ALU.add).then_inc(S_("ada_out"), 1)
                else:
                    v.tensor_tensor(modT[:, 4 * i:4 * i + 4, :], ps[:, 7, 0:8].rearrange("p (a b) -> p a b", a=4),
                                    pcol("ada_b", 4 * i, 4).unsqueeze(2).to_broadcast([P, 4, 2]), ALU.add).then_inc(S_("ada_out"), 1)

            def gated_ffn(layer, up):
                for j in range(12):
                    dve.wait_ge(S_("tap"), 12 * layer + j + 1)
                    for tap, sh in ((1, 1), (0, 2)):
                        for n in range(4):
                            ft = 2 * j + n % 2 + FT * (n // 2)
                            src = ps[:, 4 + 2 * (j % 2) + n // 2, (n % 2) * S:(n % 2 + 1) * S - sh]
                            dst = u[j % 2][:, n, sh:S]
                            last = v.scalar_tensor_tensor(dst, src, pcol("ffn_conv_w", (layer * 3 + tap) * 48 + ft), dst, ALU.mult, ALU.add)
                        if tap:
                            link(last)
                    last.then_inc(S_("conv"), 1)
                    low_parts(dve, up.upto(j) + 1)
                    dve.wait_ge(S_("gelu"), 12 * layer + j + 1)
                    v.tensor_tensor(aT[:, 2 * j:2 * j + 2, :], gl[j % 2][:, :, :], u[j % 2][:, 2:4, :], ALU.mult).then_inc(S_("aT"), 1)
                    low_parts(dve, up.upto(j + 1))

            def log1p_exp_neg(e, w, w2, acc, n):
                link(v.tensor_scalar(w, e, 2.0, None, ALU.add))
                link(v.reciprocal(w, w))
                link(v.tensor_tensor(w, w, e, ALU.mult))
                link(v.tensor_tensor(w2, w, w, ALU.mult))
                link(v.tensor_scalar(acc, w2, 2.0 / 15, 2.0 / 13, ALU.mult, ALU.add))
                for c in (11, 9, 7, 5, 3, 1):
                    link(v.tensor_tensor(acc, acc, w2, ALU.mult))
                    link(v.tensor_scalar(acc, acc, 2.0 / c, None, ALU.add))
                link(v.tensor_tensor(acc, acc, w, ALU.mult))

            p_mix0.vector(dve)
            r_mix0.vector(dve)
            for i in range(0, 3):
                ada_out(i)
            n_ffn0.vector_scale(dve)
            low_parts(dve, up_ffn0.upto(-1))
            n_ffn0.evacuate(dve, 1)
            low_parts(dve, up_ffn0.upto(0))
            dve.wait_ge(S_("par_in"), 16)
            v.tensor_scalar(small[:, 112:128], pcol("ga_b", 0, 16), 0.5, None, ALU.mult)
            lam = pcol("lam", 0, 8)
            link(v.tensor_scalar(tmpc[:, 0:8], lam, -1.0, None, ALU.mult))
            v.tensor_tensor(tmpc[:, 0:8], tmpc[:, 0:8], lam, ALU.min).then_inc(S_("lam_abs"), 1)
            dve.wait_ge(S_("lam_exp"), 1)
            log1p_exp_neg(tmpc[:, 0:8], tmpc[:, 8:16], tmpc[:, 16:24], tmpc[:, 24:32], 8)
            link(v.tensor_scalar(tmpc[:, 0:8], lam, 0.0, None, ALU.min))
            link(v.tensor_tensor(tmpc[:, 0:8], tmpc[:, 0:8], tmpc[:, 24:32], ALU.subtract))
            v.tensor_scalar(small[:, 128:136], tmpc[:, 0:8], 4.0, None, ALU.mult)
            v.tensor_scalar(small[:, 136:144], tmpc[:, 0:8], -4.0, None, ALU.mult).then_inc(S_("lru_consts"), 1)
            gated_ffn(0, up_ffn0)
            p_ffn0.vector(dve)
            r_ffn0.vector(dve)
            for i in range(3, 6):
                ada_out(i)
            n_mix1.vector_scale(dve)
            n_mix1.evacuate(dve, 1)

            def lru_conv(i):
                dve.wait_ge(S_("lru_tap"), 2 * i + 2)
                for sh in (1, 2, 3):
                    for n in range(2):
                        ft = 2 * i + n
                        dst = xc[:, ft, sh:S]
                        src = ps[:, 4 + 2 * (i % 2), n * S:(n + 1) * S - sh]
                        last = v.scalar_tensor_tensor(dst, src, pcol("lru_conv_w", (3 - sh) * 8 + ft), dst, ALU.mult, ALU.add)
                    if sh < 3:
                        link(last)
                last.then_inc(S_("lru_xc"), 1)

            def lru_in(i):
                b2 = slice(2 * i, 2 * i + 2)
                dve.wait_ge(S_("lru_exp"), 2 * i + 2)
                link(v.tensor_tensor(mu[:, b2, :], av[:, b2, :], av[:, b2, :], ALU.mult))
                last = v.scalar_tensor_tensor(mu[:, b2, :], mu[:, b2, :], 1.0, th[:, b2, :], ALU.add, ALU.mult)
                last.then_inc(S_("lru_sq"), 1)
                link(v.scalar_tensor_tensor(ti[:, b2, :], ti[:, b2, :], 1.0, xc[:, b2, :], ALU.add, ALU.mult))

            lru_conv(0)
            for i in range(1, 4):
                lru_conv(i)
                lru_in(i - 1)
            lru_in(3)
            for i in range(4):
                b2 = slice(2 * i, 2 * i + 2)
                dve.wait_ge(S_("lru_mult"), i + 1)
                link(v.scalar_tensor_tensor(ti[:, b2, :], ti[:, b2, :], 0.5, mu[:, b2, :], ALU.mult, ALU.mult))
                for ft in (2 * i, 2 * i + 1):
                    last = v.tensor_tensor_scan(th[:, ft, :], av[:, ft, :], ti[:, ft, :], 0.0, ALU.mult, ALU.add)
                link(last)
                dve.wait_ge(S_("lru_gelu"), i + 1)
                v.tensor_tensor(lT[:, b2, :], th[:, b2, :], gb[:, b2, :], ALU.mult).then_inc(S_("lT"), 1)
                if i:
                    low_parts(dve, p_mix1.first + 2 * i)

            p_mix1.vector(dve)
            r_mix1.vector(dve)
            for i in range(6, 9):
                ada_out(i)
            n_ffn1.vector_scale(dve)
            low_parts(dve, up_ffn1.upto(-1))
            n_ffn1.evacuate(dve, 1)
            low_parts(dve, up_ffn1.upto(0))
            gated_ffn(1, up_ffn1)
            p_ffn1.vector(dve)
            r_ffn1.vector(dve)
            n_ctx.vector_scale(dve)
            for i in range(9, 12):
                ada_out(i)
            for at, name, blk, which in ((0, "mix_g2", 8, 0), (8, "mix_g2", 8, 1), (16, "ffn_g2", 32, 0)):
                v.scalar_tensor_tensor(modc[:, at:at + 8], modT[:, blk:blk + 8, which:which + 1].rearrange("p a b -> p (a b)"),
                                       1.0, pcol(name, 0, 8), ALU.add, ALU.mult).then_inc(S_("modc"), 1)
            v.tensor_scalar(hw2[:, :], pcol("conv_w2", 0, 60), 0.5, None, ALU.mult).then_inc(S_("half_w"), 1)
            dve.wait_ge(S_("modc"), 3)
            dve.wait_ge(S_("half_w"), 1)
            n_ctx.evacuate(dve, 1)
            n_lat.vector_scale(dve)
            n_lat.evacuate(dve, 1)

            for n in range(12):
                dve.wait_ge(S_("qkv_tap"), n + 1)
                segs = 1 if n < H4 else 2
                src3 = ps[:, n % 8, 0:segs * S].rearrange("p (a b) -> p a b", a=segs)
                dst3 = cu[n % 2][:, 0:segs * S].rearrange("p (a b) -> p a b", a=segs)
                for tap in (0, 1, 3, 4):
                    d = tap - 2
                    if d < 0:
                        o_, i_ = dst3[:, :, -d:S], src3[:, :, 0:S + d]
                    else:
                        o_, i_ = dst3[:, :, 0:S - d], src3[:, :, d:S]
                    last = v.scalar_tensor_tensor(o_, i_, hw2[:, tap * 12 + n:tap * 12 + n + 1], o_, ALU.mult, ALU.add)
                    if tap < 4:
                        link(last)
                last.then_inc(S_("qkv_conv"), 1)
                dve.wait_ge(S_("qkv_tanh"), n + 1)
                w = segs * S
                dst = (qT[:, n, :] if n < 4 else kT[:, n - 4, :] if n < 8 else vT[:, n - 8, :])
                v.scalar_tensor_tensor(dst, ct[n % 2][:, 0:w], 1.0, cu[n % 2][:, 0:w], ALU.add, ALU.mult).then_inc(S_("qkv_silu"), 1)

            dve.wait_ge(S_("rope_in"), 16)
            for n, (what, t) in enumerate(TOKU):
                src = ps[:, (12 + n) % 8, :]
                s3 = src.rearrange("p (h d) -> p h d", h=H4)
                if what in ("z", "rg"):
                    dst = (zt if what == "z" else rgt)[:, t - TT, :]
                    dve.wait_ge(S_("tok_act"), TOKA[n] + 1)
                    v.scalar_tensor_tensor(dst, dst, 1.0, src, ALU.add, ALU.mult).then_inc(S_("tok_v"), 1)
                elif what in ("rq", "rk"):
                    unit_done(dve, n)
                    dst = rq[:, t - TT, :, :] if what == "rq" else rk[:, t, :, :]
                    cosb = rope[:, t, 0:1, :].to_broadcast([P, H4, P])
                    v.tensor_tensor(dst, s3, cosb, ALU.mult)
                    v.tensor_tensor(tmpr[:, :, 0:64], s3[:, :, 64:128], rope[:, t, 1:2, 0:64].to_broadcast([P, H4, 64]), ALU.mult)
                    link(v.tensor_tensor(tmpr[:, :, 64:128], s3[:, :, 0:64], rope[:, t, 1:2, 64:128].to_broadcast([P, H4, 64]), ALU.mult))
                    v.tensor_tensor(dst, dst, tmpr[:, :, :], ALU.add).then_inc(S_("tok_v"), 1)
                    dve.wait_ge(S_("tok_v"), TOKV[n] + 1)
            dve.wait_ge(S_("beta_tanh"), 1)
            dve.wait_ge(S_("headv_in"), 16)
            z0, z1, z2, z3, z4 = (absc[:, i, 0:40] for i in range(5))
            v.tensor_tensor(absc[:, 0, 0:32].rearrange("p (a b) -> p a b", a=TT2), AB[:, :, 0:8],
                            absc[:, 7:8, 8:16].to_broadcast([P, TT2, 8]), ALU.add)
            link(v.tensor_scalar(absc[:, 0, 32:40], absc[:, 7, 16:24], -1.0, None, ALU.mult))
            link(v.tensor_scalar(z1, z0, -1.0, None, ALU.mult))
            v.tensor_tensor(z1, z1, z0, ALU.min).then_inc(S_("sp_in"), 1)
            dve.wait_ge(S_("sp_exp"), 1)
            log1p_exp_neg(z1, z2, z3, z4, 40)
            link(v.tensor_scalar(z0, z0, 0.0, None, ALU.max))
            link(v.tensor_tensor(z0, z0, z4, ALU.add))
            link(v.tensor_scalar(z0, z0, -1.0, None, ALU.mult))
            dve.wait_ge(S_("a_exp"), 1)
            v.tensor_tensor(dec[:, :, 0:8], absc[:, 0, 0:32].rearrange("p (a b) -> p a b", a=TT2),
                            absc[:, 6:7, 0:8].to_broadcast([P, TT2, 8]), ALU.mult)
            v.tensor_copy(dec[:, :, 8:16], absc[:, 0:1, 32:40].to_broadcast([P, TT2, 8])).then_inc(S_("dec"), 1)
            dve.wait_ge(S_("beta_tanh"), 1)
            v.tensor_scalar(beta[:, :, :], beta[:, :, :], 0.5, 0.5, ALU.mult, ALU.add).then_inc(S_("beta"), 1)
            dve.wait_ge(S_("lens"), 1)
            v.tensor_scalar(rsq[:, 0:24], ps[:, 1, 0:24], EPS, None, ALU.add).then_inc(S_("lengths"), 1)
            dve.wait_ge(S_("lengths_r"), 1)
            for n in range(len(TRANS)):
                what, t = TRANS[n]
                if what in ("v", "kn", "qn"):
                    dve.wait_ge(S_("trans"), n + 1)
                    if what == "v":
                        v.tensor_copy(v_t[:, t, :, :], TB(n)).then_inc(S_("trans_v"), 1)
                    else:
                        c = 8 + t * 4 if what == "kn" else (t - TT) * 4
                        dst = kn[:, t, :, :] if what == "kn" else qn[:, t - TT, :, :]
                        v.tensor_tensor(dst, TB(n), rsq[:, c:c + 4].unsqueeze(2).to_broadcast([P, H4, P]), ALU.mult).then_inc(S_("trans_v"), 1)

            dve.wait_ge(S_("trans_v"), 10)
            dve.wait_ge(S_("EX"), 1)
            dve.wait_ge(S_("beta"), 1)
            dve.wait_ge(S_("lvl_in"), 16)

            def bc(a):
                return a.unsqueeze(2).to_broadcast([P, H4, P])

            def bh(a):
                return a.unsqueeze(1).to_broadcast([P, H4, P])

            def output_part(kind, step, d, inter, inner):
                t = TILE_OF[d][step]
                c = 8 * kind + 4 * d
                o_ = y2[kind][:, t - TT, :, :]
                done = 4 * (kind == 0) + later(step, d)
                if step == 2:
                    link(v.tensor_copy(o_, B4(inner)))
                else:
                    dve.wait_ge(S_("o_out"), done - 1)
                    link(v.tensor_tensor(o_, o_, B4(inner), ALU.add))
                for h in range(H4):
                    last = v.scalar_tensor_tensor(o_[:, h, :], ps[:, inter, h * P:(h + 1) * P],
                                                  EX[:, C_GE if d else C_LE, t, c + h:c + h + 1], o_[:, h, :], ALU.mult, ALU.add)
                last.then_inc(S_("o_out"), 1)

            def update_state(state, kind, step, d, b, sem):
                t = TILE_OF[d][step]
                c = 8 * kind + 4 * d
                if step == 0:
                    v.tensor_copy(state, B4(b)).then_inc(sem, 1)
                else:
                    for h in range(H4):
                        last = v.scalar_tensor_tensor(state[:, h, :], state[:, h, :], EX[:, C_ONE, t, c + h:c + h + 1],
                                                      ps[:, b, h * P:(h + 1) * P], ALU.mult, ALU.add)
                    last.then_inc(sem, 1)

            for n in range(2 * TT2):
                t, d = divmod(n, 2)
                dve.wait_ge(S_("decay"), n + 1)
                dve.wait_ge(S_("kk"), t + 1)
                for h in range(H4):
                    last = v.scalar_tensor_tensor(Am[4 * d + t][:, h, :], ps[:, 2 + t % 2, h * P:(h + 1) * P],
                                                  beta[:, t, 4 * d + h:4 * d + h + 1], E[d][:, h, :], ALU.mult, ALU.mult)
                last.then_inc(S_("A"), 1)
            for d in DIRS:
                dve.wait_ge(S_("decay"), 2 * TT2 + d + 1)
                link(v.tensor_tensor(rET[d], rET[d], bh(cst[:, C_GE if d else C_LE, :]), ALU.mult))
            def invert_blocks():
                dve.wait_ge(S_("blocks_in"), 16 * 2 * NB)
                for i in range(1, BLK):
                    for d in DIRS:
                        done = slice(BLK - i, BLK) if d else slice(0, i)
                        r = BLK - 1 - i if d else i
                        prod = block_tmp[:, d, 0:i * i].rearrange("p (c j) -> p c j", c=i)
                        last = v.tensor_tensor(prod, inverses[:, d, done, done].rearrange("p j c -> p c j"),
                                               blocks[:, d, r, done].unsqueeze(1).to_broadcast([P, i, i]), ALU.mult)
                    link(last)
                    for d in DIRS:
                        done = slice(BLK - i, BLK) if d else slice(0, i)
                        r = BLK - 1 - i if d else i
                        last = v.tensor_reduce(inverses[:, d, r, done], block_tmp[:, d, 0:i * i].rearrange("p (c j) -> p c j", c=i),
                                               AX.X, ALU.add, negate=True)
                    if i < BLK - 1:
                        link(last)
                last.then_inc(S_("inverses"), 1)

            def expand(step, d):
                t = TILE_OF[d][step]
                rows = inverse_rows[:, d, H4 * t:H4 * (t + 1), :].unsqueeze(2).to_broadcast([P, H4, NB, BLK])
                mask = lvl[:, 2 * LEVELS, :].rearrange("p (b j) -> p b j", b=NB).unsqueeze(1).to_broadcast([P, H4, NB, BLK])
                v.tensor_tensor(X[d].rearrange("p h (b j) -> p h b j", b=NB), rows, mask, ALU.mult).then_inc(S_("X_in"), 1)

            link(v.memset(inverses[:, :, :, :], 0.0))
            for d in DIRS:
                diagonal = inverses[:, d, :, :].rearrange("p i j -> p (i j)")[:, 0:BLK * BLK:BLK + 1]
                last = v.memset(diagonal, 1.0)
            link(last)
            for step in range(STEPS):
                if step == 2:
                    invert_blocks()
                if step >= 2:
                    for d in DIRS:
                        if step > 2:
                            dve.wait_ge(S_("ro"), later(step - 1, d))
                        dve.wait_ge(S_("rqk"), later(step, d))
                        v.tensor_tensor(rPm[d], B4(4 * d), rET[d], ALU.mult).then_inc(S_("rPm"), 1)
                if step < 3:
                    for d in DIRS:
                        dve.wait_ge(S_("rdS"), nth(step, d))
                        update_state(rSt[d], 1, step, d, 4 * d + 3, S_("rstate"))
                if step >= 2:
                    for d in DIRS:
                        dve.wait_ge(S_("ro"), later(step, d))
                        output_part(1, step, d, 4 * d + 1, 4 * d + 2)
            def retention_centre():
                for t in range(TT):
                    dve.wait_ge(S_("o_out"), 4)
                    last = v.tensor_reduce(tmpc[:, 8 + 4 * t:12 + 4 * t], y2[1][:, t, :, :], AX.X, ALU.add)
                link(last)
                link(v.tensor_scalar(tmpc[:, 0:8], tmpc[:, 8:16], 1.0 / P, None, ALU.mult))
                for t in range(TT):
                    last = v.tensor_tensor(y2[1][:, t, :, :], y2[1][:, t, :, :], bc(tmpc[:, 4 * t:4 * t + 4]), ALU.subtract)
                last.then_inc(S_("centred"), 1)

            def retention_variance():
                dve.wait_ge(S_("head_sq"), 8)
                v.tensor_scalar(small[:, 168:176], small[:, 152:160], 1.0 / P, EPS, ALU.mult, ALU.add).then_inc(S_("head_var"), 1)

            def retention_norm(t):
                dve.wait_ge(S_("head_rstd"), 1)
                dve.wait_ge(S_("normg2_in"), 16)
                y = y2[1][:, t, :, :]
                link(v.tensor_tensor(y, y, bc(small[:, 168 + 4 * t:172 + 4 * t]), ALU.mult))
                link(v.tensor_tensor(y, y, normg2[:, 1:2, :].to_broadcast([P, H4, P]), ALU.mult))
                v.scalar_tensor_tensor(y, y, 0.5, rgt[:, t, :].rearrange("p (a b) -> p a b", a=H4), ALU.mult, ALU.mult).then_inc(S_("mixed"), 1)

            def delta_gates(t):
                dve.wait_ge(S_("normg2_in"), 16)
                z = zt[:, t, :].rearrange("p (a b) -> p a b", a=H4)
                link(v.scalar_tensor_tensor(z, z, 0.5, normg2[:, 0:1, :].to_broadcast([P, H4, P]), ALU.mult, ALU.mult))

            beside = {(0, 0): retention_centre, (0, 2): retention_variance,
                      (1, 1): lambda: retention_norm(0), (1, 2): lambda: retention_norm(1),
                      (2, 0): lambda: delta_gates(0), (2, 2): lambda: delta_gates(1)}
            for step in range(STEPS):
                if step == 0:
                    dve.wait_ge(S_("inverse_rows_in"), 16 * 2 * NB)
                    for d in DIRS:
                        expand(step, d)
                if step:
                    dve.wait_ge(S_("vnew"), 2 * step)
                for l in range(LEVELS):
                    for d in DIRS:
                        dve.wait_ge(S_("Y"), level(step, l, d))
                        v.tensor_tensor(Yt[d], B4(4 * d), bh(lvl[:, d * LEVELS + l, :]), ALU.mult).then_inc(S_("Y_out"), 1)
                    if l == 0:
                        for d in DIRS:
                            t = TILE_OF[d][step]
                            bt = beta[:, t, 4 * d:4 * d + 4]
                            v.tensor_tensor(small[:, 176 + 4 * d:180 + 4 * d], bt, EX[:, C_GE if d else C_LE, t, 4 * d:4 * d + 4], ALU.mult).then_inc(S_("beg"), 1)
                            v.tensor_tensor(Rv[d], v_t[:, t, :, :], bc(bt), ALU.mult)
                            dve.wait_ge(S_("beg"), nth(step, d))
                            v.tensor_tensor(Rk[d], kn[:, t, :, :], bc(small[:, 176 + 4 * d:180 + 4 * d]), ALU.mult).then_inc(S_("R"), 1)
                    if (step, l) in beside:
                        beside[step, l]()
                    if l == 1 and step >= 2:
                        for d in DIRS:
                            dve.wait_ge(S_("decay"), 2 * TT2 + 2 + later(step, d))
                            v.tensor_tensor(ET[d], ET[d], bh(cst[:, C_GE if d else C_LE, :]), ALU.mult).then_inc(S_("ET"), 1)
                    for d in DIRS:
                        dve.wait_ge(S_("Z"), level(step, l, d))
                        last = v.tensor_tensor(XT[d], XT[d], B4(4 * d + 1), ALU.subtract)
                        if l < LEVELS - 1:
                            last = v.tensor_tensor(X[d], X[d], B4(4 * d + 2), ALU.subtract)
                        last.then_inc(S_("X_out"), 1)
                if step < 3:
                    for d in DIRS:
                        expand(step + 1, d)
                if step >= 2:
                    for d in DIRS:
                        dve.wait_ge(S_("ET"), later(step, d))
                        dve.wait_ge(S_("qk"), later(step, d))
                        v.tensor_tensor(ET[d], B4(4 * d + 2), ET[d], ALU.mult).then_inc(S_("Pm"), 1)
                if step < 3:
                    for d in DIRS:
                        dve.wait_ge(S_("dS"), nth(step, d))
                        update_state(St[d], 0, step, d, 4 * d + 3, S_("state"))
                if step >= 2:
                    for d in DIRS:
                        dve.wait_ge(S_("o"), later(step, d))
                        output_part(0, step, d, 4 * d, 4 * d + 2)
            for i, t in enumerate((1, 0)):
                dve.wait_ge(S_("head_sq"), 8 + 4 * (i + 1))
                c = 144 + 4 * t
                v.tensor_scalar(small[:, c + 16:c + 20], small[:, c:c + 4], 1.0 / P, EPS, ALU.mult, ALU.add).then_inc(S_("head_var"), 1)
            for i, t in enumerate((1, 0)):
                dve.wait_ge(S_("head_rstd"), i + 2)
                for h in range(H4):
                    last = v.scalar_tensor_tensor(y2[0][:, t, h, :], y2[0][:, t, h, :], small[:, 160 + 4 * t + h:161 + 4 * t + h],
                                                  zt[:, t, h * P:(h + 1) * P], ALU.mult, ALU.mult)
                last.then_inc(S_("mixed"), 1)
            dve.wait_ge(S_("yT"), 4)
            v.tensor_copy(yT[:, 2:4, :].rearrange("p a b -> p (a b)"), ps[:, 6, :]).then_inc(S_("yT_v"), 1)
            r_mix2.vector(dve)
            n_ffn2.vector_scale(dve)
            low_parts(dve, up_ffn2.upto(-1))
            n_ffn2.evacuate(dve, 1)
            low_parts(dve, up_ffn2.upto(0))
            for j in range(11):
                g_, u_ = ps[:, 4 + 2 * (j % 2), :], ps[:, 5 + 2 * (j % 2), :]
                glj = gl[j % 2].rearrange("p a b -> p (a b)")
                dve.wait_ge(S_("tanh2"), j + 1)
                link(v.scalar_tensor_tensor(glj, glj, 1.0, g_, ALU.add, ALU.mult))
                v.scalar_tensor_tensor(aT[:, 2 * j:2 * j + 2, :].rearrange("p a b -> p (a b)"), glj, 0.5, u_, ALU.mult, ALU.mult).then_inc(S_("aT2"), 1)
                low_parts(dve, up_ffn2.upto(j + 1))
            p_ffn2.vector(dve)
            r_ffn2.vector(dve)
            dve.wait_ge(S_("gain"), 16 * 5)
            for t in range(TT):
                dve.wait_ge(S_("last_rstd"), t + 1)
                v.scalar_tensor_tensor(xn[:, t, :], x[:, t, :], smallp[:, 26 + t:27 + t], gains[:, 0, :], ALU.mult, ALU.mult).then_inc(S_("final"), 1)

        @block.tensor
        def _(pe):
            pe.wait_ge(S_("cst_in"), 16)
            n_mix0.tensor(pe)
            pe.wait_ge(S_("rel_in"), 32)
            for g in range(GROUPS):
                last = mm(ps[0:HEADS, g, 0:WLEN], relb[0:BUCKETS, HEADS * g:HEADS * (g + 1)], onehot[0:BUCKETS, g, :], True, True)
            last.then_inc(S_("tables"), 1)
            n_mix0.done(pe)
            pe.wait_ge(S_("table"), 1)
            for kind, a, g in ORDER:
                if kind in "VK":
                    w = landed(pe, (kind, a, g)).rearrange("p (k n) -> p k n", k=KT)
                    for n in range(2):
                        unit = UNIT[(kind, a, g)] + n
                        if unit >= 3:
                            pe.wait_ge(S_("proj_out"), unit - 2)
                        if kind == "V":
                            for k in range(KT):
                                last = mm(ps[:, unit % 3, :], hT[:, k, n * P:(n + 1) * P], w[:, k, :], k == 0, k == KT - 1)
                        else:
                            for m in range(2):
                                for k in range(KT):
                                    last = mm(ps[:, unit % 3, m * S:(m + 1) * S], w[:, k, (2 * n + m) * P:(2 * n + m + 1) * P], hT[:, k, :],
                                              k == 0, k == KT - 1)
                        last.then_inc(S_("proj" if n == 0 else "chunk_used"), 1)
                elif kind == "S":
                    pe.wait_ge(S_("proj_out"), UNIT[("K", a // 2, 2)] + 2)
                    if a:
                        pe.wait_ge(S_("logits"), a)
                    q = QKb[(a // 2) % 2]
                    for gg in range(GROUPS):
                        mm(ps[:, 3 + gg, 0:256], q[:, gg, a % 2, P:2 * P], q[:, gg, 2 + a % 2, :], True, True)
                        last = mm(ps[:, 3 + gg, 256:384], q[:, gg, a % 2, 0:P], q[:, gg, 2 + a % 2, 0:P], True, True)
                    last.then_inc(S_("scores"), 1)
                elif kind == "T":
                    pe.wait_ge(S_("probs"), a + 1)
                    blocks = [(gg, c) for gg in range(GROUPS) for c in (256, 0)] + [(gg, 128) for gg in range(GROUPS)]
                    for i, (gg, c) in enumerate(blocks):
                        n = i // 4
                        if i == 0 and a:
                            pe.wait_ge(S_("pT_out"), 3 * a)
                        if i == 4 and a:
                            pe.wait_ge(S_("oT"), a)
                        if i == 8:
                            pe.wait_ge(S_("pT_out"), 3 * a + 1)
                        last = nc.tensor.transpose(ps[:, 6 + n % 2, (i % 4) * P:(i % 4 + 1) * P], L[a % 2][:, gg, c:c + P], ident)
                        if i % 4 == 3 or i == 8:
                            last.then_inc(S_("pT"), 1)
                else:
                    pe.wait_ge(S_("pT_out"), 3 * a + 3)
                    pe.wait_ge(S_("proj_out"), UNIT[("V", a // 4, 2)] + 2)
                    h4 = a % 4
                    for gg in range(GROUPS):
                        mm(ps[:, 7, 0:P], V[:, 0, gg, h4, :], PT[:, 2 * gg, :], gg == 0, gg == GROUPS - 1)
                    for gg in range(GROUPS):
                        mm(ps[:, 7, P:S], V[:, 0, gg, h4, :], PT[:, 2 * gg + 1, :], gg == 0, False)
                    for gg in range(GROUPS):
                        last = mm(ps[:, 7, P:S], V[:, 1, gg, h4, :], PT[:, 6 + gg, :], False, gg == GROUPS - 1)
                    last.then_inc(S_("head_out"), 1)

            def heads_projection(i):
                first, final = i == 1, i == 0
                w = landed(pe, ("wo2", i, 0)).rearrange("p (k n) -> p k n", k=H4)
                for t in range(TT):
                    for n in range(2):
                        for h in range(H4):
                            last = mm(ps[:, 2 * t + n, :], yT[:, H4 * i + h, t * P:(t + 1) * P], w[:, h, n * 512:(n + 1) * 512],
                                      first and h == 0, final and h == H4 - 1)
                    if final and t == 0:
                        last.then_inc(S_("out_y"), 1)
                last.then_inc(S_("chunk_used"), 1)

            def ada(i, first):
                w = landed(pe, ("ada", i, 0)).rearrange("p (k n) -> p k n", k=KT)
                pe.wait_ge(S_("cond"), 1)
                if i >= 2:
                    pe.wait_ge(S_("ada_row_out"), i - 1)
                for k in range(KT):
                    last = mm(ps[0:2, 5 + i % 2, :], condT[:, k, :], w[:, k, :], k == 0, k == KT - 1)
                last.then_inc(S_("chunk_used"), 1)
                if not first:
                    ada_turn(i - 1)

            def ada_turn(i):
                pe.wait_ge(S_("ada_row_out"), i + 1)
                if i:
                    pe.wait_ge(S_("ada_out"), i)
                if i // 2 in (2, 5):
                    last = mm(ps[:, 7, :], sel[:, :], row[:, i % 2, :], True, True)
                else:
                    for m in range(4):
                        last = nc.tensor.transpose(ps[:, 7, 2 * m:2 * m + 2], row[:, i % 2, m * P:(m + 1) * P], cst[0:2, C_ID, 0:2])
                last.then_inc(S_("ada_t"), 1)

            def ada_three(i):
                for n in range(3):
                    ada(i + n, n == 0)
                ada_turn(i + 2)
                pe.wait_ge(S_("ada_out"), i + 3)

            pe.wait_ge(S_("oT"), HEADS)
            pe.wait_ge(S_("sel_in"), 16)
            p_mix0.tensor(pe)
            ada_three(0)
            n_ffn0.tensor(pe)
            n_ffn0.done(pe)
            up_ffn0.tensor(pe)
            p_ffn0.tensor(pe)
            ada_three(3)
            n_mix1.tensor(pe)
            n_mix1.done(pe)

            def lru_proj(i):
                w = landed(pe, ("lin", i, 0)).rearrange("p (k n) -> p k n", k=KT)
                if i >= 2:
                    pe.wait_ge(S_("lru_xc"), i - 1)
                    pe.wait_ge(S_("lru_gb"), i - 1)
                for n in range(4):
                    for k in range(KT):
                        last = mm(ps[:, 4 + 2 * (i % 2) + n // 2, (n % 2) * S:(n % 2 + 1) * S], w[:, k, n * P:(n + 1) * P], hT[:, k, :],
                                  k == 0, k == KT - 1)
                last.then_inc(S_("chunk_used"), 1)

            def lru_gate(i, w):
                pe.wait_ge(S_("lru_xc"), i + 1)
                if i >= 2:
                    pe.wait_ge(S_("lru_tanh"), 2 * (i - 1))
                for which in range(2):
                    for n in range(2):
                        for k in range(2):
                            last = mm(ps[:, 2 * (i % 2) + which, n * S:(n + 1) * S], w[:, which, i, k, n * P:(n + 1) * P], xc[:, 2 * i + k, :],
                                      k == 0, k == 1)
                last.then_inc(S_("lgate"), 1)

            lru_proj(0)
            pe.wait_ge(S_("gate_w_in"), 16)
            for i in range(1, 4):
                lru_proj(i)
                lru_gate(i - 1, lgw)
            lru_gate(3, lgw)
            p_mix1.tensor(pe)
            ada_three(6)
            n_ffn1.tensor(pe)
            n_ffn1.done(pe)
            up_ffn1.tensor(pe)
            p_ffn1.tensor(pe)
            ada_three(9)
            pe.wait_ge(S_("modc"), 3)
            n_ctx.tensor(pe)
            n_ctx.done(pe)
            n_lat.tensor(pe)
            n_lat.done(pe)

            for c in range(3):
                w = landed(pe, ("win", c, 0)).rearrange("p (k n) -> p k n", k=KT)
                for m in range(H4):
                    n = 4 * c + m
                    if n >= 8:
                        pe.wait_ge(S_("qkv_conv"), n - 7)
                    t0 = S if c == 0 else 0
                    for k in range(KT):
                        last = mm(ps[:, n % 8, 0:2 * S - t0], w[:, k, m * P:(m + 1) * P], hT2[:, k, t0:2 * S], k == 0, k == KT - 1)
                    last.then_inc(S_("qkv" if m < 3 else "chunk_used"), 1)
            prev = None
            for n, (what, t) in enumerate(TOKU):
                if what != prev:
                    w = landed(pe, ("win", 3 + WHATS.index(what), 0)).rearrange("p (k n) -> p k n", k=KT)
                    prev = what
                b = 12 + n - 8
                if b < 12:
                    pe.wait_ge(S_("qkv_conv"), b + 1)
                else:
                    wait_unit(pe, b - 12)
                for k in range(KT):
                    last = mm(ps[:, (12 + n) % 8, :], hT2[:, k, t * P:(t + 1) * P], w[:, k, :], k == 0, k == KT - 1)
                last.then_inc(S_("tokproj" if t < 3 else "chunk_used"), 1)
            pe.wait_ge(S_("wab_in"), 16)
            wait_unit(pe, 6)
            for t in range(TT2):
                for k in range(KT):
                    last = mm(AB[:, t, :], hT2[:, k, t * P:(t + 1) * P], wab[:, k, :], k == 0, k == KT - 1)
            last.then_inc(S_("ab"), 1)
            for n in range(len(TOKU)):
                wait_unit(pe, n)
            pe.wait_ge(S_("qk_sq"), 1)
            for i in range(24):
                last = mm(ps[:, 1, i:i + 1], sqk[:, LENAT(i):LENAT(i) + P], cst[:, C_ONE, 0:1], True, True)
            last.then_inc(S_("lens"), 1)
            pe.wait_ge(S_("dec"), 1)
            for m in range(5):
                last = mm(ps[:, 0, 64 * m:64 * m + 64], cst[:, m, :], dec[:, :, :].rearrange("p a b -> p (a b)"), True, True)
            last.then_inc(S_("sums"), 1)
            pe.wait_ge(S_("qkv_silu"), 12)
            pe.wait_ge(S_("EX"), 1)
            pe.wait_ge(S_("lengths"), 1)
            pe.wait_ge(S_("beta"), 1)
            for n, (what, t) in enumerate(TRANS):
                if n >= 8:
                    trans_out(pe, n - 8)
                src = {"v": vT, "kn": kT, "qn": qT}.get(what)
                if what in ("rqT", "rkT"):
                    s_ = rq[:, t - TT, :, :] if what == "rqT" else rk[:, t, :, :]
                elif what in ("knT", "qnT"):
                    trans_out(pe, TRANS.index((what[0:2], t)))
                    s_ = kn[:, t, :, :] if what == "knT" else qn[:, t - TT, :, :]
                else:
                    c0 = (t - TT if what == "qn" else t) * P
                    s_ = src[:, :, c0:c0 + P]
                for h in range(H4):
                    last = nc.tensor.transpose(ps[:, n % 8, h * P:(h + 1) * P], s_[:, h, :], ident)
                last.then_inc(S_("trans"), 1)
            for n in range(len(TRANS)):
                trans_out(pe, n)

            def heads(bank, left_of, right_of, start=True, stop=True):
                for h in range(H4):
                    last = mm(ps[:, bank, h * P:(h + 1) * P], left_of[:, h, :], right_of[:, h, :], start, stop)
                return last

            def tile(a, t):
                return a[:, :, t * P:(t + 1) * P]

            def lemask(d):
                return cst[:, C_GE if d else C_LE, :]

            def decay_transposed(d, bank):
                for h in range(H4):
                    last = mm(ps[:, bank, h * P:(h + 1) * P], gS[d][:, h, :], lemask(d), True, True)
                last.then_inc(S_("diff"), 1)

            for n in range(2 * TT2):
                t, d = divmod(n, 2)
                pe.wait_ge(S_("gS"), n + 1)
                if n >= 2:
                    pe.wait_ge(S_("decay"), n - 1)
                mm(ps[:, n % 2, :], lemask(d), gS[d].rearrange("p a b -> p (a b)"), True, True).then_inc(S_("diff"), 1)
                if d == 0:
                    if t >= 2:
                        pe.wait_ge(S_("A"), 2 * (t - 1))
                    heads(2 + t % 2, tile(kT, t), tile(kT, t)).then_inc(S_("kk"), 1)
            for d in DIRS:
                pe.wait_ge(S_("gS"), 2 * TT2 + d + 1)
                decay_transposed(d, 4 + d)
            pe.wait_ge(S_("A"), 2 * TT2)
            pe.wait_ge(S_("decay"), 2 * TT2 + 2)
            for step in range(STEPS):
                if step >= 2:
                    for d in DIRS:
                        t = TILE_OF[d][step]
                        if step > 2:
                            pe.wait_ge(S_("rPm"), later(step - 1, d))
                        heads(4 * d, tile(rkT, t), tile(rqT, t - TT)).then_inc(S_("rqk"), 1)
                    for d in DIRS:
                        t = TILE_OF[d][step]
                        pe.wait_ge(S_("rstate"), nth(step - 1, d))
                        if step > 2:
                            pe.wait_ge(S_("o_out"), later(step - 1, d))
                        heads(4 * d + 1, tile(rqT, t - TT), rSt[d])
                if step < 3:
                    for d in DIRS:
                        pe.wait_ge(S_("rkdec"), nth(step, d))
                        if step:
                            pe.wait_ge(S_("rstate"), nth(step - 1, d))
                        heads(4 * d + 3, rkdec[d], rv[:, TILE_OF[d][step], :, :]).then_inc(S_("rdS"), 1)
                if step >= 2:
                    for d in DIRS:
                        pe.wait_ge(S_("rPm"), later(step, d))
                        heads(4 * d + 2, rPm[d], rv[:, TILE_OF[d][step], :, :]).then_inc(S_("ro"), 1)
            for step in range(STEPS):
                pe.wait_ge(S_("o_out"), 4 + max(step - 2, 0) * 2)
                if step:
                    pe.wait_ge(S_("vnew_out"), 2 * step)
                for d in DIRS:
                    pe.wait_ge(S_("X_in"), nth(step, d))
                    for h in range(H4):
                        last = nc.tensor.transpose(ps[:, 4 * d, h * P:(h + 1) * P], X[d][:, h, :], ident)
                    last.then_inc(S_("X_turned"), 1)
                if step >= 2:
                    for d in DIRS:
                        pe.wait_ge(S_("gS"), 2 * TT2 + 2 + later(step, d))
                        pe.wait_ge(S_("state"), nth(step - 1, d))
                        decay_transposed(d, 4 * d + 3)
                for l in range(LEVELS):
                    for d in DIRS:
                        t = TILE_OF[d][step]
                        if l:
                            pe.wait_ge(S_("X_out"), level(step, l - 1, d))
                        else:
                            pe.wait_ge(S_("XT_in"), nth(step, d))
                        heads(4 * d, Am[4 * d + t], XT[d]).then_inc(S_("Y"), 1)
                    if l == LEVELS - 1 and step >= 2:
                        for d in DIRS:
                            t = TILE_OF[d][step]
                            heads(4 * d + 2, tile(kT, t), tile(qT, t - TT)).then_inc(S_("qk"), 1)
                    for d in DIRS:
                        pe.wait_ge(S_("Y_out"), level(step, l, d))
                        last = heads(4 * d + 1, X[d], Yt[d])
                        if l < LEVELS - 1:
                            last = heads(4 * d + 2, Yt[d], X[d])
                        last.then_inc(S_("Z"), 1)
                if step:
                    for d in DIRS:
                        pe.wait_ge(S_("X_out"), level(step, LEVELS - 1, d))
                        pe.wait_ge(S_("R"), nth(step, d))
                        heads(4 * d, Rk[d], XT[d]).then_inc(S_("wT"), 1)
                for d in DIRS:
                    if step == 0:
                        pe.wait_ge(S_("X_out"), level(step, LEVELS - 1, d))
                        pe.wait_ge(S_("R"), nth(step, d))
                        heads(4 * d + 1, XT[d], Rv[d]).then_inc(S_("vnew"), 1)
                    else:
                        pe.wait_ge(S_("wT_out"), nth(step - 1, d))
                        pe.wait_ge(S_("state"), nth(step - 1, d))
                        for h in range(H4):
                            mm(ps[:, 4 * d + 1, h * P:(h + 1) * P], XT[d][:, h, :], Rv[d][:, h, :], True, False)
                            last = mm(ps[:, 4 * d + 1, h * P:(h + 1) * P], wT[d][:, h, :], St[d][:, h, :], False, True)
                        last.then_inc(S_("vnew"), 1)
                if step >= 2:
                    for d in DIRS:
                        heads(4 * d, tile(qT, TILE_OF[d][step] - TT), St[d])
                if step < 3:
                    for d in DIRS:
                        pe.wait_ge(S_("vnew_out"), nth(step, d))
                        pe.wait_ge(S_("kdec"), nth(step, d))
                        if step >= 2:
                            pe.wait_ge(S_("decay"), 2 * TT2 + 2 + later(step, d))
                        elif step:
                            pe.wait_ge(S_("state"), nth(step - 1, d))
                        heads(4 * d + 3, kdec[d], vnew[d]).then_inc(S_("dS"), 1)
                if step >= 2:
                    for d in DIRS:
                        pe.wait_ge(S_("Pm"), later(step, d))
                        pe.wait_ge(S_("vnew_out"), nth(step, d))
                        heads(4 * d + 2, ET[d], vnew[d]).then_inc(S_("o"), 1)

            def y_transposes(k, bank):
                for i in range(2):
                    for t in range(TT):
                        last = nc.tensor.transpose(ps[:, bank, i * S + t * P:i * S + (t + 1) * P], y2[(k + i) // 4][:, t, (k + i) % 4, :], ident)
                last.then_inc(S_("yT"), 1)

            pe.wait_ge(S_("mixed"), 2)
            pe.wait_ge(S_("vnew_out"), 8)
            y_transposes(4, 5)
            y_transposes(6, 7)
            pe.wait_ge(S_("yT_a"), 2)
            pe.wait_ge(S_("o_out"), 8)
            heads_projection(1)
            pe.wait_ge(S_("mixed"), 4)
            y_transposes(0, 4)
            y_transposes(2, 6)
            pe.wait_ge(S_("yT_a"), 3)
            pe.wait_ge(S_("yT_v"), 1)
            heads_projection(0)
            n_ffn2.tensor(pe)
            n_ffn2.done(pe)
            up_ffn2.tensor(pe)
            p_ffn2.tensor(pe)


def cols(a):
    return np.ascontiguousarray(a.reshape(-1, P).T)


def tiles(w):
    k, n = w.shape[0] // P, w.shape[1]
    return w.reshape(k, P, n).transpose(1, 0, 2).reshape(P, k * n)


def weight_stream(i):
    qkv, lin, win = i["attn_w_qkv"][0], i["lru_w_in"][0], i["w_in_2"][0]
    halves = lambda w, half, n: np.concatenate([w[:, n * 256:(n + 1) * 256], w[:, half + n * 256:half + (n + 1) * 256]], 1)
    W = np.zeros((NCH, P, SLOT), np.float32)
    starts = {0: 0, 1: 512, 2: 1024, 3: 1536, 4: 2064, 5: 2576, 6: 3088, 7: 3600}
    for c, (kind, a, b) in enumerate(STREAM):
        if kind == "V":
            at = ((b * 3 + 2) * HEADS + 4 * a) * P
            w = qkv[:, at:at + 512]
        elif kind == "K":
            q, k = ((b * 3 + s) * HEADS * P + 2 * a * P for s in range(2))
            w = np.concatenate([qkv[:, q:q + 256], qkv[:, k:k + 256]], 1)
        elif kind == "wo":
            w = i["attn_w_o"][0][a * 512:(a + 1) * 512]
        elif kind == "ada":
            w = i["ada_w_2"][0][:, a * 512:(a + 1) * 512]
        elif kind == "up":
            w = halves(i["ffn_w_up"][a], FF, b)
        elif kind == "down":
            w = i["ffn_w_down"][a][b * 512:(b + 1) * 512]
        elif kind == "lin":
            w = halves(lin, D, a)
        elif kind == "lout":
            w = i["lru_w_out"][0][a * 512:(a + 1) * 512]
        elif kind == "win":
            w = win[:, starts[a]:starts[a] + 512]
        elif kind == "wo2":
            w = i["w_out_2"][0][a * 512:(a + 1) * 512]
        elif kind == "up2":
            w = halves(i["w_ffn_in_2"][0], FF2, a)
        else:
            w = i["w_ffn_out_2"][0][a * 512:(a + 1) * 512]
        t = tiles(w)
        W[c, :, :t.shape[1]] = t
    return W


def constants():
    r = np.arange(P)
    l, m = r[:, None], r[None, :]
    cst = np.zeros((P, NCONST, P), np.float32)
    for n, mask in enumerate((l <= m, l >= m, l > m, l < m, l >= 0 * m, l == m)):
        cst[:, n, :] = mask
    for n in range(LEVELS):
        w = BLK << n
        same = l // (2 * w) == m // (2 * w)
        cst[:, 6 + n, :] = same & (l // w % 2 == 0) & (m // w % 2 == 1)
        cst[:, 6 + LEVELS + n, :] = same & (l // w % 2 == 1) & (m // w % 2 == 0)
    cst[:, 6 + 2 * LEVELS, :] = l // BLK == m // BLK
    dist = S - 1 - np.arange(WLEN)
    exact = BUCKETS // 2
    dd = np.maximum(dist, 1).astype(np.float64)
    large = exact + (np.log(dd / exact) / np.log(MAX_DISTANCE / exact) * (BUCKETS - exact)).astype(np.int32)
    bucket = np.where(dist < exact, dist, np.minimum(large, BUCKETS - 1))
    onehot = np.zeros((BUCKETS, GROUPS, WLEN), np.float32)
    negm = np.full((HEADS, GROUPS, WLEN), NEG, np.float32)
    for g, dil in enumerate(DILATIONS):
        for n, d in enumerate(dist):
            if d >= 0 and d % dil == 0 and d // dil <= BAND:
                onehot[bucket[n], g, n] = 1
                negm[:, g, n] = 0
    f = np.float32
    t = np.arange(S)
    zero, ctx_len = np.zeros(S), np.full(S, float(S))
    pos = [np.concatenate(p).astype(f) for p in ((t, ctx_len), (zero, t // 64), (zero, t % 64))]
    ang = []
    for p, n in zip(pos, (16, 24, 24)):
        inv = (f(10000.0) ** (-np.arange(n, dtype=f) / f(n))).astype(f)
        ang.append(p[:, None] * inv[None, :])
    ang = np.concatenate(ang, 1).astype(f)
    c, s = np.cos(ang).astype(f), np.sin(ang).astype(f)
    rope = np.stack([np.concatenate([c, c], 1), np.concatenate([-s, s], 1)], 1)
    rope = np.ascontiguousarray(rope.reshape(TT2, P, 2, P).transpose(1, 0, 2, 3))
    sel = np.zeros((2, P), f)
    sel[0] = 1
    return {"cst": cst, "onehot": onehot, "negm": negm, "rope": rope, "sel": sel}


def kernel(**inputs):
    import concourse.bacc as bacc
    from concourse.bass_utils import run_bass_kernel_spmd

    i = {k: np.asarray(v) for k, v in inputs.items()}
    par = np.concatenate([
        cols(i["norm_mix_pre"]), cols(i["norm_ffn_pre"]), cols(i["lru_conv_w"]), cols(i["lru_conv_b"]),
        cols(i["lru_ga_b"]), cols(i["lru_gx_b"]), cols(i["lru_lambda"]), cols(i["norm_mix_g_2"]),
        cols(i["norm_ffn_g_2"]), cols(i["ffn_conv_w"]), cols(i["ffn_conv_b"]), cols(i["conv_w_2"]), cols(i["ada_b_2"]),
        np.stack([cols(i["c_2"]), cols(i["c_ctx_2"])], 2).reshape(P, 16)], 1)
    gate_w = np.stack([i[n][0].reshape(4, 2, P, 256).transpose(2, 0, 1, 3) for n in ("lru_ga_w", "lru_gx_w")], 1)
    ada_b = i["ada_b_2"][0]
    arrays = {
        "x": i["x"][0], "ctx": i["ctx_2"][0], "W": weight_stream(i), "par": par, "gate_w": gate_w,
        "rel_bias": i["rel_bias"],
        "gains": np.concatenate([i["norm_mix_post"][0:1], i["norm_ffn_post"][0:1], i["norm_mix_post"][1:2],
                                 i["norm_ffn_post"][1:2], i["final_g_2"][None]], 0),
        "ada_gate_b": np.stack([ada_b[2 * D:3 * D], ada_b[5 * D:6 * D]], 0),
        "wab": i["w_in_2"][0][:, 2048:2064].reshape(KT, P, 16).transpose(1, 0, 2),
        "normg2": np.concatenate([i["gdn_norm_g_2"], i["ret_norm_g_2"]], 0),
        "head_vec": np.concatenate([i["gdn_a_log_2"].reshape(1, 8), i["gdn_dt_bias_2"].reshape(1, 8),
                                    i["ret_decay_logit_2"].reshape(1, 8)], 1),
        **constants(),
    }
    arrays = {k: np.ascontiguousarray(a) for k, a in arrays.items()}
    nc = bacc.Bacc("TRN2", target_bir_lowering=False, num_devices=1)
    aps = {k: nc.dram_tensor(f"in_{k}", a.shape, F32, kind="ExternalInput").ap() for k, a in arrays.items()}
    out = nc.dram_tensor("out_x", (S, D), F32, kind="ExternalOutput").ap()
    build_program(nc, aps, out)
    r = run_bass_kernel_spmd(nc, [{f"in_{k}": a for k, a in arrays.items()}], core_ids=[0])
    return r.results[0]["out_x"].reshape(1, S, D)
```
